# Optimizing a Trainium2 kernel written in Bass

```python
import math
import jax, jax.numpy as jnp
from jax import lax
import numpy as np

D_MODEL = 1024
BATCH = 1
SEQ = 256
DEPTH = 2

N_MIXERS = 2
N_MLA_LAYERS = (DEPTH + 1) // 2
N_DIFF_LAYERS = DEPTH // 2

MLA_NOPE = 128
MLA_ROPE = 64
MLA_V = 128
MLA_HEADS = D_MODEL // MLA_V
MLA_Q_LORA = 384
MLA_KV_LORA = 256
MLA_ROPE_THETA = 10000.0

DIFF_HEAD_DIM = 64
DIFF_HEADS = D_MODEL // (2 * DIFF_HEAD_DIM)
DIFF_ROT_DIM = DIFF_HEAD_DIM // 4
ROPE_THETA = 500000.0

D_FF = 4 * D_MODEL
Q_BLOCK = 128
DEEPNORM_ALPHA = (2 * DEPTH) ** 0.25
DEEPNORM_BETA = (8 * DEPTH) ** -0.25
LN_EPS = 1e-5
RMS_EPS = 1e-6


def _layernorm(x, g, b):
    xf = x.astype(jnp.float32)
    mu = jnp.mean(xf, axis=-1, keepdims=True)
    var = jnp.mean(jnp.square(xf - mu), axis=-1, keepdims=True)
    y = (xf - mu) * lax.rsqrt(var + LN_EPS) * g.astype(jnp.float32) + b.astype(jnp.float32)
    return y.astype(x.dtype)

def _rmsnorm(x, g):
    xf = x.astype(jnp.float32)
    y = xf * lax.rsqrt(jnp.mean(jnp.square(xf), axis=-1, keepdims=True) + RMS_EPS)
    return (y * g.astype(jnp.float32)).astype(x.dtype)

def _rope(x, positions, theta):
    d = x.shape[-1]
    inv_freq = theta ** (-jnp.arange(0, d, 2, dtype=jnp.float32) / d)
    ang = positions.astype(jnp.float32)[:, :, None] * inv_freq
    cos = jnp.cos(ang)[:, :, None, :]
    sin = jnp.sin(ang)[:, :, None, :]
    xf = x.astype(jnp.float32)
    x1, x2 = xf[..., : d // 2], xf[..., d // 2:]
    out = jnp.concatenate([x1 * cos - x2 * sin, x2 * cos + x1 * sin], axis=-1)
    return out.astype(x.dtype)

def _partial_rope(x, positions, rot_dim, theta):
    return jnp.concatenate([_rope(x[..., :rot_dim], positions, theta), x[..., rot_dim:]], axis=-1)

def _to_blocks(t):
    b, s = t.shape[0], t.shape[1]
    return t.reshape(b, s // Q_BLOCK, Q_BLOCK, *t.shape[2:]).swapaxes(0, 1)

def _from_blocks(t):
    n, b, qb = t.shape[0], t.shape[1], t.shape[2]
    return t.swapaxes(0, 1).reshape(b, n * qb, *t.shape[3:])

def _causal_probs(q_blk, k, q_start, scale):
    s = jnp.einsum('bqhd,bkhd->bhqk', q_blk, k).astype(jnp.float32) * scale
    q_idx = q_start + jnp.arange(q_blk.shape[1])
    k_idx = jnp.arange(k.shape[1])
    s = jnp.where(k_idx[None, :] <= q_idx[:, None], s, -jnp.inf)
    return jax.nn.softmax(s, axis=-1)

def _mla(x, positions, w_dq, q_norm, w_uq, w_dkv, kv_norm, w_ukv, w_o):
    b, s, _ = x.shape
    h = MLA_HEADS
    cq = _rmsnorm(x @ w_dq, q_norm)
    q = (cq @ w_uq).reshape(b, s, h, MLA_NOPE + MLA_ROPE)
    q = jnp.concatenate([q[..., :MLA_NOPE], _rope(q[..., MLA_NOPE:], positions, MLA_ROPE_THETA)], axis=-1)
    ckv = x @ w_dkv
    c_kv = _rmsnorm(ckv[..., :MLA_KV_LORA], kv_norm)
    k_pe = _rope(ckv[..., None, MLA_KV_LORA:], positions, MLA_ROPE_THETA)
    kv = (c_kv @ w_ukv).reshape(b, s, h, MLA_NOPE + MLA_V)
    k = jnp.concatenate([kv[..., :MLA_NOPE], jnp.broadcast_to(k_pe, (b, s, h, MLA_ROPE))], axis=-1)
    v = kv[..., MLA_NOPE:]
    scale = (MLA_NOPE + MLA_ROPE) ** -0.5
    starts = jnp.arange(s // Q_BLOCK) * Q_BLOCK

    def block(args):
        q_blk, start = args
        p = _causal_probs(q_blk, k, start, scale)
        return jnp.einsum('bhqk,bkhd->bqhd', p.astype(v.dtype), v)

    o = _from_blocks(lax.map(block, (_to_blocks(q), starts)))
    return o.reshape(b, s, h * MLA_V) @ w_o

def _diff_attn(x, positions, w_qkv, lq1, lk1, lq2, lk2, subln, w_o, lambda_init):
    b, s, _ = x.shape
    h, dh = DIFF_HEADS, DIFF_HEAD_DIM
    q, k, v = jnp.split(x @ w_qkv, 3, axis=-1)
    q = _partial_rope(q.reshape(b, s, 2 * h, dh), positions, DIFF_ROT_DIM, ROPE_THETA).reshape(b, s, h, 2, dh)
    k = _partial_rope(k.reshape(b, s, 2 * h, dh), positions, DIFF_ROT_DIM, ROPE_THETA).reshape(b, s, h, 2, dh)
    v = v.reshape(b, s, h, 2 * dh)
    k1, k2 = k[..., 0, :], k[..., 1, :]
    lam = (jnp.exp(jnp.sum(lq1.astype(jnp.float32) * lk1.astype(jnp.float32)))
           - jnp.exp(jnp.sum(lq2.astype(jnp.float32) * lk2.astype(jnp.float32)))
           + lambda_init)
    scale = dh ** -0.5
    starts = jnp.arange(s // Q_BLOCK) * Q_BLOCK

    def block(args):
        q_blk, start = args
        p1 = _causal_probs(q_blk[..., 0, :], k1, start, scale)
        p2 = _causal_probs(q_blk[..., 1, :], k2, start, scale)
        a = p1 - lam * p2
        return jnp.einsum('bhqk,bkhd->bqhd', a.astype(v.dtype), v)

    o = _from_blocks(lax.map(block, (_to_blocks(q), starts)))
    o = _rmsnorm(o, subln) * (1.0 - lambda_init)
    return o.reshape(b, s, h * 2 * dh) @ w_o

def _sqrelu_mlp(x, w_up, w_down):
    return jnp.square(jax.nn.relu(x @ w_up)) @ w_down

def first_inputs(seed: int = 0) -> dict:
    key = jax.random.key(seed)
    ks = jax.random.split(key, 24)
    f32 = jnp.float32
    nrm = lambda k, shape, scale: jax.random.normal(k, shape, f32) * scale
    na, nd, L = N_MLA_LAYERS, N_DIFF_LAYERS, DEPTH
    x = jax.random.normal(ks[0], (BATCH, SEQ, D_MODEL), f32)
    offsets = jax.random.randint(ks[1], (BATCH, 1), 0, 4096, dtype=jnp.int32)
    positions = (jnp.arange(SEQ, dtype=jnp.int32)[None, :] + offsets).astype(jnp.int32)
    return {
        "x": x,
        "positions": positions,
        "ln_mix_g": 1.0 + nrm(ks[2], (L, D_MODEL), 0.02),
        "ln_mix_b": nrm(ks[3], (L, D_MODEL), 0.02),
        "mla_w_dq": nrm(ks[4], (na, D_MODEL, MLA_Q_LORA), D_MODEL ** -0.5),
        "mla_q_norm": 1.0 + nrm(ks[5], (na, MLA_Q_LORA), 0.02),
        "mla_w_uq": nrm(ks[6], (na, MLA_Q_LORA, MLA_HEADS * (MLA_NOPE + MLA_ROPE)), MLA_Q_LORA ** -0.5),
        "mla_w_dkv": nrm(ks[7], (na, D_MODEL, MLA_KV_LORA + MLA_ROPE), D_MODEL ** -0.5),
        "mla_kv_norm": 1.0 + nrm(ks[8], (na, MLA_KV_LORA), 0.02),
        "mla_w_ukv": nrm(ks[9], (na, MLA_KV_LORA, MLA_HEADS * (MLA_NOPE + MLA_V)), MLA_KV_LORA ** -0.5),
        "mla_w_o": nrm(ks[10], (na, MLA_HEADS * MLA_V, D_MODEL), DEEPNORM_BETA * (MLA_HEADS * MLA_V) ** -0.5),
        "diff_w_qkv": nrm(ks[11], (nd, D_MODEL, 3 * DIFF_HEADS * 2 * DIFF_HEAD_DIM), D_MODEL ** -0.5),
        "diff_lambda_q1": nrm(ks[12], (nd, DIFF_HEAD_DIM), 0.1),
        "diff_lambda_k1": nrm(ks[13], (nd, DIFF_HEAD_DIM), 0.1),
        "diff_lambda_q2": nrm(ks[14], (nd, DIFF_HEAD_DIM), 0.1),
        "diff_lambda_k2": nrm(ks[15], (nd, DIFF_HEAD_DIM), 0.1),
        "diff_subln": 1.0 + nrm(ks[16], (nd, 2 * DIFF_HEAD_DIM), 0.02),
        "diff_w_o": nrm(ks[17], (nd, DIFF_HEADS * 2 * DIFF_HEAD_DIM, D_MODEL), DEEPNORM_BETA * D_MODEL ** -0.5),
        "ln_ffn_g": 1.0 + nrm(ks[18], (L, D_MODEL), 0.02),
        "ln_ffn_b": nrm(ks[19], (L, D_MODEL), 0.02),
        "ffn_w_up": nrm(ks[20], (L, D_MODEL, D_FF), D_MODEL ** -0.5),
        "ffn_w_down": nrm(ks[21], (L, D_FF, D_MODEL), DEEPNORM_BETA * D_FF ** -0.5),
    }

def first_block(x, positions, ln_mix_g, ln_mix_b, mla_w_dq, mla_q_norm, mla_w_uq, mla_w_dkv,
              mla_kv_norm, mla_w_ukv, mla_w_o, diff_w_qkv, diff_lambda_q1, diff_lambda_k1,
              diff_lambda_q2, diff_lambda_k2, diff_subln, diff_w_o, ln_ffn_g, ln_ffn_b,
              ffn_w_up, ffn_w_down):
    for i in range(DEPTH):
        j = i // N_MIXERS
        if i % N_MIXERS == 0:
            m = _mla(x, positions, mla_w_dq[j], mla_q_norm[j], mla_w_uq[j], mla_w_dkv[j],
                     mla_kv_norm[j], mla_w_ukv[j], mla_w_o[j])
        else:
            lambda_init = 0.8 - 0.6 * math.exp(-0.3 * i)
            m = _diff_attn(x, positions, diff_w_qkv[j], diff_lambda_q1[j], diff_lambda_k1[j],
                           diff_lambda_q2[j], diff_lambda_k2[j], diff_subln[j], diff_w_o[j],
                           lambda_init)
        x = _layernorm(DEEPNORM_ALPHA * x + m, ln_mix_g[i], ln_mix_b[i])
        x = _layernorm(DEEPNORM_ALPHA * x + _sqrelu_mlp(x, ffn_w_up[i], ffn_w_down[i]),
                       ln_ffn_g[i], ln_ffn_b[i])
    return x


N_MEM = 256
D_MIX = D_MODEL
XA_HEADS = 4
XA_HEAD_DIM = D_MODEL // 16
D_XA = XA_HEADS * XA_HEAD_DIM
D_TOK = D_MIX - D_XA
CONV_WIDTH = 3
ML_HEADS = 4
ML_HEAD_DIM = D_TOK // ML_HEADS
ML_CHUNK = 64
QK_CONV_WIDTH = 4
D_FF_2 = 256 * int(math.ceil(8 * D_MODEL / 3 / 256))
DEEPNORM_ALPHA_2 = (2.0 * DEPTH) ** 0.25
DEEPNORM_BETA_2 = (8.0 * DEPTH) ** -0.25
N_CONV_LAYERS = (DEPTH + 1) // 2
N_MLSTM_LAYERS = DEPTH // 2
D_IN_CONV = 3 * D_TOK + D_XA
D_IN_MLSTM = 4 * D_TOK + 2 * ML_HEADS + D_XA


def layer_norm(x, g, b):
    xf = x.astype(jnp.float32)
    mu = jnp.mean(xf, -1, keepdims=True)
    var = jnp.mean(jnp.square(xf - mu), -1, keepdims=True)
    y = (xf - mu) * lax.rsqrt(var + LN_EPS)
    return (y * g.astype(jnp.float32) + b.astype(jnp.float32)).astype(x.dtype)

def swiglu(x, w_gate, w_up, w_down):
    return (jax.nn.silu(x @ w_gate) * (x @ w_up)) @ w_down

def causal_dwconv(u, w):
    width = w.shape[0]
    s = u.shape[1]
    up = jnp.pad(u, ((0, 0), (width - 1, 0), (0, 0)))
    out = up[:, width - 1:width - 1 + s] * w[width - 1]
    for j in range(width - 1):
        out = out + up[:, j:j + s] * w[j]
    return out

def memory_cross_attention(q, mem_kv):
    b, s, _ = q.shape
    q = q.reshape(b, s, XA_HEADS, XA_HEAD_DIM)
    k, v = jnp.split(mem_kv, 2, -1)
    k = k.reshape(b, N_MEM, XA_HEADS, XA_HEAD_DIM)
    v = v.reshape(b, N_MEM, XA_HEADS, XA_HEAD_DIM)
    scores = jnp.einsum('bshd,bmhd->bhsm', q, k).astype(jnp.float32) * (XA_HEAD_DIM ** -0.5)
    p = jax.nn.softmax(scores, -1).astype(v.dtype)
    o = jnp.einsum('bhsm,bmhd->bshd', p, v)
    return o.reshape(b, s, D_XA)

def short_conv_mixer(u, conv_w):
    b_gate, c_gate, x_in = jnp.split(u, 3, -1)
    return b_gate * causal_dwconv(c_gate * x_in, conv_w)

def mlstm_chunkwise(q, k, v, log_i, log_f):
    b, s, _ = q.shape
    h_, dh, L = ML_HEADS, ML_HEAD_DIM, ML_CHUNK
    nc = s // L

    def to_chunks(t):
        return t.astype(jnp.float32).reshape(b, nc, L, h_, dh).transpose(1, 0, 3, 2, 4)

    def gate_chunks(g):
        return g.astype(jnp.float32).reshape(b, nc, L, h_).transpose(1, 0, 3, 2)

    qc, kc, vc = to_chunks(q), to_chunks(k) * (dh ** -0.5), to_chunks(v)
    ic, fc = gate_chunks(log_i), gate_chunks(log_f)
    causal = jnp.tril(jnp.ones((L, L), dtype=bool))

    def step(carry, xs):
        c_st, n_st, m_st = carry
        q_, k_, v_, li, lf = xs
        bcum = jnp.cumsum(lf, -1)
        log_d = bcum[..., :, None] - bcum[..., None, :] + li[..., None, :]
        log_d = jnp.where(causal, log_d, -jnp.inf)
        log_inter = bcum + m_st[..., None]
        m_t = jnp.maximum(log_inter, jnp.max(log_d, -1))
        w_intra = jnp.exp(log_d - m_t[..., None])
        w_inter = jnp.exp(log_inter - m_t)
        sc = jnp.einsum('bhtd,bhsd->bhts', q_, k_) * w_intra
        num = (jnp.einsum('bhts,bhse->bhte', sc, v_)
               + w_inter[..., None] * jnp.einsum('bhtd,bhde->bhte', q_, c_st))
        den = jnp.sum(sc, -1) + w_inter * jnp.einsum('bhtd,bhd->bht', q_, n_st)
        h = num / jnp.maximum(jnp.abs(den), jnp.exp(-m_t))[..., None]
        b_last = bcum[..., -1]
        log_w = b_last[..., None] - bcum + li
        m_new = jnp.maximum(b_last + m_st, jnp.max(log_w, -1))
        w_k = jnp.exp(log_w - m_new[..., None])
        decay = jnp.exp(b_last + m_st - m_new)
        c_new = decay[..., None, None] * c_st + jnp.einsum('bhs,bhsd,bhse->bhde', w_k, k_, v_)
        n_new = decay[..., None] * n_st + jnp.einsum('bhs,bhsd->bhd', w_k, k_)
        return (c_new, n_new, m_new), h

    init = (jnp.zeros((b, h_, dh, dh), jnp.float32),
            jnp.zeros((b, h_, dh), jnp.float32),
            jnp.zeros((b, h_), jnp.float32))
    _, hs = lax.scan(step, init, (qc, kc, vc, ic, fc))
    return hs.transpose(1, 0, 3, 2, 4).reshape(b, s, h_, dh)

def mlstm_mixer(u, b_gates, qk_conv_w, head_norm_g):
    b, s, _ = u.shape
    qk, v, o_pre, gates = jnp.split(u, [2 * D_TOK, 3 * D_TOK, 4 * D_TOK], -1)
    qk = jax.nn.silu(causal_dwconv(qk, qk_conv_w))
    q, k = jnp.split(qk, 2, -1)
    gates = gates.astype(jnp.float32) + b_gates.astype(jnp.float32)
    log_i = gates[..., :ML_HEADS]
    log_f = jax.nn.log_sigmoid(gates[..., ML_HEADS:])
    h = mlstm_chunkwise(q, k, v, log_i, log_f)
    mu = jnp.mean(h, -1, keepdims=True)
    var = jnp.mean(jnp.square(h - mu), -1, keepdims=True)
    h = (h - mu) * lax.rsqrt(var + LN_EPS) * head_norm_g.astype(jnp.float32)
    return jax.nn.sigmoid(o_pre) * h.reshape(b, s, D_TOK).astype(u.dtype)

def second_inputs(seed: int = 0) -> dict:
    key = jax.random.key(seed)
    ks = jax.random.split(key, 20)
    nrm = jax.random.normal
    f32 = jnp.float32
    x = nrm(ks[0], (BATCH, SEQ, D_MODEL), f32)
    mem = nrm(ks[1], (BATCH, N_MEM, D_MODEL), f32)
    ln_g = 1.0 + 0.02 * nrm(ks[2], (DEPTH, 3, D_MODEL), f32)
    ln_b = 0.02 * nrm(ks[3], (DEPTH, 3, D_MODEL), f32)
    ffn_w_gate = nrm(ks[4], (DEPTH, 2, D_MODEL, D_FF_2), f32) * D_MODEL ** -0.5
    ffn_w_up = nrm(ks[5], (DEPTH, 2, D_MODEL, D_FF_2), f32) * D_MODEL ** -0.5
    ffn_w_down = nrm(ks[6], (DEPTH, 2, D_FF_2, D_MODEL), f32) * (D_FF_2 ** -0.5 * DEEPNORM_BETA_2)
    w_kv_mem = nrm(ks[7], (DEPTH, D_MODEL, 2 * D_XA), f32) * D_MODEL ** -0.5
    w_out = nrm(ks[8], (DEPTH, D_MIX, D_MODEL), f32) * (D_MIX ** -0.5 * DEEPNORM_BETA_2)
    w_in_conv = nrm(ks[9], (N_CONV_LAYERS, D_MODEL, D_IN_CONV), f32) * D_MODEL ** -0.5
    conv_w = nrm(ks[10], (N_CONV_LAYERS, CONV_WIDTH, D_TOK), f32) * CONV_WIDTH ** -0.5
    w_in_mlstm = nrm(ks[11], (N_MLSTM_LAYERS, D_MODEL, D_IN_MLSTM), f32) * D_MODEL ** -0.5
    w_in_mlstm = w_in_mlstm.at[:, :, 4 * D_TOK:4 * D_TOK + 2 * ML_HEADS].multiply(0.1)
    b_i = 0.1 * nrm(ks[12], (N_MLSTM_LAYERS, ML_HEADS), f32)
    b_f = jnp.linspace(3.0, 6.0, ML_HEADS, dtype=f32) + 0.1 * nrm(ks[13], (N_MLSTM_LAYERS, ML_HEADS), f32)
    b_gates = jnp.concatenate([b_i, b_f], -1)
    qk_conv_w = nrm(ks[14], (N_MLSTM_LAYERS, QK_CONV_WIDTH, 2 * D_TOK), f32) * QK_CONV_WIDTH ** -0.5
    head_norm_g = 1.0 + 0.02 * nrm(ks[15], (N_MLSTM_LAYERS, ML_HEADS, ML_HEAD_DIM), f32)
    return {"x": x, "mem": mem, "ln_g": ln_g, "ln_b": ln_b,
            "ffn_w_gate": ffn_w_gate, "ffn_w_up": ffn_w_up, "ffn_w_down": ffn_w_down,
            "w_kv_mem": w_kv_mem, "w_out": w_out,
            "w_in_conv": w_in_conv, "conv_w": conv_w,
            "w_in_mlstm": w_in_mlstm, "b_gates": b_gates,
            "qk_conv_w": qk_conv_w, "head_norm_g": head_norm_g}

def second_block(x, mem, ln_g, ln_b, ffn_w_gate, ffn_w_up, ffn_w_down, w_kv_mem, w_out,
              w_in_conv, conv_w, w_in_mlstm, b_gates, qk_conv_w, head_norm_g):
    alpha = DEEPNORM_ALPHA_2
    for l in range(DEPTH):
        x = layer_norm(alpha * x + 0.5 * swiglu(x, ffn_w_gate[l, 0], ffn_w_up[l, 0], ffn_w_down[l, 0]),
                       ln_g[l, 0], ln_b[l, 0])
        mem_kv = mem @ w_kv_mem[l]
        j = l // N_MIXERS
        if l % N_MIXERS == 0:
            u = x @ w_in_conv[j]
            tok = short_conv_mixer(u[..., :3 * D_TOK], conv_w[j])
        else:
            u = x @ w_in_mlstm[j]
            tok = mlstm_mixer(u[..., :4 * D_TOK + 2 * ML_HEADS], b_gates[j], qk_conv_w[j], head_norm_g[j])
        xa = memory_cross_attention(u[..., -D_XA:], mem_kv)
        mix = jnp.concatenate([tok, xa], -1) @ w_out[l]
        x = layer_norm(alpha * x + mix, ln_g[l, 1], ln_b[l, 1])
        x = layer_norm(alpha * x + 0.5 * swiglu(x, ffn_w_gate[l, 1], ffn_w_up[l, 1], ffn_w_down[l, 1]),
                       ln_g[l, 2], ln_b[l, 2])
    return x


def setup_inputs(seed=0):
    out = dict(first_inputs(seed))
    for name, value in second_inputs(seed + 1).items():
        if name != "x":
            out[name + "_2"] = value
    return out


def reference(
    x, positions, ln_mix_g, ln_mix_b, mla_w_dq, mla_q_norm, mla_w_uq, mla_w_dkv, mla_kv_norm,
    mla_w_ukv, mla_w_o, diff_w_qkv, diff_lambda_q1, diff_lambda_k1, diff_lambda_q2,
    diff_lambda_k2, diff_subln, diff_w_o, ln_ffn_g, ln_ffn_b, ffn_w_up, ffn_w_down, mem_2,
    ln_g_2, ln_b_2, ffn_w_gate_2, ffn_w_up_2, ffn_w_down_2, w_kv_mem_2, w_out_2, w_in_conv_2,
    conv_w_2, w_in_mlstm_2, b_gates_2, qk_conv_w_2, head_norm_g_2,
):
    x = first_block(
        x, positions, ln_mix_g, ln_mix_b, mla_w_dq, mla_q_norm, mla_w_uq, mla_w_dkv,
        mla_kv_norm, mla_w_ukv, mla_w_o, diff_w_qkv, diff_lambda_q1, diff_lambda_k1,
        diff_lambda_q2, diff_lambda_k2, diff_subln, diff_w_o, ln_ffn_g, ln_ffn_b, ffn_w_up,
        ffn_w_down,
    )
    return second_block(
        x, mem_2, ln_g_2, ln_b_2, ffn_w_gate_2, ffn_w_up_2, ffn_w_down_2, w_kv_mem_2, w_out_2,
        w_in_conv_2, conv_w_2, w_in_mlstm_2, b_gates_2, qk_conv_w_2, head_norm_g_2,
    )


_drawn_inputs = setup_inputs


def setup_inputs(seed=0):
    import zlib

    import numpy as np

    out = dict(_drawn_inputs(seed))
    spreads = {}
    factors = {'mla_q_norm': 8.0,
     'mla_kv_norm': 8.0,
     'diff_lambda_q1': 2.986,
     'diff_lambda_q2': 8.0,
     'diff_subln': 8.0,
     'head_norm_g_2': 8.0}
    for name, (base, spread) in spreads.items():
        noise = np.random.default_rng([zlib.crc32(name.encode()), seed]).standard_normal(out[name].shape)
        drawn = base * np.exp(spread * noise) if base else spread * noise
        out[name] = __import__('jax').numpy.asarray(drawn.astype(out[name].dtype))
    for name, factor in factors.items():
        out[name] = (out[name] * factor).astype(out[name].dtype)
    return out
```

```python
import math
from contextlib import ExitStack

import numpy as np

import concourse.bass as bass
from concourse import mybir

F32 = mybir.dt.float32
F32R = mybir.dt.float32r
I32 = mybir.dt.int32
ALU = mybir.AluOpType
ACT = mybir.ActivationFunctionType
AX = mybir.AxisListType

P = 128
SLOTS = 4
LN_EPS = 1e-5
RMS_EPS = 1e-6
NEG = -1e30
MAGIC_ROUND = 1.5 * 2.0 ** 23
RSQRT_SEED = float(0x5F3759DF)


class Unit:

    def __init__(self, slot, use, src, dims):
        self.slot, self.use, self.src, self.dims = slot, use, src, dims
        self.size = int(np.prod(dims))
        self.at = self.free = 0


def build(nc, a, out):
    S, D = a["x"].shape[1:]
    TT = S // P
    KC = D // P
    BC = KC // 2
    NMEM = a["mem_2"].shape[1]
    assert TT == 2 and NMEM == S
    QL = a["mla_w_dq"].shape[2]
    KVL = a["mla_kv_norm"].shape[1]
    ROPE = a["mla_w_dkv"].shape[2] - KVL
    H1 = 8
    NOPE = a["mla_w_uq"].shape[2] // H1 - ROPE
    VD = a["mla_w_ukv"].shape[2] // H1 - NOPE
    DH = a["diff_lambda_q1"].shape[1]
    ROT = DH // 4
    XH, XD = 4, D // 16
    DXA = XH * XD
    DTOK = D - DXA
    MH = 4
    MD = DTOK // MH
    CW = a["conv_w_2"].shape[1]
    QW = a["qk_conv_w_2"].shape[1]
    ALPHA = 4 ** 0.25
    LAMBDA_INIT = 0.8 - 0.6 * math.exp(-0.3)
    N_LN = 10
    QC, VC = QL // P, KVL // P
    TC = DTOK // P
    assert NOPE == VD == 2 * DH == P and ROPE == XD == DH == 64

    ctx = ExitStack()
    with ctx:
        def sb(name, shape, dt=F32):
            return ctx.enter_context(nc.sbuf_tensor(name, shape, dt))

        def sem(name):
            return ctx.enter_context(nc.semaphore(name))

        SLOT = 2 * D
        raw = sb("raw", [P, SLOTS, SLOT])
        whi = sb("whi", [P, SLOTS, SLOT], F32R)
        wlo = sb("wlo", [P, SLOTS, SLOT], F32R)
        xthi = sb("xthi", [P, KC, S], F32R)
        xtlo = sb("xtlo", [P, KC, S], F32R)
        ythi = sb("ythi", [P, KC, S], F32R)
        ytlo = sb("ytlo", [P, KC, S], F32R)
        hhi = sb("hhi", [P, 2, S], F32R)
        hlo = sb("hlo", [P, 2, S], F32R)
        x = sb("x", [P, TT, D])
        res = sb("res", [P, TT, D])
        gb = sb("gb", [P, 2, D])
        kvm = sb("kvm", [P, 2, 2, 2 * S])
        ARENA = 9100
        arena = sb("arena", [P, ARENA])
        ident = sb("ident", [P, P])
        masks = sb("masks", [P, 2, P])
        NROW = [P, 0]
        rope_f = sb("rope_f", [P, ROPE // 2 + ROT // 2])
        rope_m = sb("rope_m", [P, TT, 2, ROPE])
        rope_d = sb("rope_d", [P, TT, 2, ROT])
        pos_i = sb("pos_i", [P, TT], I32)
        pos_f = sb("pos_f", [P, TT])
        ones = sb("ones", [P, S])
        sel = sb("sel", [MH, MH, P])
        stats = sb("stats", [P, 8, 6])
        mv = sb("mv", [P, 8, 2])
        rs = sb("rs", [P, 16])
        nt = sb("nt", [P, 2, 16])
        small = sb("small", [P, 96])

        ps = ctx.enter_context(nc.psum_tensor("ps", [P, 8, 512], F32))

        class Arena:
            def __init__(self, base=0):
                self.at = base

            def take(self, *shape):
                n = int(np.prod(shape))
                v = arena[:, self.at:self.at + n]
                self.at += n
                assert self.at <= ARENA, self.at
                if len(shape) == 1:
                    return v
                names = "abcd"[:len(shape)]
                return v.rearrange(f"p ({' '.join(names)}) -> p {' '.join(names)}",
                                   **{n_: s_ for n_, s_ in zip(names[1:], shape[1:])})

        def layer_norm_params(n):
            if n < 4:
                kind = ("mix", "ffn")[n % 2]
                return [a[f"ln_{kind}_{w}"][n // 2] for w in "gb"]
            return [a[f"ln_{w}_2"][(n - 4) // 3, (n - 4) % 3] for w in "gb"]

        rows = []
        for n in range(N_LN - 1):
            for w, src in zip("gb", layer_norm_params(n)):
                rows.append((f"ln{n}{w}", src.rearrange("(c p) -> c p", p=P)))
        rows.append(("q_norm", a["mla_q_norm"][0].rearrange("(c p) -> c p", p=P)))
        rows.append(("kv_norm", a["mla_kv_norm"][0].rearrange("(c p) -> c p", p=P)))
        rows.append(("subln", a["diff_subln"]))
        rows.append(("conv_w", a["conv_w_2"][0].rearrange("w (c p) -> (w c) p", p=P)))
        rows.append(("qk_conv_w", a["qk_conv_w_2"][0].rearrange("w (c p) -> (w c) p", p=P)))
        COL, row_dmas, at = {}, [], 0
        for name, src in rows:
            COL[name] = at
            n, done = src.shape[0], 0
            while done < n:
                k = min(n - done, P - at % P)
                row_dmas.append((at // P, at % P, src[done:done + k], k))
                done, at = done + k, at + k
        NPAR = at
        par = sb("par", [P, NPAR])
        PAR_TILES = -(-NPAR // P)
        par_rows = res[:, 0, 0:PAR_TILES * P].rearrange("p (k n) -> p k n", n=P)

        def col(name, c=0):
            return par[:, COL[name] + c:COL[name] + c + 1]

        users = [[] for _ in range(SLOTS)]
        order = []
        turn = [SLOTS - 1]
        clock = [0]
        barrier = [0]

        def new_unit(slot, src, dims, at=None):
            u = Unit(slot, len(users[slot]) + 1, src, dims)
            if at is None:
                clock[0] += 1
                at = clock[0]
            u.at = at
            u.free = max(barrier[0], users[slot][-1].at if users[slot] else 0)
            u.dmas = dims[0] if len(dims) == 3 else 1
            u.loaded = (users[slot][-1].loaded if users[slot] else 0) + 16 * u.dmas
            users[slot].append(u)
            return u

        def units(srcs):
            got = []
            for src, dims in srcs:
                u = new_unit(turn[0] % SLOTS, src, dims)
                turn[0] += 1
                got.append(u)
                order.append(u)
            return got

        def by_rows(w, n, k):
            v = w.rearrange("(c p) n -> p c n", p=P)
            return [(v[:, c:c + k, :], (k, n)) for c in range(0, w.shape[0] // P, k)]

        def by_cols(w, starts, n=2 * P):
            v = w.rearrange("(c p) n -> p c n", p=P)
            return [(v[:, :, s:s + n], (w.shape[0] // P, n)) for s in starts]

        class FFN:

            def __init__(self, up, gate, down):
                self.gated = gate is not None
                self.wup, self.wgate = (w if w is None else w.rearrange("(c p) n -> p c n", p=P)
                                        for w in (up, gate))
                self.wdown = down.rearrange("(c p) n -> p c n", p=P)
                self.steps = up.shape[1] // (2 * P)
                self.per = 1 if self.gated else 2
                self.kinds = "GUD" if self.gated else "UD"
                self.first = {}
                for s in range(self.steps):
                    for k in self.kinds:
                        src, dims = self.source(k, s, 0)
                        self.first[k, s] = new_unit(self.slot(k, s), src, dims,
                                                    clock[0] + 4 * s + {"G": 1, "U": 2, "D": 7}[k])
                clock[0] += 4 * self.steps + 8
                barrier[0] = self.first["U", self.steps - (1 if self.gated else 2)].at
                turn[0] = 0

            def slot(self, kind, s):
                if self.gated and kind == "D" and s == self.steps - 1:
                    return 3
                return "GUD".index(kind) if self.gated else "UD".index(kind) + 2 * (s % 2)

            def source(self, kind, s, i):
                if kind == "D":
                    c = 2 * s
                    src = (self.wdown[:, c:c + 2, :] if isinstance(i, int) and i == 0 else
                           self.wdown[:, bass.ds(i * (2 * self.per) + c, 2), :])
                    return src, (2, D)
                w = self.wgate if kind == "G" else self.wup
                c = 2 * P * s
                src = (w[:, :, c:c + 2 * P] if isinstance(i, int) and i == 0 else
                       w[:, :, bass.ds(i * (2 * P * self.per) + c, 2 * P)])
                return src, (KC, 2 * P)

        wl = {}
        mw = {}
        uq = a["mla_w_uq"][0].rearrange("(c p) (h e) -> p c h e", p=P, e=NOPE + ROPE)
        ukv = a["mla_w_ukv"][0].rearrange("(c p) (h e) -> p c h e", p=P, e=NOPE + VD)
        mla_u = units(by_rows(a["mla_w_dq"][0], QL, 4) + by_rows(a["mla_w_dkv"][0], KVL + ROPE, 4)
                      + [(uq[:, :, :, NOPE:], (QC, H1, ROPE)),
                         (uq[:, :, 0:4, 0:NOPE], (QC, 4, NOPE)),
                         (uq[:, :, 4:8, 0:NOPE], (QC, 4, NOPE)),
                         (ukv[:, :, :, 0:NOPE], (VC, H1, NOPE)),
                         (ukv[:, :, :, NOPE:], (VC, H1, VD))]
                      + by_rows(a["mla_w_o"][0], D, 2))

        def ffn(up, gate, down):
            f = FFN(up, gate, down)
            order.append(f)
            return f

        ffns = [ffn(a["ffn_w_up"][0], None, a["ffn_w_down"][0])]
        mem_u = units([u for l in range(2) for u in by_cols(a["w_kv_mem_2"][l], [0, 2 * P])])
        diff_u = units([(v[:, c:c + 2, g * D:(g + 1) * D], (2, D))
                        for v in [a["diff_w_qkv"][0].rearrange("(c p) n -> p c n", p=P)]
                        for g in range(3) for c in range(0, KC, 2)]
                       + by_rows(a["diff_w_o"][0], D, 2))
        ffns.append(ffn(a["ffn_w_up"][1], None, a["ffn_w_down"][1]))

        def swiglu(l, i):
            return ffn(a["ffn_w_up_2"][l, i], a["ffn_w_gate_2"][l, i], a["ffn_w_down_2"][l, i])

        ffns.append(swiglu(0, 0))
        conv_u = units(by_cols(a["w_in_conv_2"][0],
                               [g * DTOK + 2 * P * i for i in range(TC // 2) for g in (1, 2, 0)]
                               + [3 * DTOK]) + by_rows(a["w_out_2"][0], D, 2))
        ffns.append(swiglu(0, 1))
        ffns.append(swiglu(1, 0))
        wm = a["w_in_mlstm_2"][0]
        wmv = wm.rearrange("(c p) n -> p c n", p=P)
        ml_u = units(by_cols(wm, [2 * P * i for i in range(TC)])
                     + by_cols(wm, [4 * DTOK], 2 * MH) + by_cols(wm, [4 * DTOK + 2 * MH], DXA)
                     + [(wmv[:, c:c + 2, g * DTOK:(g + 1) * DTOK], (2, DTOK))
                        for g in (2, 3) for c in range(0, KC, 2)]
                     + by_rows(a["w_out_2"][1], D, 2))
        ffns.append(swiglu(1, 1))

        w_loaded = [sem(f"w_loaded{s}") for s in range(SLOTS)]
        w_hi = [sem(f"w_hi{s}") for s in range(SLOTS)]
        w_lo = [sem(f"w_lo{s}") for s in range(SLOTS)]
        w_done = [sem(f"w_done{s}") for s in range(SLOTS)]

        def slot_view(t, u):
            v = t[:, u.slot, 0:u.size]
            if len(u.dims) == 2:
                return v.rearrange("p (a b) -> p a b", b=u.dims[1])
            return v.rearrange("p (a b c) -> p a b c", b=u.dims[1], c=u.dims[2])

        def load(sp, u, src=None, i=0):
            if isinstance(i, int):
                if u.use + i > 1:
                    sp.wait_ge(w_lo[u.slot], u.use + i - 1)
            else:
                sp.wait_ge(w_lo[u.slot], i + (u.use - 1))
            src = u.src if src is None else src
            if u.dmas == 1:
                sp.dma_start(slot_view(raw, u), src).then_inc(w_loaded[u.slot], 16)
            else:
                for c in range(u.dmas):
                    sp.dma_start(slot_view(raw, u)[:, c], src[:, c]).then_inc(w_loaded[u.slot], 16)

        def split_hi(act, u, i=0):
            if isinstance(i, int):
                act.wait_ge(w_loaded[u.slot], u.loaded + 16 * i)
                if u.use + i > 1:
                    act.wait_ge(w_done[u.slot], u.use + i - 1)
            else:
                act.wait_ge(w_loaded[u.slot], i * 16 + u.loaded)
                act.wait_ge(w_done[u.slot], i + (u.use - 1))
            nc.scalar.activation(whi[:, u.slot, 0:u.size], raw[:, u.slot, 0:u.size],
                                 ACT.Copy).then_inc(w_hi[u.slot], 1)

        def split_lo(dve, u, i=0):
            dve.wait_ge(w_hi[u.slot], i + u.use)
            nc.vector.tensor_tensor(wlo[:, u.slot, 0:u.size], raw[:, u.slot, 0:u.size],
                                    whi[:, u.slot, 0:u.size].bitcast(F32),
                                    ALU.subtract).then_inc(w_lo[u.slot], 1)

        def wait_split(pe, u, i=0):
            pe.wait_ge(w_lo[u.slot], i + u.use)

        def wait_done(eng, u, i=0):
            eng.wait_ge(w_done[u.slot], i + u.use)

        flat = []
        for item in order:
            if isinstance(item, FFN):
                head = [("G", 0), ("U", 0), ("D", 0)] if item.gated else \
                       [("U", 0), ("D", 0), ("U", 1), ("D", 1)]
                flat += [item.first[k] for k in head]
            else:
                flat.append(item)

        class Splitter:
            def __init__(self, eng, split):
                self.eng, self.split, self.n = eng, split, 0

            def after(self, u):
                while self.n < len(flat) and flat[self.n].free <= (u.at if u else 0):
                    self.split(self.eng, flat[self.n])
                    self.n += 1

        row_loaded = sem("row_loaded")
        x_loaded = sem("x_loaded")
        mem_loaded = sem("mem_loaded")
        consts = sem("consts")
        gb_loaded = sem("gb_loaded")
        lam_loaded = sem("lam_loaded")
        gain_loaded = sem("gain_loaded")
        dve_step = sem("dve_step")
        act_step = sem("act_step")
        par_t = sem("par_t")
        par_c = sem("par_c")
        rope_ang = sem("rope_ang")
        rope_sin = sem("rope_sin")
        acc_half = sem("acc_half")
        ln_z = sem("ln_z")
        ln_t = sem("ln_t")
        x_32 = sem("x_32")
        x_hi = sem("x_hi")
        x_lo = sem("x_lo")
        x_new = sem("x_new")
        f_act = sem("f_act")
        f_h = sem("f_h")
        f_hi = sem("f_hi")
        f_lo = sem("f_lo")
        out_done = sem("out_done")

        block = ctx.enter_context(nc.Block())

        class Chain:

            def __init__(self, eng, s):
                self.eng, self.s, self.n = eng, s, 0

            def __call__(self, ins):
                self.n += 1
                ins.then_inc(self.s, 1)
                self.eng.wait_ge(self.s, self.n)

            def mark(self, ins):
                self.n += 1
                ins.then_inc(self.s, 1)

        def rsqrt(link, y, v, k):
            t = nt[:, 0, 0:k]
            link(nc.vector.tensor_scalar(y.bitcast(I32), v.bitcast(I32), -0.5, RSQRT_SEED,
                                         ALU.mult, ALU.add))
            for _ in range(4):
                link(nc.vector.scalar_tensor_tensor(out=t, in0=y, scalar=-0.5, in1=y,
                                                    op0=ALU.mult, op1=ALU.mult))
                link(nc.vector.tensor_tensor(t, t, v, ALU.mult))
                link(nc.vector.scalar_tensor_tensor(out=y, in0=t, scalar=1.5, in1=y,
                                                    op0=ALU.add, op1=ALU.mult))

        def product(out_, w, xs, first, last):
            (wh, wlow), (xh, xl) = w, xs
            m = None
            for n, (p, q) in enumerate(((wh, xh), (wh, xl), (wlow, xh))):
                m = nc.tensor.matmul(out_, p, q, start=first and n == 0, stop=last and n == 2,
                                     skip_group_check=True)
            return m

        def w_parts(u, *ix):
            return tuple(slot_view(t, u)[(slice(None), *ix)] for t in (whi, wlo))

        def t_parts(pair, c, lo=0, n=S):
            return tuple(t[:, c, lo:lo + n] for t in pair)

        xt, yt = (xthi, xtlo), (ythi, ytlo)

        def columns_product(pe, u, c0, outs, act_pair=xt, width=P, off=0, kc=KC, x_from=None):
            for j, o in enumerate(outs):
                for c in range(kc):
                    if x_from is not None and j == 0:
                        pe.wait_ge(x_lo, x_from + c // 2 + 1)
                    m = product(o, w_parts(u, c, slice(off + j * width, off + (j + 1) * width)),
                                t_parts(act_pair, c0 + c), c == 0, c == kc - 1)
            return m

        def acc_product(pe, u, pair, chunk0, first, last, half=False):
            for t in range(TT):
                for n in range(2):
                    for c in range(u.dims[0]):
                        m = product(ps[:, 2 * t + n, :],
                                    t_parts(pair, chunk0 + c, t * P, P),
                                    w_parts(u, c, slice(n * 512, n * 512 + 512)),
                                    first and c == 0, last and c == u.dims[0] - 1)
                if half and t == 0:
                    m.then_inc(acc_half, 1)
            m.then_inc(w_done[u.slot], 1)

        def T(o, i, n=P):
            return nc.tensor.transpose(o, i, ident[0:i.shape[0], 0:i.shape[0]])

        def tchunk(c, lo=0, n=S):
            return ps[:, 4 + c // 2, (c % 2) * S + lo:(c % 2) * S + lo + n]

        def ln_tensor(pe, n):
            for t in range(TT):
                pe.wait_ge(ln_z, TT * n + t + 1)
                for c in range(KC):
                    m = T(tchunk(c, t * P, P), x[:, t, c * P:(c + 1) * P])
                    if t == TT - 1 and c % 2:
                        m.then_inc(ln_t, 1)

        def pair(t, b):
            return t[:, 2 * b:2 * b + 2, :].rearrange("p a b -> p (a b)")

        def shifted(b):
            return res[:, b // 2, (b % 2) * 2 * S:(b % 2 + 1) * 2 * S]

        def ln_scalar(act, n):
            for b in range(BC):
                act.wait_ge(x_32, BC * n + b + 1)
                nc.scalar.activation(pair(xthi, b), shifted(b), ACT.Copy).then_inc(x_hi, 1)

        def ln_vector(dve, link, n, last_unit):
            for t in range(TT):
                if t == 0:
                    dve.wait_ge(acc_half, n + 1)
                    if n > 0:
                        dve.wait_ge(x_new, 2 * n)
                else:
                    wait_done(dve, last_unit)
                r = res[:, t, :]
                link(nc.vector.scalar_tensor_tensor(
                    out=r, in0=x[:, t, :], scalar=ALPHA,
                    in1=ps[:, 2 * t:2 * t + 2, :].rearrange("p a b -> p (a b)"),
                    op0=ALU.mult, op1=ALU.add))
                for j in range(2):
                    link(nc.vector.bn_stats(stats[:, j, :], r[:, j * 512:(j + 1) * 512]))
                link(nc.vector.bn_aggr(mv[:, t, :], stats[:, 0:2, :].rearrange("p a b -> p (a b)")))
                link(nc.vector.tensor_scalar_add(nt[:, 1, t:t + 1], mv[:, t, 1:2], LN_EPS))
                rsqrt(link, rs[:, t:t + 1], nt[:, 1, t:t + 1], 1)
                nc.vector.tensor_scalar(x[:, t, :], r, mv[:, t, 0:1], rs[:, t:t + 1],
                                        ALU.subtract, ALU.mult).then_inc(ln_z, 1)

        def ln_vector_t(dve, link, n):
            for i in range(BC + 1):
                if i < BC:
                    dve.wait_ge(ln_t, BC * (n + 1) + i + 1)
                    for j in range(2):
                        c = 2 * i + j
                        m = nc.vector.tensor_scalar(shifted(i)[:, j * S:(j + 1) * S], tchunk(c),
                                                    col(f"ln{n}g", c), col(f"ln{n}b", c),
                                                    ALU.mult, ALU.add)
                        if j == 0:
                            link.mark(m)
                    m.then_inc(x_32, 1)
                b = i - 1
                if b >= 0:
                    dve.wait_ge(x_hi, BC * (n + 1) + b + 1)
                    nc.vector.tensor_tensor(pair(xtlo, b), shifted(b), pair(xthi, b).bitcast(F32),
                                            ALU.subtract).then_inc(x_lo, 1)

        def ln_gpsimd(pool, n):
            pool.wait_ge(ln_t, BC * (n + 2))
            pool.wait_ge(gb_loaded, 32 * (n + 1))
            for k, op in enumerate((ALU.mult, ALU.add)):
                for t in range(TT):
                    m = nc.gpsimd.tensor_tensor(x[:, t, :], x[:, t, :], gb[:, k, :], op)
                m.then_inc(x_new, 1)
                pool.wait_ge(x_new, 2 * n + k + 1)
            load_gb(pool, n + 1)

        def load_gb(pool, n):
            for k, src in enumerate(layer_norm_params(n)):
                pool.dma_start(gb[:, k, :], src.rearrange("(a n) -> a n", a=1).broadcast_to([P, D])) \
                    .then_inc(gb_loaded, 16)

        GATE, UP = 4, 5

        def ffn_loops(f):
            if f.gated:
                return (2, f.steps - 2), (1, f.steps - 2)
            return (2, (f.steps - 2) // 2), (1, (f.steps - 3) // 2)

        def ffn_sync(sp, f):
            head = [("G", 0), ("U", 0), ("D", 0)] if f.gated else [("U", 0), ("D", 0), ("U", 1), ("D", 1)]
            for k in head:
                load(sp, f.first[k])
            if f.gated:
                for k in "GU":
                    load(sp, f.first[k, 1])
                with sp.Fori(0, f.steps - 2) as i:
                    for k, s in (("G", 2), ("U", 2), ("D", 1)):
                        load(sp, f.first[k, s], f.source(k, s, i)[0], i)
                load(sp, f.first["D", f.steps - 1])
            else:
                with sp.Fori(0, (f.steps - 2) // 2) as i:
                    for j in range(2):
                        for k in "UD":
                            load(sp, f.first[k, 2 + j], f.source(k, 2 + j, i)[0], i)

        def ffn_up(pe, f, base, s, i=0):
            for kind in f.kinds[:-1]:
                u = f.first[kind, s]
                bank = GATE if kind == "G" else UP
                wait_split(pe, u, i)
                if not (isinstance(i, int) and i == 0 and s == 0):
                    pe.wait_ge(f_act if kind == "G" else f_h, i * f.per + (base + s))
                for j in range(2):
                    for c in range(KC):
                        if isinstance(i, int) and s == 0 and j == 0 and kind == f.kinds[0]:
                            pe.wait_ge(x_lo, x_count[id(f)] + c // 2 + 1)
                        m = product(ps[:, bank, j * S:(j + 1) * S],
                                    w_parts(u, c, slice(j * P, (j + 1) * P)), t_parts(xt, c),
                                    c == 0, c == KC - 1)
                m.then_inc(w_done[u.slot], 1)

        def ffn_down(pe, f, base, s, i=0, first=False, last=False):
            u = f.first["D", s]
            wait_split(pe, u, i)
            pe.wait_ge(f_lo, i * f.per + (base + s + 1))
            acc_product(pe, u, (hhi, hlo), 0, first, last, half=last)

        def ffn_tensor(pe, f, base, between=None):
            (s0, turns), _ = ffn_loops(f)
            ffn_up(pe, f, base, 0)
            ffn_up(pe, f, base, 1)
            ffn_down(pe, f, base, 0, first=True)
            if between:
                between()
            with pe.Fori(0, turns) as i:
                for j in range(f.per):
                    ffn_up(pe, f, base, s0 + j, i)
                    ffn_down(pe, f, base, s0 + j - 1, i)
            ffn_down(pe, f, base, f.steps - 1, last=True)

        def f_view(k):
            return arena[:, k * 2 * S:(k + 1) * 2 * S]

        def ffn_scalar(act, f, base, split, between=None):
            def features(s, i=0):
                kind = f.kinds[0]
                u = f.first[kind, s]
                wait_done(act, u, i)
                if not (isinstance(i, int) and base + s == 0):
                    act.wait_ge(f_h, i * f.per + (base + s))
                nc.scalar.activation(f_view(0), ps[:, GATE if f.gated else UP, :],
                                     ACT.Silu if f.gated else ACT.Relu).then_inc(f_act, 1)

            def high(s, i=0):
                act.wait_ge(f_h, i * f.per + (base + s + 1))
                if isinstance(i, int) and s == 0:
                    pass
                else:
                    wait_done(act, f.first["D", s - 1], i)
                nc.scalar.activation(hhi[:, :, :].rearrange("p a b -> p (a b)"), f_view(1),
                                     ACT.Copy).then_inc(f_hi, 1)

            ffn_split_loop(act, f, features, high, split, split_hi, between)

        def ffn_vector(dve, f, base, split, between=None):
            def features(s, i=0):
                dve.wait_ge(f_act, i * f.per + (base + s + 1))
                if f.gated:
                    wait_done(dve, f.first["U", s], i)
                if not (isinstance(i, int) and base + s == 0):
                    dve.wait_ge(f_lo, i * f.per + (base + s))
                nc.vector.scalar_tensor_tensor(out=f_view(1), in0=f_view(0),
                                               scalar=0.5 if f.gated else 1.0, in1=ps[:, UP, :],
                                               op0=ALU.mult, op1=ALU.mult).then_inc(f_h, 1)

            def low(s, i=0):
                dve.wait_ge(f_hi, i * f.per + (base + s + 1))
                nc.vector.tensor_tensor(hlo[:, :, :].rearrange("p a b -> p (a b)"), f_view(1),
                                        hhi[:, :, :].rearrange("p a b -> p (a b)").bitcast(F32),
                                        ALU.subtract).then_inc(f_lo, 1)

            ffn_split_loop(dve, f, features, low, split, split_lo, between)

        def ffn_split_loop(eng, f, features, part, split, split_one, between):
            last = f.steps - 1
            if f.gated:
                features(0)
                split_one(eng, f.first["G", 1])
                split_one(eng, f.first["U", 1])
                part(0)
                with eng.Fori(0, last - 1) as i:
                    features(1, i)
                    split_one(eng, f.first["G", 2], i)
                    split_one(eng, f.first["U", 2], i)
                    part(1, i)
                    split_one(eng, f.first["D", 1], i)
                split_one(eng, f.first["D", last])
                features(last)
                part(last)
                split.after(f.first["D", last - 1])
            else:
                features(0)
                split_one(eng, f.first["U", 2])
                part(0)
                if between:
                    between()
                with eng.Fori(0, (last - 3) // 2) as i:
                    for s in (1, 2):
                        features(s, i)
                        split_one(eng, f.first["U", s + 2], i)
                        part(s, i)
                        split_one(eng, f.first["D", s + 1], i)
                features(last - 2)
                split_one(eng, f.first["U", last])
                part(last - 2)
                split_one(eng, f.first["D", last - 1])
                features(last - 1)
                part(last - 1)
                split.after(f.first["U", last - 1])
                split_one(eng, f.first["D", last])
                features(last)
                part(last)
                split.after(f.first["D", last - 1])

        ffn_base, n = {}, 0
        for f in ffns:
            ffn_base[id(f)] = n
            n += f.steps
        x_count = {id(f): BC * (k + 1) for f, k in zip(ffns, (0, 2, 3, 5, 6, 8))}

        class Attention:

            def __init__(self, name, heads, maps, causal, scale, mem):
                self.name, self.heads, self.maps, self.causal, self.scale = \
                    name, heads, maps, causal, scale
                self.width = 3 * P if causal else 4 * P
                self.rows = ((0, P), (P, 3 * P)) if causal else ((0, 2 * P), (2 * P, 4 * P))
                self.blocks = [(0, 0, 0), (1, 1, P), (1, 0, 2 * P)] if causal else \
                    [(0, 0, 0), (0, 1, P), (1, 0, 2 * P), (1, 1, 3 * P)]
                self.place = {(0, 0): 0, (1, 0): P, (1, 1): 2 * P} if causal else \
                    {(0, 0): 0, (1, 0): P, (0, 1): 2 * P, (1, 1): 3 * P}
                self.p = mem.take(2, maps, self.width)
                self.pt = mem.take(2, self.width)
                self.scored = sem(f"{name}_scored")
                self.maxed = sem(f"{name}_maxed")
                self.exped = sem(f"{name}_exped")
                self.normed = sem(f"{name}_normed")
                self.turned = sem(f"{name}_turned")
                self.copied = sem(f"{name}_copied")
                self.summed = sem(f"{name}_summed")

            def s_bank(self, h, m):
                return ps[:, (h % 2) * self.maps + m, 0:self.width]

            def tensor(self, pe, score, result, read, count0=0):
                for i in range(self.heads + 2):
                    if i < self.heads:
                        if i >= 2:
                            pe.wait_ge(self.exped, 2 * self.maps * (i - 1))
                        for m in range(self.maps):
                            last = score(i, m, self.s_bank(i, m))
                        last.then_inc(self.scored, 1)
                    h = i - 1
                    if 0 <= h < self.heads:
                        pe.wait_ge(self.normed, h + 1)
                        if h >= 2:
                            pe.wait_ge(self.copied, h - 1)
                        for q, k, c in self.blocks:
                            to = self.place[q, k]
                            last = T(ps[:, 4 + h % 2, to:to + P], self.p[:, h % 2, 0, c:c + P])
                        last.then_inc(self.turned, 1)
                    h = i - 2
                    if 0 <= h < self.heads:
                        pe.wait_ge(self.copied, h + 1)
                        if h >= 2:
                            pe.wait_ge(read, count0 + h - 1)
                        result(h, self.pt[:, h % 2, :], ps[:, 6 + h % 2, :]).then_inc(self.summed, 1)

            def m_at(self, h):
                return small[:, 8 * (h % 2):8 * (h % 2) + 8]

            def vector(self, dve, link, normalise, read=None):
                for i in range(self.heads + 2):
                    if i < self.heads:
                        dve.wait_ge(self.scored, i + 1)
                        if i:
                            dve.wait_ge(self.maxed, i)
                        for m in range(self.maps):
                            bank = self.s_bank(i, m)
                            if self.causal:
                                d = bank[:, 0:2 * P].rearrange("p (a b) -> p a b", b=P)
                                link(nc.vector.tensor_tensor(
                                    d, d, masks[:, 0:1, :].broadcast_to([P, 2, P]), ALU.add))
                            for t, (lo, hi) in enumerate(self.rows):
                                link.mark(nc.vector.tensor_reduce(
                                    out=small[:, 16 + 2 * m + t:17 + 2 * m + t], in_=bank[:, lo:hi],
                                    axis=AX.X, op=ALU.max))
                        dve.wait_ge(link.s, link.n)
                        nc.vector.tensor_scalar(self.m_at(i)[:, 0:2 * self.maps],
                                                small[:, 16:16 + 2 * self.maps], -self.scale, None,
                                                ALU.mult).then_inc(self.maxed, 1)
                    h = i - 1
                    if 0 <= h < self.heads:
                        dve.wait_ge(self.exped, 2 * self.maps * (h + 1))
                        r = small[:, 32:32 + 2 * self.maps]
                        if h:
                            dve.wait_ge(self.normed, h)
                        link(nc.vector.reciprocal(r, self.sums(h)))
                        normalise(link, h, self.p[:, h % 2], r, self.rows, self.normed)
                    h = i - 2
                    if 0 <= h < self.heads and read:
                        read(h)

            def sums(self, h):
                return small[:, 40 + 8 * (h % 2):40 + 8 * (h % 2) + 2 * self.maps]

            def scalar(self, act, read):
                for i in range(self.heads + 2):
                    if i < self.heads:
                        act.wait_ge(self.maxed, i + 1)
                        if i >= 2:
                            act.wait_ge(self.turned, i - 1)
                        for m in range(self.maps):
                            for t, (lo, hi) in enumerate(self.rows):
                                k = 2 * m + t
                                nc.scalar.activation(
                                    self.p[:, i % 2, m, lo:hi], self.s_bank(i, m)[:, lo:hi], ACT.Exp,
                                    bias=self.m_at(i)[:, k:k + 1], scale=self.scale,
                                    accum_out=self.sums(i)[:, k:k + 1]).then_inc(self.exped, 1)
                    h = i - 1
                    if 0 <= h < self.heads:
                        act.wait_ge(self.turned, h + 1)
                        if h >= 2:
                            act.wait_ge(self.summed, h - 1)
                        nc.scalar.activation(self.pt[:, h % 2, :], ps[:, 4 + h % 2, 0:self.width],
                                             ACT.Copy).then_inc(self.copied, 1)
                    h = i - 2
                    if 0 <= h < self.heads:
                        act.wait_ge(self.summed, h + 1)
                        read(h, ps[:, 6 + h % 2, :])

        def scale_rows(link, h, p, r, rows_, done):
            for t, (lo, hi) in enumerate(rows_):
                m = nc.vector.tensor_scalar(p[:, 0, lo:hi], p[:, 0, lo:hi], r[:, t:t + 1], None,
                                            ALU.mult)
                if t == 0:
                    link.mark(m)
            m.then_inc(done, 1)

        A = Arena()
        mla_qn = A.take(H1, S)
        mla_kn = A.take(H1, S)
        mla_qp = A.take(H1 // 2, S)
        mla_kp = A.take(S)
        mla_v = A.take(TT, H1 * VD)
        mla_att = Attention("mla", H1, 1, True, (NOPE + ROPE) ** -0.5, A)
        latent = res[:, :, 0:QL + KVL + P]
        qpe = latent[:, :, 0:H1 * ROPE]
        rope_tmp = mla_att.p.rearrange("p a b c -> p (a b c)")[:, 0:H1 * ROPE]
        m_square = sem("m_square")
        m_latent = sem("m_latent")
        m_turned = sem("m_turned")
        m_hi = sem("m_hi")
        m_lo = sem("m_lo")
        m_qpe = sem("m_qpe")
        m_qpt = sem("m_qpt")
        m_copied = sem("m_copied")
        m_vcopied = sem("m_vcopied")
        LC = QC + VC + 1

        def latent_bank(i, lo=0, n=S):
            return ps[:, 4 + i // 2, (i % 2) * S + lo:(i % 2) * S + lo + n]

        def mla_tensor(pe):
            dq, dkv, (qp, qn0, qn1, kn, v), o = mla_u[0:2], mla_u[2:4], mla_u[4:9], mla_u[9:]
            for group, bank0 in ((dq, 0), (dkv, 2)):
                for j, u in enumerate(group):
                    wait_split(pe, u)
                    for t in range(TT):
                        for c in range(4):
                            if j + t == 0 or (t == 0 and bank0 == 0):
                                pe.wait_ge(x_lo, (4 * j + c) // 2 + 1)
                            m = product(ps[:, bank0 + t, 0:u.dims[1]],
                                        t_parts(xt, 4 * j + c, t * P, P), w_parts(u, c),
                                        4 * j + c == 0, 4 * j + c == KC - 1)
                    m.then_inc(w_done[u.slot], 1)
            for t in range(TT):
                pe.wait_ge(m_latent, t + 1)
                for i in range(LC):
                    m = T(latent_bank(i, t * P, P), latent[:, t, i * P:(i + 1) * P])
                    if t == TT - 1 and i % 2:
                        m.then_inc(m_turned, 1)
            wait_split(pe, qp)
            pe.wait_ge(m_lo, QC)
            for t in range(TT):
                for c in range(QC):
                    m = product(ps[:, t, :], t_parts(xt, c, t * P, P),
                                tuple(w.rearrange("p a b -> p (a b)") for w in w_parts(qp, c)),
                                c == 0, c == QC - 1)
            m.then_inc(w_done[qp.slot], 1)
            pe.wait_ge(m_lo, QC + VC)
            pe.wait_ge(m_hi, LC)
            for u, bank in ((qn0, 2), (qn1, 4)):
                wait_split(pe, u)
                for h in range(4):
                    for c in range(QC):
                        m = product(ps[:, bank + h // 2, (h % 2) * S:(h % 2) * S + S],
                                    w_parts(u, c, h), t_parts(xt, c), c == 0, c == QC - 1)
                m.then_inc(w_done[u.slot], 1)
            wait_split(pe, kn)
            for h in range(H1):
                if h == 4:
                    pe.wait_ge(m_copied, 2)
                bank = (6 if h < 4 else 2) + (h % 4) // 2
                for c in range(VC):
                    m = product(ps[:, bank, (h % 2) * S:(h % 2) * S + S], w_parts(kn, c, h),
                                t_parts(xt, QC + c), c == 0, c == VC - 1)
            m.then_inc(w_done[kn.slot], 1)
            wait_split(pe, v)
            pe.wait_ge(m_copied, 4)
            for t in range(TT):
                if t == 1:
                    pe.wait_ge(m_qpe, TT)
                for n in range(2):
                    for c in range(VC):
                        m = product(ps[:, (4, 0)[t] + n, :], t_parts(xt, QC + c, t * P, P),
                                    tuple(w.rearrange("p a b -> p (a b)")
                                          for w in w_parts(v, c, slice(4 * n, 4 * n + 4))),
                                    c == 0, c == VC - 1)
            m.then_inc(w_done[v.slot], 1)
            pe.wait_ge(m_copied, 6)
            for t in range(TT):
                for i in range(H1 // 2):
                    m = T(ps[:, 6 + i // 2, (i % 2) * S + t * P:(i % 2) * S + t * P + P],
                          qpe[:, t, i * P:(i + 1) * P])
            m.then_inc(m_qpt, 1)
            pe.wait_ge(m_copied, 10)
            pe.wait_ge(m_vcopied, 2 * TT)

            def score(h, m_, bank):
                r = slice(ROPE * (h % 2), ROPE * (h % 2) + ROPE)
                for q, ks, lo, hi in ((0, 0, 0, P), (1, 1, P, 2 * P), (1, 0, 2 * P, 3 * P)):
                    qs, kk = slice(q * P, q * P + P), slice(ks * P, ks * P + P)
                    nc.tensor.matmul(bank[:, lo:hi], mla_qn[:, h, qs], mla_kn[:, h, kk],
                                     start=True, stop=False, skip_group_check=True)
                    m = nc.tensor.matmul(bank[:, lo:hi], mla_qp[r, h // 2, qs], mla_kp[r, kk],
                                         start=False, stop=True, skip_group_check=True)
                return m

            def result(h, pt, o_):
                vs = slice(h * VD, (h + 1) * VD)
                nc.tensor.matmul(o_[:, 0:S], mla_v[:, 0, vs], pt[:, 0:S], start=True, stop=False,
                                 skip_group_check=True)
                return nc.tensor.matmul(o_[:, P:S], mla_v[:, 1, vs], pt[:, 2 * P:3 * P],
                                        start=False, stop=True, skip_group_check=True)

            mla_att.tensor(pe, score, result, m_ylo)
            out_tensor(pe, o, m_ylo)

        def out_tensor(pe, o, ylo, counts=(2, 4, 6, 8)):
            for j, u in enumerate(o):
                wait_split(pe, u)
                pe.wait_ge(ylo, counts[j])
                acc_product(pe, u, yt, 2 * j, j == 0, j == len(o) - 1, half=j == len(o) - 1)

        m_yhi = sem("m_yhi")
        m_ylo = sem("m_ylo")

        def y_hi(act, signal, c, src):
            nc.scalar.activation(ythi[:, c, :], src, ACT.Copy).then_inc(signal, 1)

        def y_lo(dve, hi, n, lo, c, src):
            dve.wait_ge(hi, n)
            nc.vector.tensor_tensor(ytlo[:, c, :], src, ythi[:, c, :].bitcast(F32),
                                    ALU.subtract).then_inc(lo, 1)

        def mla_scalar(act, link, split):
            dq, dkv, (qp, qn0, qn1, kn, v), o = mla_u[0:2], mla_u[2:4], mla_u[4:9], mla_u[9:]
            for group, bank, n, k in ((dq, 0, QL, 0), (dkv, 2, KVL, TT)):
                split.after(group[0])
                wait_done(act, group[1])
                for t in range(TT):
                    nc.scalar.activation(res[:, t, 256 * k:256 * k + n], ps[:, bank + t, 0:n], ACT.Square,
                                         accum_out=small[:, k + t:k + t + 1]).then_inc(m_square, 1)
                split.after(group[1])
            for i in range(LC):
                act.wait_ge(m_turned, i // 2 + 1)
                if i < LC - 1:
                    g = col("q_norm", i) if i < QC else col("kv_norm", i - QC)
                    nc.scalar.activation(xthi[:, i, :], latent_bank(i), ACT.Copy,
                                         scale=g).then_inc(m_hi, 1)
                else:
                    nc.scalar.activation(mla_kp, latent_bank(i), ACT.Copy).then_inc(m_hi, 1)
            for u, bank, dst in ((qn0, 2, mla_qn[:, 0:4]), (qn1, 4, mla_qn[:, 4:8]),
                                 (kn, 6, mla_kn[:, 0:4]), (kn, 2, mla_kn[:, 4:8])):
                wait_done(act, u)
                for j in range(2):
                    nc.scalar.activation(dst[:, 2 * j:2 * j + 2].rearrange("p a b -> p (a b)"),
                                         ps[:, bank + j, :], ACT.Copy).then_inc(m_copied, 1)
                split.after(u)
            split.after(v)
            act.wait_ge(m_qpt, 1)
            for j in range(2):
                nc.scalar.activation(mla_qp[:, 2 * j:2 * j + 2].rearrange("p a b -> p (a b)"),
                                     ps[:, 6 + j, :], ACT.Copy).then_inc(m_copied, 1)
            mla_att.scalar(act, read=lambda h, o_: y_hi(act, m_yhi, h, o_[:, 0:S]))

        def rotate(link, src, dst, tables, heads, half, tmp):
            cc, ss = tables
            n = 2 * half

            def every(tb, lo, hi):
                return tb[:, lo:hi].rearrange("p (a b) -> p a b", a=1).broadcast_to([P, heads, hi - lo])

            link.mark(nc.vector.tensor_tensor(tmp[:, :, 0:half], src[:, :, half:n], every(ss, 0, half),
                                              ALU.mult))
            link.mark(nc.vector.tensor_tensor(tmp[:, :, half:n], src[:, :, 0:half],
                                              every(ss, half, n), ALU.mult))
            link(nc.vector.tensor_tensor(dst, src, every(cc, 0, n), ALU.mult))
            return nc.vector.tensor_tensor(dst, dst, tmp, ALU.add)

        def mla_vector(dve, link, split):
            dq, dkv, (qp, qn0, qn1, kn, v), o = mla_u[0:2], mla_u[2:4], mla_u[4:9], mla_u[9:]
            split.after(dq[0])
            split.after(dq[1])
            split.after(dkv[0])
            dve.wait_ge(m_square, 2 * TT)
            link.mark(nc.vector.tensor_scalar(nt[:, 1, 0:2], small[:, 0:2], 1.0 / QL, RMS_EPS,
                                              ALU.mult, ALU.add))
            link(nc.vector.tensor_scalar(nt[:, 1, 2:4], small[:, 2:4], 1.0 / KVL, RMS_EPS,
                                         ALU.mult, ALU.add))
            rsqrt(link, rs[:, 0:4], nt[:, 1, 0:4], 4)
            for t in range(TT):
                link.mark(nc.vector.tensor_scalar(latent[:, t, 0:QL], ps[:, t, 0:QL], rs[:, t:t + 1],
                                                  None, ALU.mult))
                link.mark(nc.vector.tensor_scalar(latent[:, t, QL:QL + KVL], ps[:, 2 + t, 0:KVL],
                                                  rs[:, 2 + t:3 + t], None, ALU.mult))
                src = ps[:, 2 + t, KVL:KVL + ROPE].rearrange("p (a b) -> p a b", a=1)
                kp = latent[:, t, QL + KVL:QL + KVL + P]
                tmp = rope_tmp[:, 0:ROPE].rearrange("p (a b) -> p a b", a=1)
                link(rotate(link, src, kp[:, 0:ROPE].rearrange("p (a b) -> p a b", a=1),
                            (rope_m[:, t, 0], rope_m[:, t, 1]), 1, ROPE // 2, tmp))
                nc.vector.tensor_copy(kp[:, ROPE:P], kp[:, 0:ROPE]).then_inc(m_latent, 1)
            split.after(dkv[1])
            for i in range(LC - 1):
                g = col("q_norm", i) if i < QC else col("kv_norm", i - QC)
                dve.wait_ge(m_hi, 2 * (i // 2) + 2)
                nc.vector.scalar_tensor_tensor(out=xtlo[:, i, :], in0=latent_bank(i), scalar=g,
                                               in1=xthi[:, i, :].bitcast(F32), op0=ALU.mult,
                                               op1=ALU.subtract).then_inc(m_lo, 1)
            wait_done(dve, qp)
            dve.wait_ge(m_turned, LC // 2)
            split.after(qp)
            for t in range(TT):
                src = ps[:, t, :].rearrange("p (h e) -> p h e", e=ROPE)
                dst = qpe[:, t, :].rearrange("p (h e) -> p h e", e=ROPE)
                tmp = rope_tmp.rearrange("p (h e) -> p h e", e=ROPE)
                rotate(link, src, dst, (rope_m[:, t, 0], rope_m[:, t, 1]), H1, ROPE // 2,
                       tmp).then_inc(m_qpe, 1)
                dve.wait_ge(m_qpe, t + 1)
            split.after(kn)
            wait_done(dve, v)
            for t in range(TT):
                for n in range(2):
                    nc.vector.tensor_copy(mla_v[:, t, n * 512:(n + 1) * 512],
                                          ps[:, (4, 0)[t] + n, :]).then_inc(m_vcopied, 1)
            split.after(v)
            mla_att.vector(dve, link, scale_rows,
                           read=lambda h: y_lo(dve, m_yhi, h + 1, m_ylo, h, ps[:, 6 + h % 2, 0:S]))

        mem_tok = arena[:, 4 * S:4 * S + TT * D].rearrange("p (t d) -> p t d", d=D)
        mem_t = sem("mem_t")
        mem_hi = sem("mem_hi")
        mem_lo = sem("mem_lo")
        mem_c = sem("mem_c")

        def mem_bank(c):
            return ps[:, 6 + (c // 2) % 2, (c % 2) * S:(c % 2) * S + S]

        def mem_tensor_t(pe, chunks):
            pe.wait_ge(mem_loaded, 16)
            pe.wait_ge(x_lo, BC * 2)
            for c in chunks:
                if c >= 4 and c % 2 == 0:
                    pe.wait_ge(mem_lo, c // 2 - 1)
                for t in range(TT):
                    m = T(mem_bank(c)[:, t * P:(t + 1) * P], mem_tok[:, t, c * P:(c + 1) * P])
                if c % 2:
                    m.then_inc(mem_t, 1)

        def mem_scalar_t(act, chunks):
            for b in range(chunks[0] // 2, chunks[-1] // 2 + 1):
                act.wait_ge(mem_t, b + 1)
                nc.scalar.activation(pair(ythi, b), ps[:, 6 + b % 2, :], ACT.Copy).then_inc(mem_hi, 1)

        def mem_vector_t(dve, chunks):
            for b in range(chunks[0] // 2, chunks[-1] // 2 + 1):
                dve.wait_ge(mem_hi, b + 1)
                nc.vector.tensor_tensor(pair(ytlo, b), ps[:, 6 + b % 2, :], pair(ythi, b).bitcast(F32),
                                        ALU.subtract).then_inc(mem_lo, 1)

        def mem_tensor(pe):
            pe.wait_ge(mem_lo, BC)
            for l in range(2):
                k, v = mem_u[2 * l:2 * l + 2]
                if l:
                    pe.wait_ge(mem_c, 2)
                wait_split(pe, k)
                columns_product(pe, k, 0, [ps[:, 6, j * S:(j + 1) * S] for j in range(2)],
                                yt).then_inc(w_done[k.slot], 1)
                wait_split(pe, v)
                for t in range(TT):
                    for c in range(KC):
                        m = product(ps[:, 7, t * S:(t + 1) * S], t_parts(yt, c, t * P, P),
                                    w_parts(v, c), c == 0, c == KC - 1)
                m.then_inc(w_done[v.slot], 1)

        def mem_scalar(act, split):
            for l in range(2):
                for j in range(2):
                    u = mem_u[2 * l + j]
                    wait_done(act, u)
                    nc.scalar.activation(kvm[:, l, j, :], ps[:, 6 + j, :], ACT.Copy).then_inc(mem_c, 1)
                    split.after(u)

        def mem_vector(dve, split):
            for u in mem_u:
                split.after(u)

        A = Arena()
        d_tok = A.take(TT, D)
        d_q = A.take(KC, S)
        d_k = A.take(KC, S)
        d_v = res
        d_att = Attention("diff", KC, 2, True, DH ** -0.5, A)
        d_tmp, d_src = (d_att.p.rearrange("p a b c -> p (a b c)")[:, k * 512:(k + 1) * 512].rearrange(
            "p (t h e) -> p t h e", h=2 * KC, e=ROT) for k in range(2))
        d_o = d_tok
        lam = small[:, 60:61]
        d_copied = sem("d_copied")
        d_rot = sem("d_rot")
        d_t = sem("d_t")
        d_tc = sem("d_tc")
        d_vc = sem("d_vc")
        d_oc = sem("d_oc")
        d_on = sem("d_on")
        d_ot = sem("d_ot")
        d_yhi = sem("d_yhi")
        d_ylo = sem("d_ylo")
        d_sq = sem("d_sq")

        def diff_tensor(pe):
            q, k, v, o = (diff_u[4 * g:4 * g + 4] for g in range(4))

            def project(group, bank0):
                for j, u in enumerate(group):
                    wait_split(pe, u)
                    for t in range(TT):
                        for n in range(2):
                            for c in range(2):
                                if bank0 == 0 and t + n == 0:
                                    pe.wait_ge(x_lo, 2 * BC + j + 1)
                                m = product(ps[:, bank0 + 2 * t + n, :],
                                            t_parts(xt, 2 * j + c, t * P, P),
                                            w_parts(u, c, slice(n * 512, n * 512 + 512)),
                                            j + c == 0, 2 * j + c == KC - 1)
                    m.then_inc(w_done[u.slot], 1)

            def turn_over(n):
                for t in range(TT):
                    pe.wait_ge(d_rot, TT * n + t + 1)
                    for c in range(KC):
                        m = T(ps[:, c // 2, (c % 2) * S + t * P:(c % 2) * S + t * P + P],
                              d_tok[:, t, c * P:(c + 1) * P])
                        if t == TT - 1 and c % 2:
                            m.then_inc(d_t, 1)

            project(q, 0)
            project(k, 4)
            turn_over(0)
            pe.wait_ge(d_copied, 4)
            project(v, 4)
            pe.wait_ge(d_tc, 4)
            turn_over(1)
            pe.wait_ge(d_tc, 8)
            pe.wait_ge(d_vc, TT)

            def score(h, m_, bank):
                r = slice(DH * m_, DH * m_ + DH)
                for q_, k_, lo in ((0, 0, 0), (1, 1, P), (1, 0, 2 * P)):
                    m = nc.tensor.matmul(bank[:, lo:lo + P], d_q[r, h, q_ * P:q_ * P + P],
                                         d_k[r, h, k_ * P:k_ * P + P], start=True, stop=True,
                                         skip_group_check=True)
                return m

            def result(h, pt, o_):
                vs = slice(h * P, (h + 1) * P)
                nc.tensor.matmul(o_[:, 0:P], pt[:, 0:P], d_v[:, 0, vs], start=True, stop=True,
                                 skip_group_check=True)
                nc.tensor.matmul(o_[:, P:2 * P], pt[:, P:2 * P], d_v[:, 0, vs], start=True,
                                 stop=False, skip_group_check=True)
                return nc.tensor.matmul(o_[:, P:2 * P], pt[:, 2 * P:3 * P], d_v[:, 1, vs],
                                        start=False, stop=True, skip_group_check=True)

            d_att.tensor(pe, score, result, d_oc)
            for t in range(TT):
                pe.wait_ge(d_on, t + 1)
                for c in range(KC):
                    m = T(tchunk(c, t * P, P), d_o[:, t, c * P:(c + 1) * P])
                    if t == TT - 1 and c % 2:
                        m.then_inc(d_ot, 1)
            out_tensor(pe, o, d_ylo, (1, 2, 3, 4))

        def diff_scalar(act, link, split):
            q, k, v, o = (diff_u[4 * g:4 * g + 4] for g in range(4))

            def transposes(n):
                for j in range(4):
                    act.wait_ge(d_t, 4 * n + j + 1)
                    nc.scalar.activation(
                        (d_q, d_k)[n][:, 2 * j:2 * j + 2].rearrange("p a b -> p (a b)"),
                        ps[:, j, :], ACT.Copy).then_inc(d_tc, 1)

            for n, group in enumerate((q, k)):
                for u in group[:-1]:
                    split.after(u)
                wait_done(act, group[-1])
                if n:
                    act.wait_ge(d_t, 4)
                for t in range(TT):
                    nc.scalar.activation(
                        d_tok[:, t, :], ps[:, 4 * n + 2 * t:4 * n + 2 * t + 2, :].rearrange(
                            "p a b -> p (a b)"), ACT.Copy).then_inc(d_copied, 1)
                split.after(group[-1])
            transposes(0)
            for u in v[:-1]:
                split.after(u)
            wait_done(act, v[-1])
            for t in range(TT):
                nc.scalar.activation(d_v[:, t, :],
                                     ps[:, 4 + 2 * t:6 + 2 * t, :].rearrange("p a b -> p (a b)"),
                                     ACT.Copy).then_inc(d_vc, 1)
            split.after(v[-1])
            transposes(1)
            d_att.scalar(act, read=lambda h, o_: nc.scalar.activation(
                d_o[:, :, h * P:(h + 1) * P], o_[:, 0:2 * P].rearrange("p (t e) -> p t e", e=P),
                ACT.Copy).then_inc(d_oc, 1))
            for b in range(BC):
                act.wait_ge(d_ot, b + 1)
                nc.scalar.activation(pair(ythi, b), ps[:, 4 + b, :], ACT.Copy,
                                     scale=small[:, 61:62]).then_inc(d_yhi, 1)

        def diff_vector(dve, link, split):
            q, k, v, o = (diff_u[4 * g:4 * g + 4] for g in range(4))
            for n, group in enumerate((q, k)):
                for u in group:
                    split.after(u)
                for t in range(TT):
                    dve.wait_ge(d_copied, TT * n + t + 1)
                    tok = d_tok[:, t, :].rearrange("p (h e) -> p h e", e=DH)[:, :, 0:ROT]
                    src = d_src[:, t]
                    link(nc.vector.tensor_copy(src, tok))
                    rotate(link, src, tok, (rope_d[:, t, 0], rope_d[:, t, 1]), 2 * KC, ROT // 2,
                           d_tmp[:, t]).then_inc(d_rot, 1)
            for u in v:
                split.after(u)

            def difference(link_, h, p, r, rows_, done):
                link_(nc.vector.tensor_scalar(small[:, 36:38], r[:, 2:4], lam, None, ALU.mult))
                for t, (lo, hi) in enumerate(rows_):
                    link_.mark(nc.vector.tensor_scalar(p[:, 1, lo:hi], p[:, 1, lo:hi],
                                                       small[:, 36 + t:37 + t], None, ALU.mult))
                dve.wait_ge(link_.s, link_.n)
                for t, (lo, hi) in enumerate(rows_):
                    m = nc.vector.scalar_tensor_tensor(out=p[:, 0, lo:hi], in0=p[:, 0, lo:hi],
                                                       scalar=r[:, t:t + 1], in1=p[:, 1, lo:hi],
                                                       op0=ALU.mult, op1=ALU.add)
                    if t == 0:
                        link_.mark(m)
                m.then_inc(done, 1)

            d_att.vector(dve, link, difference)
            dve.wait_ge(d_oc, KC)
            heads = "p (h e) -> p h e"
            for t in range(TT):
                sq = res[:, t, :]
                link(nc.vector.tensor_tensor(sq, d_o[:, t, :], d_o[:, t, :], ALU.mult))
                link(nc.vector.tensor_reduce(out=nt[:, 1, t * KC:(t + 1) * KC],
                                             in_=sq.rearrange(heads, e=P), axis=AX.X, op=ALU.add))
            link(nc.vector.tensor_scalar(nt[:, 1, :], nt[:, 1, :], 1.0 / P, RMS_EPS, ALU.mult, ALU.add))
            rsqrt(link, rs[:, 0:2 * KC], nt[:, 1, 0:2 * KC], 2 * KC)
            for t in range(TT):
                v_ = d_o[:, t, :].rearrange(heads, e=P)
                r = rs[:, t * KC:(t + 1) * KC].rearrange("p (h e) -> p h e", e=1).broadcast_to([P, KC, P])
                nc.vector.tensor_tensor(v_, v_, r, ALU.mult).then_inc(d_on, 1)
            for b in range(BC):
                dve.wait_ge(d_yhi, b + 1)
                nc.vector.scalar_tensor_tensor(out=pair(ytlo, b), in0=ps[:, 4 + b, :],
                                               scalar=small[:, 61:62],
                                               in1=pair(ythi, b).bitcast(F32), op0=ALU.mult,
                                               op1=ALU.subtract).then_inc(d_ylo, 1)

        def cross(name, layer, xq, mem, ylo, count0):
            att = Attention(name, XH, 1, False, XD ** -0.5, mem)
            yhi = sem(f"{name}_yhi")
            keys = kvm[:, layer, 0, :].rearrange("p (c s) -> p c s", s=S)
            vals = kvm[:, layer, 1, :].rearrange("p (t e) -> p t e", e=DXA)

            def rows_of(h):
                return slice(XD * (h % 2), XD * (h % 2) + XD)

            def score(h, m_, bank):
                for t in range(TT):
                    m = nc.tensor.matmul(bank[:, t * S:(t + 1) * S],
                                         xq[rows_of(h), h // 2, t * P:(t + 1) * P],
                                         keys[rows_of(h), h // 2, :], start=True, stop=True,
                                         skip_group_check=True)
                return m

            def result(h, pt, o_):
                for t in range(TT):
                    m = nc.tensor.matmul(o_[rows_of(h), 0:S], vals[:, t, h * XD:(h + 1) * XD],
                                         pt[:, t * S:(t + 1) * S], start=t == 0, stop=t == TT - 1,
                                         skip_group_check=True)
                return m

            def read_hi(h, o_):
                nc.scalar.activation(ythi[rows_of(h), TC + h // 2, :], o_[rows_of(h), 0:S],
                                     ACT.Copy).then_inc(yhi, 1)

            def scalar(act):
                att.scalar(act, read_hi)

            def vector(dve, link):
                def read_lo(h):
                    dve.wait_ge(yhi, h + 1)
                    nc.vector.tensor_tensor(ytlo[rows_of(h), TC + h // 2, :],
                                            ps[rows_of(h), 6 + h % 2, 0:S],
                                            ythi[rows_of(h), TC + h // 2, :].bitcast(F32),
                                            ALU.subtract).then_inc(ylo, 1)
                att.vector(dve, link, scale_rows, read_lo)

            return (lambda pe: att.tensor(pe, score, result, ylo, count0)), scalar, vector

        A = Arena()
        PAD = CW - 1
        c_c = A.take(2, 2, S)
        c_x = A.take(2, 2, PAD + S)
        c_s = A.take(2, 2, S)
        c_y = A.take(2, 2, S)
        c_q = A.take(2, S)
        c_zero = sem("c_zero")
        c_copied = sem("c_copied")
        c_tok = sem("c_tok")
        c_yhi = sem("c_yhi")
        c_ylo = sem("c_ylo")
        c_qc = sem("c_qc")
        TRI = TC // 2
        cross0_tensor, cross0_scalar, cross0_vector = cross("cross0", 0, c_q, A, c_ylo, TC)

        def conv_tensor(pe):
            o = conv_u[3 * TRI + 1:]
            for n in range(3 * TRI + 1):
                u = conv_u[n]
                i = n // 3
                bank = 6 if n == 3 * TRI else (i % 2) * 3 + n % 3
                if 2 <= i < TRI:
                    pe.wait_ge(c_tok, i - 1)
                wait_split(pe, u)
                columns_product(pe, u, 0, [ps[:, bank, j * S:(j + 1) * S] for j in range(2)],
                                x_from=5 * BC if n == 0 else None).then_inc(w_done[u.slot], 1)
            pe.wait_ge(c_qc, 1)
            pe.wait_ge(c_tok, TRI)
            cross0_tensor(pe)
            out_tensor(pe, o, c_ylo, (2, 4, 6, TC + XH))

        def conv_scalar(act, link, split):
            def high(i):
                act.wait_ge(c_tok, i + 1)
                for j in range(2):
                    nc.scalar.activation(ythi[:, 2 * i + j, :], c_y[:, i % 2, j, :],
                                         ACT.Copy).then_inc(c_yhi, 1)

            for i in range(TRI):
                c, x_, b = conv_u[3 * i:3 * i + 3]
                wait_done(act, c)
                if i >= 2:
                    act.wait_ge(c_tok, i - 1)
                nc.scalar.activation(c_c[:, i % 2].rearrange("p a b -> p (a b)"),
                                     ps[:, (i % 2) * 3, :], ACT.Copy).then_inc(c_copied, 1)
                split.after(c)
                if i:
                    high(i - 1)
                split.after(x_)
                split.after(b)
            q = conv_u[3 * TRI]
            wait_done(act, q)
            nc.scalar.activation(c_q.rearrange("p a b -> p (a b)"), ps[:, 6, :],
                                 ACT.Copy).then_inc(c_qc, 1)
            split.after(q)
            high(TRI - 1)
            cross0_scalar(act)

        def conv_vector(dve, link, split):
            link(nc.vector.memset(c_x[:, :, :, 0:PAD], 0.0))

            def low(i):
                for j in range(2):
                    dve.wait_ge(c_yhi, 2 * i + j + 1)
                    nc.vector.tensor_tensor(ytlo[:, 2 * i + j, :], c_y[:, i % 2, j, :],
                                            ythi[:, 2 * i + j, :].bitcast(F32),
                                            ALU.subtract).then_inc(c_ylo, 1)

            for i in range(TRI):
                c, x_, b = conv_u[3 * i:3 * i + 3]
                k = i % 2
                split.after(c)
                dve.wait_ge(c_copied, i + 1)
                wait_done(dve, x_)
                link(nc.vector.tensor_tensor(
                    c_x[:, k, :, PAD:], c_c[:, k], ps[:, 3 * k + 1, :].rearrange(
                        "p (a b) -> p a b", b=S), ALU.mult))
                split.after(x_)
                for w in range(CW):
                    for j in range(2):
                        tap = c_x[:, k, j, w:w + S]
                        weight = col("conv_w", w * TC + 2 * i + j)
                        if w == 0:
                            m = nc.vector.tensor_scalar(c_s[:, k, j], tap, weight, None, ALU.mult)
                        else:
                            m = nc.vector.scalar_tensor_tensor(out=c_s[:, k, j], in0=tap, scalar=weight,
                                                               in1=c_s[:, k, j], op0=ALU.mult,
                                                               op1=ALU.add)
                        link.mark(m)
                    dve.wait_ge(link.s, link.n)
                wait_done(dve, b)
                if i >= 2:
                    dve.wait_ge(c_yhi, 2 * (i - 1))
                nc.vector.tensor_tensor(c_y[:, k].rearrange("p a b -> p (a b)"),
                                        c_s[:, k].rearrange("p a b -> p (a b)"),
                                        ps[:, 3 * k + 2, :], ALU.mult).then_inc(c_tok, 1)
                split.after(b)
                if i:
                    low(i - 1)
            split.after(conv_u[3 * TRI])
            low(TRI - 1)
            cross0_vector(dve, link)

        A = Arena()
        QPAD = QW - 1
        l_x = A.take(2, 2, QPAD + S)
        l_s = A.take(2, 2, S)
        shared = A.at
        l_qk = A.take(2 * TC, S)
        l_v = A.take(TT, MH, MD + 1)
        l_o = A.take(TT, DTOK)
        l_gain = A.take(DTOK)
        B_ = Arena()
        cross1_mem = B_
        l_q = res[:, 1, D // 2:].rearrange("p (c s) -> p c s", s=S)
        l_h = res[:, :, :].rearrange("p t d -> p (t d)")[:, 0:TT * DTOK].rearrange(
            "p (t d) -> p t d", d=DTOK)
        C_ = Arena()
        l_e = C_.take(3 * P)
        l_w = C_.take(2, 3 * P)
        l_sc = C_.take(2, 3 * P)
        assert C_.at <= shared
        rowt = kvm[0:MH, 0, :, :].rearrange("p a (b s) -> p (a b) s", s=S)
        g_tok = small[:, 64:80]
        g_tmp = small[:, 80:88]
        gcol = sb("gcol", [P, 2, TT, MH])
        g_bias = sb("g_bias", [P, 2 * MH])
        names = ("l_copied", "l_conv", "l_qkd", "l_g", "l_gexp", "l_gln", "l_gts", "l_gt", "l_row",
                 "l_col", "l_gc", "l_xq", "l_vc", "l_oc", "l_og", "l_mb", "l_sT", "l_ed", "l_wd",
                 "l_scd", "l_num", "l_hd", "l_tok", "l_tt", "l_yhi", "l_ylo")
        L = {n: sem(n) for n in names}
        cross1_tensor, cross1_scalar, cross1_vector = cross("cross1", 1, l_q, B_, L["l_ylo"], 0)
        assert B_.at <= shared
        QK, GX, XQ = ml_u[0:TC], ml_u[TC], ml_u[TC + 1]
        VU, OU, WO = ml_u[TC + 2:TC + 6], ml_u[TC + 6:TC + 10], ml_u[TC + 10:]

        def head_rows(h):
            got, f = [], h * MD
            while f < (h + 1) * MD:
                n = min(P - f % P, (h + 1) * MD - f)
                got.append((f // P, slice(f % P, f % P + n)))
                f += n
            return got

        def ml_tensor(pe):
            for j, u in enumerate(QK):
                wait_split(pe, u)
                if j >= 2:
                    pe.wait_ge(L["l_copied"], j - 1)
                columns_product(pe, u, 0, [ps[:, j % 2, n * S:(n + 1) * S] for n in range(2)],
                                x_from=8 * BC if j == 0 else None).then_inc(w_done[u.slot], 1)
            wait_split(pe, GX)
            for t in range(TT):
                for c in range(KC):
                    m = product(ps[:, 2, t * 2 * MH:(t + 1) * 2 * MH], t_parts(xt, c, t * P, P),
                                w_parts(GX, c), c == 0, c == KC - 1)
            m.then_inc(w_done[GX.slot], 1)
            wait_split(pe, XQ)
            columns_product(pe, XQ, 0, [ps[:, 3, n * S:(n + 1) * S] for n in range(2)]) \
                .then_inc(w_done[XQ.slot], 1)

            def tokens(group, banks):
                for j, u in enumerate(group):
                    wait_split(pe, u)
                    for t in range(TT):
                        for lo, hi in ((0, 512), (512, DTOK)):
                            for c in range(2):
                                m = product(ps[:, banks[t] + lo // 512, 0:hi - lo],
                                            t_parts(xt, 2 * j + c, t * P, P),
                                            w_parts(u, c, slice(lo, hi)), j + c == 0,
                                            2 * j + c == KC - 1)
                    m.then_inc(w_done[u.slot], 1)

            tokens(VU, (4, 6))
            pe.wait_ge(L["l_g"], 2)
            for k in range(2):
                for t in range(TT):
                    m = T(ps[0:MH, 2, k * S + t * P:k * S + t * P + P],
                          g_tok[:, t * 2 * MH + k * MH:t * 2 * MH + (k + 1) * MH])
            m.then_inc(L["l_gt"], 1)
            pe.wait_ge(L["l_copied"], TC)
            pe.wait_ge(L["l_vc"], TT)
            tokens(OU, (0, 4))
            pe.wait_ge(L["l_row"], 3)
            pe.wait_ge(L["l_xq"], 1)
            for k in range(2):
                for t in range(TT):
                    m = T(ps[:, 3, (k * TT + t) * MH:(k * TT + t + 1) * MH],
                          rowt[:, 2 * k, t * P:(t + 1) * P])
            m.then_inc(L["l_col"], 1)
            pe.wait_ge(L["l_gc"], 2)
            pe.wait_ge(L["l_oc"], TT)
            cross1_tensor(pe)
            pe.wait_ge(L["l_ylo"], XH)
            pe.wait_ge(L["l_qkd"], TC)
            for i in range(MH + 1):
                if i < MH:
                    if i >= 2:
                        pe.wait_ge(L["l_ed"], i - 1)
                        pe.wait_ge(L["l_scd"], i - 1)
                    nc.tensor.matmul(ps[:, 6 + i % 2, 0:S], sel[:, i, :], rowt[:, 3, :], start=True,
                                     stop=True, skip_group_check=True).then_inc(L["l_mb"], 1)
                    pieces = head_rows(i)
                    for to, k0, q0 in ((slice(0, S), 0, 0), (slice(S, 3 * P), P, P)):
                        for n, (c, r) in enumerate(pieces):
                            m = nc.tensor.matmul(ps[:, 2 + i % 2, to], l_qk[r, TC + c, k0:k0 + P],
                                                 l_qk[r, c, q0:S], start=n == 0,
                                                 stop=n == len(pieces) - 1, skip_group_check=True)
                    m.then_inc(L["l_sT"], 1)
                h = i - 1
                if h >= 0:
                    pe.wait_ge(L["l_scd"], h + 1)
                    if h >= 2:
                        pe.wait_ge(L["l_hd"], h - 1)
                    b = ps[:, h % 2, :]
                    sc = l_sc[:, h % 2]
                    n1 = MD + 1
                    nc.tensor.matmul(b[:, 0:n1], sc[:, 0:P], l_v[:, 0, h, :], start=True, stop=True,
                                     skip_group_check=True)
                    nc.tensor.matmul(b[:, n1:2 * n1], sc[:, P:S], l_v[:, 0, h, :], start=True,
                                     stop=False, skip_group_check=True)
                    nc.tensor.matmul(b[:, n1:2 * n1], sc[:, S:3 * P], l_v[:, 1, h, :], start=False,
                                     stop=True, skip_group_check=True).then_inc(L["l_num"], 1)
            for t in range(TT):
                pe.wait_ge(L["l_tok"], t + 1)
                for c in range(TC):
                    m = T(tchunk(c, t * P, P), l_h[:, t, c * P:(c + 1) * P])
                    if t == TT - 1 and c % 2:
                        m.then_inc(L["l_tt"], 1)
            out_tensor(pe, WO, L["l_ylo"], (XH + 1, XH + 2, XH + 3, XH + 3))

        def ml_scalar(act, link, split):
            for j in range(TC + 1):
                if j < TC:
                    u = QK[j]
                    wait_done(act, u)
                    if j == 0:
                        act.wait_ge(L["l_conv"], 1)
                    if j >= 2:
                        act.wait_ge(L["l_conv"], j)
                    nc.scalar.activation(l_x[:, j % 2, :, QPAD:],
                                         ps[:, j % 2, :].rearrange("p (a b) -> p a b", b=S),
                                         ACT.Copy).then_inc(L["l_copied"], 1)
                    split.after(u)
                if j >= 1:
                    act.wait_ge(L["l_conv"], j + 1)
                    nc.scalar.activation(
                        l_qk[:, 2 * (j - 1):2 * j].rearrange("p a b -> p (a b)"),
                        l_s[:, (j - 1) % 2].rearrange("p a b -> p (a b)"),
                        ACT.Silu).then_inc(L["l_qkd"], 1)
            split.after(GX)
            wait_done(act, XQ)
            nc.scalar.activation(l_q.rearrange("p a b -> p (a b)"), ps[:, 3, :],
                                 ACT.Copy).then_inc(L["l_xq"], 1)
            split.after(XQ)
            act.wait_ge(L["l_g"], 1)
            nc.scalar.activation(g_tmp, g_tmp, ACT.Exp, scale=-1.0).then_inc(L["l_gexp"], 1)
            act.wait_ge(L["l_gexp"], 1)
            nc.scalar.activation(g_tmp, g_tmp, ACT.Ln, bias=1.0).then_inc(L["l_gln"], 1)
            for u in VU[:-1]:
                split.after(u)
            wait_done(act, VU[-1])
            for t in range(TT):
                nc.scalar.activation(
                    l_v[:, t, :, 0:MD],
                    ps[:, 4 + 2 * t:6 + 2 * t, :].rearrange("p a b -> p (a b)")[:, 0:DTOK].rearrange(
                        "p (h e) -> p h e", e=MD), ACT.Copy).then_inc(L["l_vc"], 1)
            split.after(VU[-1])
            for u in OU[:-1]:
                split.after(u)
            wait_done(act, OU[-1])
            for t in range(TT):
                nc.scalar.activation(
                    l_o[:, t, :], ps[:, 4 * t:4 * t + 2, :].rearrange(
                        "p a b -> p (a b)")[:, 0:DTOK], ACT.Sigmoid).then_inc(L["l_oc"], 1)
            split.after(OU[-1])
            act.wait_ge(L["l_gc"], 1)
            nc.scalar.activation(gcol[:, 1].rearrange("p a b -> p (a b)"),
                                 ps[:, 3, TT * MH:2 * TT * MH], ACT.Exp,
                                 scale=-1.0).then_inc(L["l_gc"], 1)
            act.wait_ge(L["l_gc"], 2)
            cross1_scalar(act)
            for h in range(MH):
                act.wait_ge(L["l_ed"], h + 1)
                if h >= 2:
                    act.wait_ge(L["l_scd"], h - 1)
                for s, (lo, hi) in enumerate(((0, S), (S, 3 * P))):
                    nc.scalar.activation(l_w[:, h % 2, lo:hi], l_e[:, lo:hi], ACT.Exp, scale=-1.0,
                                         bias=gcol[:, 0, s, h:h + 1]).then_inc(L["l_wd"], 1)
            for b in range(TC // 2):
                act.wait_ge(L["l_tt"], b + 1)
                nc.scalar.activation(pair(ythi, b), ps[:, 4 + b, :], ACT.Copy) \
                    .then_inc(L["l_yhi"], 1)

        def ml_vector(dve, link, split):
            nc.vector.memset(l_x[:, :, :, 0:QPAD], 0.0).then_inc(L["l_conv"], 1)
            link(nc.vector.memset(l_v[:, :, :, MD:], 1.0))
            for j, u in enumerate(QK):
                k = j % 2
                split.after(u)
                dve.wait_ge(L["l_copied"], j + 1)
                if j >= 2:
                    dve.wait_ge(L["l_qkd"], j - 1)
                for w in range(QW):
                    for n in range(2):
                        tap = l_x[:, k, n, w:w + S]
                        weight = col("qk_conv_w", w * 2 * TC + 2 * j + n)
                        if w == 0:
                            m = nc.vector.tensor_scalar(l_s[:, k, n], tap, weight, None, ALU.mult)
                        else:
                            m = nc.vector.scalar_tensor_tensor(out=l_s[:, k, n], in0=tap, scalar=weight,
                                                               in1=l_s[:, k, n], op0=ALU.mult,
                                                               op1=ALU.add)
                        if w == QW - 1 and n == 1:
                            m.then_inc(L["l_conv"], 1)
                        else:
                            link.mark(m)
                    if w < QW - 1:
                        dve.wait_ge(link.s, link.n)
            split.after(GX)
            wait_done(dve, GX)
            dve.wait_ge(gain_loaded, 32)
            g3 = g_tok.rearrange("p (t g) -> p t g", g=2 * MH)
            link(nc.vector.tensor_tensor(
                g3, ps[:, 2, 0:2 * TT * MH].rearrange("p (t g) -> p t g", g=2 * MH),
                g_bias[:, :].rearrange("p (a g) -> p a g", a=1).broadcast_to([P, TT, 2 * MH]), ALU.add))
            f3 = g3[:, :, MH:]
            tmp3 = g_tmp.rearrange("p (t g) -> p t g", g=MH)
            nc.vector.scalar_tensor_tensor(out=tmp3, in0=f3, scalar=-1.0, in1=f3, op0=ALU.mult,
                                           op1=ALU.max).then_inc(L["l_g"], 1)
            dve.wait_ge(L["l_gln"], 1)
            nc.vector.scalar_tensor_tensor(out=f3, in0=f3, scalar=0.0, in1=tmp3, op0=ALU.min,
                                           op1=ALU.subtract).then_inc(L["l_g"], 1)
            split.after(XQ)
            for u in VU:
                split.after(u)
            dve.wait_ge(L["l_gt"], 1)
            link(nc.vector.tensor_copy(rowt[:, 0:2, :].rearrange("p a s -> p (a s)"), ps[0:MH, 2, :]))
            a_, b_, m_ = rowt[:, 0, :], rowt[:, 1, :], rowt[:, 3, :]
            link(nc.vector.tensor_tensor_scan(rowt[:, 2, :], ones[0:MH, :], b_, 0.0,
                                              op0=ALU.mult, op1=ALU.add))
            nc.vector.tensor_tensor(a_, a_, rowt[:, 2, :], ALU.subtract).then_inc(L["l_row"], 1)
            dve.wait_ge(L["l_row"], 1)
            nc.vector.tensor_tensor_scan(m_, a_, a_, 0.0, op0=ALU.max,
                                         op1=ALU.max).then_inc(L["l_row"], 1)
            dve.wait_ge(L["l_row"], 2)
            nc.vector.tensor_tensor(rowt[:, 2, :], rowt[:, 2, :], m_, ALU.add).then_inc(L["l_row"], 1)
            for u in OU:
                split.after(u)
            dve.wait_ge(L["l_col"], 1)
            nc.vector.tensor_copy(gcol[:, 0].rearrange("p a b -> p (a b)"),
                                  ps[:, 3, 0:TT * MH]).then_inc(L["l_gc"], 1)
            cross1_vector(dve, link)
            for i in range(MH + 1):
                if i < MH:
                    dve.wait_ge(L["l_mb"], i + 1)
                    if i:
                        dve.wait_ge(L["l_wd"], 2 * i)
                    mb = ps[:, 6 + i % 2, :]
                    link(nc.vector.tensor_tensor(l_e[:, 0:S], mb[:, 0:S], mtril[:, :], ALU.add))
                    nc.vector.tensor_tensor(l_e[:, S:3 * P], mb[:, P:S], mtril[:, 0:P],
                                            ALU.add).then_inc(L["l_ed"], 1)
                    dve.wait_ge(L["l_sT"], i + 1)
                    dve.wait_ge(L["l_wd"], 2 * i + 2)
                    if i >= 2:
                        dve.wait_ge(L["l_num"], i - 1)
                    nc.vector.scalar_tensor_tensor(out=l_sc[:, i % 2], in0=ps[:, 2 + i % 2, 0:3 * P],
                                                   scalar=MD ** -0.5, in1=l_w[:, i % 2], op0=ALU.mult,
                                                   op1=ALU.mult).then_inc(L["l_scd"], 1)
                h = i - 1
                if h >= 0:
                    dve.wait_ge(L["l_num"], h + 1)
                    b = ps[:, h % 2, 0:2 * (MD + 1)].rearrange("p (t e) -> p t e", e=MD + 1)
                    dv = small[:, TT * h:TT * (h + 1)]
                    d = dv.rearrange("p (t e) -> p t e", e=1)
                    link(nc.vector.tensor_copy(d, b[:, :, MD:]))
                    link(nc.vector.scalar_tensor_tensor(out=d, in0=d, scalar=-1.0, in1=d,
                                                        op0=ALU.mult, op1=ALU.max))
                    link(nc.vector.tensor_tensor(d, d, gcol[:, 1, :, h:h + 1], ALU.max))
                    link(nc.vector.reciprocal(dv, dv))
                    for t in range(TT):
                        m = nc.vector.tensor_scalar(l_h[:, t, h * MD:(h + 1) * MD], b[:, t, 0:MD],
                                                    dv[:, t:t + 1], None, ALU.mult)
                        if t == 0:
                            link.mark(m)
                    m.then_inc(L["l_hd"], 1)
            dve.wait_ge(L["l_hd"], MH)
            dve.wait_ge(link.s, link.n)
            for t in range(TT):
                for h in range(MH):
                    link.mark(nc.vector.bn_stats(stats[:, t * MH + h, :],
                                                 l_h[:, t, h * MD:(h + 1) * MD]))
            dve.wait_ge(link.s, link.n)
            for k in range(TT * MH):
                link.mark(nc.vector.bn_aggr(mv[:, k, :], stats[:, k, :]))
            dve.wait_ge(link.s, link.n)
            link(nc.vector.tensor_scalar_add(nt[:, 1, 0:TT * MH], mv[:, :, 1], LN_EPS))
            rsqrt(link, rs[:, 0:TT * MH], nt[:, 1, 0:TT * MH], TT * MH)
            for t in range(TT):
                for h in range(MH):
                    k = t * MH + h
                    v_ = l_h[:, t, h * MD:(h + 1) * MD]
                    link.mark(nc.vector.tensor_scalar(v_, v_, mv[:, k, 0:1], rs[:, k:k + 1],
                                                      ALU.subtract, ALU.mult))
                dve.wait_ge(link.s, link.n)
                dve.wait_ge(L["l_og"], t + 1)
                nc.vector.tensor_tensor(l_h[:, t, :], l_h[:, t, :], l_o[:, t, :],
                                        ALU.mult).then_inc(L["l_tok"], 1)
            for b in range(TC // 2):
                dve.wait_ge(L["l_yhi"], b + 1)
                nc.vector.tensor_tensor(pair(ytlo, b), ps[:, 4 + b, :], pair(ythi, b).bitcast(F32),
                                        ALU.subtract).then_inc(L["l_ylo"], 1)

        def ml_gpsimd(pool):
            pool.wait_ge(gain_loaded, 32)
            for t in range(TT):
                pool.wait_ge(L["l_oc"], t + 1)
                nc.gpsimd.tensor_tensor(l_o[:, t, :], l_o[:, t, :], l_gain, ALU.mult) \
                    .then_inc(L["l_og"], 1)

        mtril = sb("mtril", [P, S])
        lam_rows = sb("lam_rows", [1, 4, DH])
        lam_t = sb("lam_t", [1, 2, DH])
        lam_e = sb("lam_e", [1, 2])
        ang = sb("ang", [P, TT, 3, ROPE // 2 + ROT // 2])
        lam_s = sem("lam_s")
        lam_x = sem("lam_x")
        lam_b = sem("lam_b")
        NF = ROPE // 2 + ROT // 2
        N_ROW_DMAS = len(row_dmas) + TT

        def freqs(theta, d):
            return [np.float32(theta) ** np.float32(-np.float32(i) / np.float32(d))
                    for i in range(0, d, 2)]

        def start_gpsimd(pool):
            load_gb(pool, 0)
            nc.gpsimd.memset(ident[:, :], 0.0)
            nc.gpsimd.memset(masks[:, :, :], 0.0)
            nc.gpsimd.memset(mtril[:, :], 0.0)
            nc.gpsimd.memset(sel[:, :, :], 0.0)
            nc.gpsimd.memset(ones[:, :], 1.0)
            for k, f in enumerate(freqs(10000.0, ROPE) + freqs(500000.0, ROT)):
                m = nc.gpsimd.memset(rope_f[:, k:k + 1], float(f))
            m.then_inc(consts, 1)
            pool.wait_ge(consts, 1)
            nc.gpsimd.affine_select(out=ident[:, :], in_=ident[:, :], compare_op=ALU.not_equal,
                                    fill=1.0, base=0, pattern=[[-1, P]], channel_multiplier=1)
            nc.gpsimd.affine_select(out=masks[:, 0, :], in_=masks[:, 0, :], compare_op=ALU.is_ge,
                                    fill=NEG, base=0, pattern=[[-1, P]], channel_multiplier=1)
            nc.gpsimd.affine_select(out=mtril[:, 0:P], in_=mtril[:, 0:P], compare_op=ALU.is_ge,
                                    fill=-NEG, base=0, pattern=[[1, P]], channel_multiplier=-1)
            nc.gpsimd.affine_select(out=sel[:, :, :], in_=sel[:, :, :], compare_op=ALU.not_equal,
                                    fill=1.0, base=0, pattern=[[1, MH], [0, P]],
                                    channel_multiplier=-1).then_inc(consts, 1)

        def start_scalar_loads(act):
            for k, r, src, n in row_dmas:
                act.dma_start(par_rows[r:r + n, k, :], src).then_inc(row_loaded, 16)
            for t in range(TT):
                act.dma_start(pos_i[:, t:t + 1], a["positions"][0, t * P:(t + 1) * P].rearrange(
                    "(p a) -> p a", a=1)).then_inc(row_loaded, 16)
            for k, w in enumerate(("q1", "k1", "q2", "k2")):
                act.dma_start(lam_rows[:, k, :], a[f"diff_lambda_{w}"]).then_inc(lam_loaded, 16)

        def start_tensor(pe):
            pe.wait_ge(consts, 2)
            pe.wait_ge(x_loaded, 16)
            for c in range(KC):
                for t in range(TT):
                    m = T(tchunk(c, t * P, P), x[:, t, c * P:(c + 1) * P])
                if c % 2:
                    m.then_inc(ln_t, 1)
            pe.wait_ge(row_loaded, 16 * N_ROW_DMAS)
            for k in range(PAR_TILES):
                n = min(P, NPAR - k * P)
                m = T(ps[:, k, 0:n], par_rows[0:n, k, :])
            m.then_inc(par_t, 1)
            pe.wait_ge(lam_x, 1)
            nc.tensor.matmul(ps[:, 3, 0:2], ones[0:1, 0:P], lam_e[:, :], start=True,
                             stop=True).then_inc(lam_b, 1)
            pe.wait_ge(par_c, 2)

        def start_scalar(act, split):
            for b in range(BC):
                act.wait_ge(ln_t, b + 1)
                nc.scalar.activation(pair(xthi, b), ps[:, 4 + b, :], ACT.Copy).then_inc(x_hi, 1)
            split.after(None)
            act.wait_ge(lam_s, 1)
            nc.scalar.activation(lam_e[:, :], lam_e[:, :], ACT.Exp).then_inc(lam_x, 1)
            act.wait_ge(rope_ang, 1)
            nc.scalar.activation(ang[:, :, 1, :], ang[:, :, 0, :], ACT.Sin).then_inc(rope_sin, 1)
            nc.scalar.activation(ang[:, :, 2, :], ang[:, :, 0, :], ACT.Sin,
                                 scale=0.5).then_inc(rope_sin, 1)

        def start_vector(dve, link, split):
            for b in range(BC):
                dve.wait_ge(x_hi, b + 1)
                nc.vector.tensor_tensor(pair(xtlo, b), ps[:, 4 + b, :], pair(xthi, b).bitcast(F32),
                                        ALU.subtract).then_inc(x_lo, 1)
            split.after(None)
            dve.wait_ge(lam_loaded, 64)
            l4 = lam_rows[:, :, :].rearrange("p (a b) e -> p a b e", b=2)
            link(nc.vector.tensor_tensor(lam_t[:, :, :], l4[:, :, 0, :], l4[:, :, 1, :], ALU.mult))
            nc.vector.tensor_reduce(out=lam_e[:, :], in_=lam_t[:, :, :], axis=AX.X,
                                    op=ALU.add).then_inc(lam_s, 1)
            dve.wait_ge(consts, 1)
            dve.wait_ge(row_loaded, 16 * N_ROW_DMAS)
            link(nc.vector.tensor_copy(pos_f[:, :], pos_i[:, :]))
            for t in range(TT):
                link.mark(nc.vector.tensor_scalar(ang[:, t, 0, :], rope_f[:, :], pos_f[:, t:t + 1],
                                                  None, ALU.mult))
            dve.wait_ge(link.s, link.n)
            th, turns = ang[:, :, 0, :], ang[:, :, 1, :]
            link(nc.vector.tensor_scalar(turns, th, 1.0 / (2 * math.pi), MAGIC_ROUND, ALU.mult, ALU.add))
            link(nc.vector.tensor_scalar_add(turns, turns, -MAGIC_ROUND))
            c1 = 6.28125
            c2 = float(np.float32(np.round((2 * math.pi - c1) * 2 ** 21) / 2 ** 21))
            c3 = float(np.float32(2 * math.pi - c1 - c2))
            for c in (c1, c2, c3):
                link(nc.vector.scalar_tensor_tensor(out=th, in0=turns, scalar=-c, in1=th,
                                                    op0=ALU.mult, op1=ALU.add))
            nc.vector.tensor_scalar(th, th, 3.1415925, -3.1415925, ALU.min,
                                    ALU.max).then_inc(rope_ang, 1)
            dve.wait_ge(rope_sin, 2)
            half = ang[:, :, 2, :]
            link(nc.vector.tensor_tensor(half, half, half, ALU.mult))
            link(nc.vector.tensor_scalar(half, half, -2.0, 1.0, ALU.mult, ALU.add))
            for tb, lo, n in ((rope_m, 0, ROPE // 2), (rope_d, ROPE // 2, ROT // 2)):
                cos, sin = ang[:, :, 2, lo:lo + n], ang[:, :, 1, lo:lo + n]
                link.mark(nc.vector.tensor_copy(tb[:, :, 0, 0:n], cos))
                link.mark(nc.vector.tensor_copy(tb[:, :, 0, n:2 * n], cos))
                link.mark(nc.vector.tensor_scalar(tb[:, :, 1, 0:n], sin, -1.0, None, ALU.mult))
                link.mark(nc.vector.tensor_copy(tb[:, :, 1, n:2 * n], sin))
            dve.wait_ge(par_t, 1)
            for k in range(PAR_TILES):
                n = min(P, NPAR - k * P)
                m = nc.vector.tensor_copy(par[:, k * P:k * P + n], ps[:, k, 0:n])
                if k < PAR_TILES - 1:
                    link.mark(m)
            m.then_inc(par_c, 1)
            dve.wait_ge(par_c, 1)
            dve.wait_ge(link.s, link.n)
            link.mark(nc.vector.tensor_scalar(small[:, 61:62], col("subln"), 1.0 - LAMBDA_INIT, None,
                                              ALU.mult))
            dve.wait_ge(lam_b, 1)
            nc.vector.tensor_copy(small[:, 62:64], ps[:, 3, 0:2]).then_inc(par_c, 1)
            dve.wait_ge(par_c, 2)
            link(nc.vector.scalar_tensor_tensor(out=lam, in0=small[:, 63:64], scalar=LAMBDA_INIT,
                                                in1=small[:, 62:63], op0=ALU.subtract,
                                                op1=ALU.subtract))

        def end_vector(dve, link):
            dve.wait_ge(gb_loaded, 32 * N_LN)
            dve.wait_ge(ln_z, TT * N_LN)
            for t in range(TT):
                link(nc.vector.tensor_tensor(x[:, t, :], x[:, t, :], gb[:, 0, :], ALU.mult))
                nc.vector.tensor_tensor(x[:, t, :], x[:, t, :], gb[:, 1, :],
                                        ALU.add).then_inc(x_new, 1)

        lasts = [mla_u[-1], ffns[0].first["D", ffns[0].steps - 1], diff_u[-1],
                 ffns[1].first["D", ffns[1].steps - 1], ffns[2].first["D", ffns[2].steps - 1],
                 conv_u[-1], ffns[3].first["D", ffns[3].steps - 1],
                 ffns[4].first["D", ffns[4].steps - 1], ml_u[-1],
                 ffns[5].first["D", ffns[5].steps - 1]]
        stages = ["mla", 0, "diff", 1, 2, "conv", 3, 4, "ml", 5]

        @block.sync
        def _(sp):
            sp.dma_start(x[:, :, :], a["x"][0].rearrange("(t p) d -> p t d", p=P)).then_inc(x_loaded, 16)
            for item in order:
                if isinstance(item, FFN):
                    ffn_sync(sp, item)
                else:
                    load(sp, item)
            for t in range(TT):
                sp.wait_ge(x_new, 2 * (N_LN - 1) + t + 1)
                sp.dma_start(out[0, t * P:(t + 1) * P, :], x[:, t, :]).then_inc(out_done, 16)
            sp.wait_ge(out_done, 16 * TT)

        @block.gpsimd
        def _(pool):
            start_gpsimd(pool)
            pool.wait_ge(m_ylo, KC)
            pool.dma_start(mem_tok, a["mem_2"][0].rearrange("(t p) d -> p t d", p=P)) \
                .then_inc(mem_loaded, 16)
            for n in range(N_LN - 1):
                if stages[n] == "ml":
                    ml_gpsimd(pool)
                ln_gpsimd(pool, n)
                if n == 7:
                    pool.dma_start(l_gain, a["head_norm_g_2"][0].rearrange("h e -> (h e)").rearrange(
                        "(a n) -> a n", a=1).broadcast_to([P, DTOK])).then_inc(gain_loaded, 16)
                    pool.dma_start(g_bias[:, :], a["b_gates_2"].broadcast_to([P, 2 * MH])) \
                        .then_inc(gain_loaded, 16)

        @block.scalar
        def _(act):
            link, split = Chain(act, act_step), Splitter(act, split_hi)
            start_scalar_loads(act)
            start_scalar(act, split)
            act.wait_ge(par_c, 1)
            mixers = {"mla": mla_scalar, "diff": diff_scalar, "conv": conv_scalar, "ml": ml_scalar}
            for n, stage in enumerate(stages):
                if stage in mixers:
                    mixers[stage](act, link, split)
                    for u in {"mla": mla_u[-4:], "diff": diff_u[-4:], "conv": conv_u[-4:],
                              "ml": ml_u[-4:]}[stage]:
                        split.after(u)
                else:
                    f = ffns[stage]
                    ffn_scalar(act, f, ffn_base[id(f)], split,
                               (lambda: mem_scalar_t(act, range(4, KC))) if stage == 0 else None)
                    split.after(lasts[n])
                    if stage == 0:
                        mem_scalar(act, split)
                if n < N_LN - 1:
                    ln_scalar(act, n)
                if n == 0:
                    mem_scalar_t(act, range(4))

        @block.vector
        def _(dve):
            link, split = Chain(dve, dve_step), Splitter(dve, split_lo)
            start_vector(dve, link, split)
            mixers = {"mla": mla_vector, "diff": diff_vector, "conv": conv_vector, "ml": ml_vector}
            for n, stage in enumerate(stages):
                if stage in mixers:
                    mixers[stage](dve, link, split)
                    for u in {"mla": mla_u[-4:], "diff": diff_u[-4:], "conv": conv_u[-4:],
                              "ml": ml_u[-4:]}[stage][:-1]:
                        split.after(u)
                else:
                    f = ffns[stage]
                    ffn_vector(dve, f, ffn_base[id(f)], split,
                               (lambda: mem_vector_t(dve, range(4, KC))) if stage == 0 else None)
                ln_vector(dve, link, n, lasts[n])
                split.after(lasts[n])
                if stage == 0:
                    mem_vector(dve, split)
                if n < N_LN - 1:
                    ln_vector_t(dve, link, n)
                if n == 0:
                    mem_vector_t(dve, range(4))
            end_vector(dve, link)

        @block.tensor
        def _(pe):
            start_tensor(pe)
            mixers = {"mla": mla_tensor, "diff": diff_tensor, "conv": conv_tensor, "ml": ml_tensor}
            for n, stage in enumerate(stages):
                if stage in mixers:
                    mixers[stage](pe)
                else:
                    f = ffns[stage]
                    if stage == 0:
                        mem_tensor_t(pe, range(4))
                    ffn_tensor(pe, f, ffn_base[id(f)],
                               (lambda: mem_tensor_t(pe, range(4, KC))) if stage == 0 else None)
                    if stage == 0:
                        mem_tensor(pe)
                        pe.wait_ge(mem_c, 4)
                if n < N_LN - 1:
                    ln_tensor(pe, n)


INPUTS = ["x", "positions", "ln_mix_g", "ln_mix_b", "mla_w_dq", "mla_q_norm", "mla_w_uq", "mla_w_dkv",
          "mla_kv_norm", "mla_w_ukv", "mla_w_o", "diff_w_qkv", "diff_lambda_q1", "diff_lambda_k1",
          "diff_lambda_q2", "diff_lambda_k2", "diff_subln", "diff_w_o", "ln_ffn_g", "ln_ffn_b",
          "ffn_w_up", "ffn_w_down", "mem_2", "ln_g_2", "ln_b_2", "ffn_w_gate_2", "ffn_w_up_2",
          "ffn_w_down_2", "w_kv_mem_2", "w_out_2", "w_in_conv_2", "conv_w_2", "w_in_mlstm_2",
          "b_gates_2", "qk_conv_w_2", "head_norm_g_2"]


def kernel(**inputs):
    import concourse.bacc as bacc
    from concourse.bass_utils import run_bass_kernel_spmd

    nc = bacc.Bacc("TRN2", target_bir_lowering=False, num_devices=1,
                   dynamic_dma_scratch_size=8192)
    arrays, aps = {}, {}
    for name in INPUTS:
        v = np.ascontiguousarray(inputs[name])
        arrays[f"in_{name}"] = v
        aps[name] = nc.dram_tensor(f"in_{name}", v.shape, mybir.dt.from_np(v.dtype),
                                   kind="ExternalInput").ap()
    out = nc.dram_tensor("out", aps["x"].shape, F32, kind="ExternalOutput").ap()
    build(nc, aps, out)
    got = run_bass_kernel_spmd(nc, [arrays], core_ids=[0])
    return got.results[0]["out"]
```

```python
import math
from contextlib import ExitStack

import numpy as np

import concourse.bass as bass
from concourse import mybir

F32 = mybir.dt.float32
F32R = mybir.dt.float32r
I32 = mybir.dt.int32
ALU = mybir.AluOpType
ACT = mybir.ActivationFunctionType
AX = mybir.AxisListType

P = 128
SLOTS = 4
LN_EPS = 1e-5
RMS_EPS = 1e-6
NEG = -1e30
MAGIC_ROUND = 1.5 * 2.0 ** 23
RSQRT_SEED = float(0x5F3759DF)


class Unit:

    def __init__(self, slot, use, src, dims):
        self.slot, self.use, self.src, self.dims = slot, use, src, dims
        self.size = int(np.prod(dims))
        self.at = self.free = 0


def build(nc, a, out):
    S, D = a["x"].shape[1:]
    TT = S // P
    KC = D // P
    BC = KC // 2
    NMEM = a["mem_2"].shape[1]
    assert TT == 2 and NMEM == S
    QL = a["mla_w_dq"].shape[2]
    KVL = a["mla_kv_norm"].shape[1]
    ROPE = a["mla_w_dkv"].shape[2] - KVL
    H1 = 8
    NOPE = a["mla_w_uq"].shape[2] // H1 - ROPE
    VD = a["mla_w_ukv"].shape[2] // H1 - NOPE
    DH = a["diff_lambda_q1"].shape[1]
    ROT = DH // 4
    XH, XD = 4, D // 16
    DXA = XH * XD
    DTOK = D - DXA
    MH = 4
    MD = DTOK // MH
    CW = a["conv_w_2"].shape[1]
    QW = a["qk_conv_w_2"].shape[1]
    ALPHA = 4 ** 0.25
    LAMBDA_INIT = 0.8 - 0.6 * math.exp(-0.3)
    N_LN = 10
    QC, VC = QL // P, KVL // P
    TC = DTOK // P
    assert NOPE == VD == 2 * DH == P and ROPE == XD == DH == 64

    ctx = ExitStack()
    with ctx:
        def sb(name, shape, dt=F32):
            return ctx.enter_context(nc.sbuf_tensor(name, shape, dt))

        def sem(name):
            return ctx.enter_context(nc.semaphore(name))

        SLOT = 2 * D
        raw = sb("raw", [P, SLOTS, SLOT])
        whi = sb("whi", [P, SLOTS, SLOT], F32R)
        wlo = sb("wlo", [P, SLOTS, SLOT], F32R)
        xthi = sb("xthi", [P, KC, S], F32R)
        xtlo = sb("xtlo", [P, KC, S], F32R)
        ythi = sb("ythi", [P, KC, S], F32R)
        ytlo = sb("ytlo", [P, KC, S], F32R)
        hhi = sb("hhi", [P, 2, S], F32R)
        hlo = sb("hlo", [P, 2, S], F32R)
        x = sb("x", [P, TT, D])
        res = sb("res", [P, TT, D])
        gb = sb("gb", [P, 2, D])
        kvm = sb("kvm", [P, 2, 2, 2 * S])
        ARENA = 9100
        arena = sb("arena", [P, ARENA])
        ident = sb("ident", [P, P])
        masks = sb("masks", [P, 2, P])
        rope_f = sb("rope_f", [P, ROPE // 2 + ROT // 2])
        rope_m = sb("rope_m", [P, TT, 2, ROPE])
        rope_d = sb("rope_d", [P, TT, 2, ROT])
        pos_i = sb("pos_i", [P, TT], I32)
        pos_f = sb("pos_f", [P, TT])
        ones = sb("ones", [P, S])
        sel = sb("sel", [MH, MH, P])
        stats = sb("stats", [P, 8, 6])
        mv = sb("mv", [P, 8, 2])
        rs = sb("rs", [P, 16])
        nt = sb("nt", [P, 2, 16])
        small = sb("small", [P, 96])

        ps = ctx.enter_context(nc.psum_tensor("ps", [P, 8, 512], F32))

        class Arena:
            def __init__(self, base=0):
                self.at = base

            def take(self, *shape):
                n = int(np.prod(shape))
                v = arena[:, self.at:self.at + n]
                self.at += n
                assert self.at <= ARENA, self.at
                if len(shape) == 1:
                    return v
                names = "abcd"[:len(shape)]
                return v.rearrange(f"p ({' '.join(names)}) -> p {' '.join(names)}",
                                   **{n_: s_ for n_, s_ in zip(names[1:], shape[1:])})

        def layer_norm_params(n):
            if n < 4:
                kind = ("mix", "ffn")[n % 2]
                return [a[f"ln_{kind}_{w}"][n // 2] for w in "gb"]
            return [a[f"ln_{w}_2"][(n - 4) // 3, (n - 4) % 3] for w in "gb"]

        rows = []
        for n in range(N_LN - 1):
            for w, src in zip("gb", layer_norm_params(n)):
                rows.append((f"ln{n}{w}", src.rearrange("(c p) -> c p", p=P)))
        rows.append(("q_norm", a["mla_q_norm"][0].rearrange("(c p) -> c p", p=P)))
        rows.append(("kv_norm", a["mla_kv_norm"][0].rearrange("(c p) -> c p", p=P)))
        rows.append(("subln", a["diff_subln"]))
        rows.append(("conv_w", a["conv_w_2"][0].rearrange("w (c p) -> (w c) p", p=P)))
        rows.append(("qk_conv_w", a["qk_conv_w_2"][0].rearrange("w (c p) -> (w c) p", p=P)))
        COL, row_dmas, at = {}, [], 0
        for name, src in rows:
            COL[name] = at
            n, done = src.shape[0], 0
            while done < n:
                k = min(n - done, P - at % P)
                row_dmas.append((at // P, at % P, src[done:done + k], k))
                done, at = done + k, at + k
        NPAR = at
        par = sb("par", [P, NPAR])
        PAR_TILES = -(-NPAR // P)
        assert PAR_TILES <= 3
        par_rows = res[:, 0, 0:PAR_TILES * P].rearrange("p (k n) -> p k n", n=P)

        def col(name, c=0):
            return par[:, COL[name] + c:COL[name] + c + 1]

        users = [[] for _ in range(SLOTS)]
        order = []
        turn = [SLOTS - 1]
        clock = [0]
        barrier = [0]

        def new_unit(slot, src, dims, at=None):
            u = Unit(slot, len(users[slot]) + 1, src, dims)
            if at is None:
                clock[0] += 1
                at = clock[0]
            u.at = at
            u.free = max(barrier[0], users[slot][-1].at if users[slot] else 0)
            u.dmas = dims[0] if len(dims) == 3 else 1
            u.loaded = (users[slot][-1].loaded if users[slot] else 0) + 16 * u.dmas
            users[slot].append(u)
            return u

        def units(srcs):
            got = []
            for src, dims in srcs:
                u = new_unit(turn[0] % SLOTS, src, dims)
                turn[0] += 1
                got.append(u)
                order.append(u)
            return got

        def by_rows(w, n, k):
            v = w.rearrange("(c p) n -> p c n", p=P)
            return [(v[:, c:c + k, :], (k, n)) for c in range(0, w.shape[0] // P, k)]

        def by_cols(w, starts, n=2 * P):
            v = w.rearrange("(c p) n -> p c n", p=P)
            return [(v[:, :, s:s + n], (w.shape[0] // P, n)) for s in starts]

        class FFN:

            def __init__(self, up, gate, down):
                self.gated = gate is not None
                self.wup, self.wgate = (w if w is None else w.rearrange("(c p) n -> p c n", p=P)
                                        for w in (up, gate))
                self.wdown = down.rearrange("(c p) n -> p c n", p=P)
                self.steps = up.shape[1] // (2 * P)
                self.per = 1 if self.gated else 2
                self.kinds = "GUD" if self.gated else "UD"
                self.first = {}
                for s in range(self.steps):
                    for k in self.kinds:
                        src, dims = self.source(k, s, 0)
                        self.first[k, s] = new_unit(self.slot(k, s), src, dims,
                                                    clock[0] + 4 * s + {"G": 1, "U": 2, "D": 7}[k])
                clock[0] += 4 * self.steps + 8
                barrier[0] = self.first["U", self.steps - (1 if self.gated else 2)].at
                turn[0] = 0

            def slot(self, kind, s):
                if self.gated and kind == "D" and s == self.steps - 1:
                    return 3
                return "GUD".index(kind) if self.gated else "UD".index(kind) + 2 * (s % 2)

            def source(self, kind, s, i):
                if kind == "D":
                    c = 2 * s
                    src = (self.wdown[:, c:c + 2, :] if isinstance(i, int) and i == 0 else
                           self.wdown[:, bass.ds(i * (2 * self.per) + c, 2), :])
                    return src, (2, D)
                w = self.wgate if kind == "G" else self.wup
                c = 2 * P * s
                src = (w[:, :, c:c + 2 * P] if isinstance(i, int) and i == 0 else
                       w[:, :, bass.ds(i * (2 * P * self.per) + c, 2 * P)])
                return src, (KC, 2 * P)

        uq = a["mla_w_uq"][0].rearrange("(c p) (h e) -> p c h e", p=P, e=NOPE + ROPE)
        ukv = a["mla_w_ukv"][0].rearrange("(c p) (h e) -> p c h e", p=P, e=NOPE + VD)
        mla_u = units(by_rows(a["mla_w_dq"][0], QL, 4) + by_rows(a["mla_w_dkv"][0], KVL + ROPE, 4)
                      + [(uq[:, :, :, NOPE:], (QC, H1, ROPE)),
                         (uq[:, :, 0:4, 0:NOPE], (QC, 4, NOPE)),
                         (uq[:, :, 4:8, 0:NOPE], (QC, 4, NOPE)),
                         (ukv[:, :, :, 0:NOPE], (VC, H1, NOPE)),
                         (ukv[:, :, :, NOPE:], (VC, H1, VD))]
                      + by_rows(a["mla_w_o"][0], D, 2))

        def ffn(up, gate, down):
            f = FFN(up, gate, down)
            order.append(f)
            return f

        ffns = [ffn(a["ffn_w_up"][0], None, a["ffn_w_down"][0])]
        mem_u = units([u for l in range(2) for u in by_cols(a["w_kv_mem_2"][l], [0, 2 * P])])
        diff_u = units([(v[:, c:c + 2, g * D:(g + 1) * D], (2, D))
                        for v in [a["diff_w_qkv"][0].rearrange("(c p) n -> p c n", p=P)]
                        for g in range(3) for c in range(0, KC, 2)]
                       + by_rows(a["diff_w_o"][0], D, 2))
        ffns.append(ffn(a["ffn_w_up"][1], None, a["ffn_w_down"][1]))

        def swiglu(l, i):
            return ffn(a["ffn_w_up_2"][l, i], a["ffn_w_gate_2"][l, i], a["ffn_w_down_2"][l, i])

        ffns.append(swiglu(0, 0))
        conv_u = units(by_cols(a["w_in_conv_2"][0],
                               [g * DTOK + 2 * P * i for i in range(TC // 2) for g in (1, 2, 0)]
                               + [3 * DTOK]) + by_rows(a["w_out_2"][0], D, 2))
        ffns.append(swiglu(0, 1))
        ffns.append(swiglu(1, 0))
        wm = a["w_in_mlstm_2"][0]
        wmv = wm.rearrange("(c p) n -> p c n", p=P)
        ml_u = units(by_cols(wm, [2 * P * i for i in range(TC)])
                     + by_cols(wm, [4 * DTOK], 2 * MH) + by_cols(wm, [4 * DTOK + 2 * MH], DXA)
                     + [(wmv[:, c:c + 2, g * DTOK:(g + 1) * DTOK], (2, DTOK))
                        for g in (2, 3) for c in range(0, KC, 2)]
                     + by_rows(a["w_out_2"][1], D, 2))
        ffns.append(swiglu(1, 1))

        w_loaded = [sem(f"w_loaded{s}") for s in range(SLOTS)]
        w_hi = [sem(f"w_hi{s}") for s in range(SLOTS)]
        w_lo = [sem(f"w_lo{s}") for s in range(SLOTS)]
        w_done = [sem(f"w_done{s}") for s in range(SLOTS)]

        def slot_view(t, u):
            v = t[:, u.slot, 0:u.size]
            if len(u.dims) == 2:
                return v.rearrange("p (a b) -> p a b", b=u.dims[1])
            return v.rearrange("p (a b c) -> p a b c", b=u.dims[1], c=u.dims[2])

        def load(sp, u, src=None, i=0):
            if isinstance(i, int):
                if u.use + i > 1:
                    sp.wait_ge(w_lo[u.slot], u.use + i - 1)
            else:
                sp.wait_ge(w_lo[u.slot], i + (u.use - 1))
            src = u.src if src is None else src
            if u.dmas == 1:
                sp.dma_start(slot_view(raw, u), src).then_inc(w_loaded[u.slot], 16)
            else:
                for c in range(u.dmas):
                    sp.dma_start(slot_view(raw, u)[:, c], src[:, c]).then_inc(w_loaded[u.slot], 16)

        def split_hi(act, u, i=0):
            if isinstance(i, int):
                act.wait_ge(w_loaded[u.slot], u.loaded + 16 * i)
                if u.use + i > 1:
                    act.wait_ge(w_done[u.slot], u.use + i - 1)
            else:
                act.wait_ge(w_loaded[u.slot], i * 16 + u.loaded)
                act.wait_ge(w_done[u.slot], i + (u.use - 1))
            nc.scalar.activation(whi[:, u.slot, 0:u.size], raw[:, u.slot, 0:u.size],
                                 ACT.Copy).then_inc(w_hi[u.slot], 1)

        def split_lo(eng, u, i=0, ops=None):
            eng.wait_ge(w_hi[u.slot], i + u.use)
            (ops or nc.vector).tensor_tensor(wlo[:, u.slot, 0:u.size], raw[:, u.slot, 0:u.size],
                                    whi[:, u.slot, 0:u.size].bitcast(F32),
                                    ALU.subtract).then_inc(w_lo[u.slot], 1)

        def wait_split(pe, u, i=0):
            pe.wait_ge(w_lo[u.slot], i + u.use)

        def wait_done(eng, u, i=0):
            eng.wait_ge(w_done[u.slot], i + u.use)

        flat = []
        for item in order:
            if isinstance(item, FFN):
                head = [("G", 0), ("U", 0), ("D", 0)] if item.gated else \
                       [("U", 0), ("D", 0), ("U", 1), ("D", 1)]
                flat += [item.first[k] for k in head]
            else:
                flat.append(item)

        class Splitter:
            def __init__(self, eng, split, others=()):
                self.eng, self.split, self.others, self.n = eng, split, others, 0

            def after(self, u, most=SLOTS):
                done = 0
                while done < most and self.n < len(flat) and flat[self.n].free <= (u.at if u else 0):
                    if flat[self.n] not in self.others:
                        self.split(self.eng, flat[self.n])
                    self.n += 1
                    done += 1

        row_loaded = sem("row_loaded")
        x_loaded = [sem(f"x_loaded{t}") for t in range(TT)]
        mem_loaded = sem("mem_loaded")
        consts = sem("consts")
        gb_loaded = sem("gb_loaded")
        lam_loaded = sem("lam_loaded")
        gain_loaded = sem("gain_loaded")
        dve_step = sem("dve_step")
        act_step = sem("act_step")
        par_t = sem("par_t")
        par_c = sem("par_c")
        rope_ang = sem("rope_ang")
        rope_sin = sem("rope_sin")
        acc_bank = sem("acc_bank")
        ln_r = sem("ln_r")
        ln_z = sem("ln_z")
        ln_z2 = sem("ln_z2")
        ln_x = sem("ln_x")
        ln_t = sem("ln_t")
        x_32 = sem("x_32")
        x_hi = sem("x_hi")
        x_lo = sem("x_lo")
        x_new = sem("x_new")
        f_act = sem("f_act")
        f_h = sem("f_h")
        f_hi = sem("f_hi")
        f_lo = sem("f_lo")
        out_done = sem("out_done")

        block = ctx.enter_context(nc.Block())

        class Chain:

            def __init__(self, eng, s):
                self.eng, self.s, self.n = eng, s, 0

            def __call__(self, ins):
                self.n += 1
                ins.then_inc(self.s, 1)
                self.eng.wait_ge(self.s, self.n)

            def mark(self, ins):
                self.n += 1
                ins.then_inc(self.s, 1)

        def rsqrt(link, y, v, k):
            t = nt[:, 0, 0:k]
            link(nc.vector.tensor_scalar(y.bitcast(I32), v.bitcast(I32), -0.5, RSQRT_SEED,
                                         ALU.mult, ALU.add))
            for _ in range(3):
                link(nc.vector.scalar_tensor_tensor(out=t, in0=y, scalar=-0.5, in1=y,
                                                    op0=ALU.mult, op1=ALU.mult))
                link(nc.vector.tensor_tensor(t, t, v, ALU.mult))
                link(nc.vector.scalar_tensor_tensor(out=y, in0=t, scalar=1.5, in1=y,
                                                    op0=ALU.add, op1=ALU.mult))

        def product(out_, w, xs, first, last):
            (wh, wlow), (xh, xl) = w, xs
            m = None
            for n, (p, q) in enumerate(((wh, xh), (wh, xl), (wlow, xh))):
                m = nc.tensor.matmul(out_, p, q, start=first and n == 0, stop=last and n == 2,
                                     skip_group_check=True)
            return m

        def w_parts(u, *ix):
            return tuple(slot_view(t, u)[(slice(None), *ix)] for t in (whi, wlo))

        def t_parts(pair, c, lo=0, n=S):
            return tuple(t[:, c, lo:lo + n] for t in pair)

        xt, yt = (xthi, xtlo), (ythi, ytlo)

        def columns_product(pe, u, c0, outs, act_pair=xt, width=P, off=0, kc=KC, x_from=None):
            for j, o in enumerate(outs):
                for c in range(kc):
                    if x_from is not None and j == 0:
                        pe.wait_ge(x_lo, x_from + c // 2 + 1)
                    m = product(o, w_parts(u, c, slice(off + j * width, off + (j + 1) * width)),
                                t_parts(act_pair, c0 + c), c == 0, c == kc - 1)
            return m

        def acc_product(pe, u, pair, chunk0, first, last, half=False):
            for t in range(TT):
                for n in range(2):
                    for c in range(u.dims[0]):
                        m = product(ps[:, 2 * t + n, :],
                                    t_parts(pair, chunk0 + c, t * P, P),
                                    w_parts(u, c, slice(n * 512, n * 512 + 512)),
                                    first and c == 0, last and c == u.dims[0] - 1)
                    if half and 2 * t + n < 3:
                        m.then_inc(acc_bank, 1)
            m.then_inc(w_done[u.slot], 1)

        def T(o, i, n=P):
            return nc.tensor.transpose(o, i, ident[0:i.shape[0], 0:i.shape[0]])

        def tchunk(c, lo=0, n=S):
            return ps[:, 4 + c // 2, (c % 2) * S + lo:(c % 2) * S + lo + n]

        def ln_tensor(pe, n):
            for b in range(BC):
                for t in range(TT):
                    if b == 0:
                        pe.wait_ge(ln_z, TT * n + t + 1)
                    if b == BC // 2:
                        pe.wait_ge(ln_z2, TT * n + t + 1)
                    for c in (2 * b, 2 * b + 1):
                        m = T(tchunk(c, t * P, P), x[:, t, c * P:(c + 1) * P])
                m.then_inc(ln_t, 1)

        def pair(t, b):
            return t[:, 2 * b:2 * b + 2, :].rearrange("p a b -> p (a b)")

        def shifted(b):
            return res[:, b // 2, (b % 2) * 2 * S:(b % 2 + 1) * 2 * S]

        ln_root, ln_shift = rs[:, 0:TT], small[:, 90:90 + TT]

        def ln_chunk(n, b, j, op):
            c = 2 * b + j
            return op(shifted(b)[:, j * S:(j + 1) * S], tchunk(c), col(f"ln{n}g", c), col(f"ln{n}b", c))

        def ln_scalar_z(act, n):
            act.wait_ge(ln_r, n + 1)
            for t in range(TT):
                nc.scalar.activation(x[:, t, D // 2:], res[:, t, D // 2:], ACT.Identity,
                                     bias=ln_shift[:, t:t + 1],
                                     scale=ln_root[:, t:t + 1]).then_inc(ln_z2, 1)

        def ln_scalar(act, n):
            def shift_bank(b):
                act.wait_ge(ln_t, BC * (n + 1) + b + 1)
                act.wait_ge(ln_z2, TT * (n + 1))
                for j in range(2):
                    ln_chunk(n, b, j, lambda o, i, g, s: nc.scalar.activation(
                        o, i, ACT.Identity, bias=s, scale=g)).then_inc(ln_x, 1)

            def high(b):
                if b % 2:
                    act.wait_ge(ln_x, 4 * n + b + 1)
                else:
                    act.wait_ge(x_32, BC // 2 * n + b // 2 + 1)
                nc.scalar.activation(pair(xthi, b), shifted(b), ACT.Copy).then_inc(x_hi, 1)

            for b in range(0, BC, 2):
                high(b)
                shift_bank(b + 1)
                high(b + 1)

        def ln_vector(dve, link, n, last_unit):
            def residual(t, j):
                if 2 * t + j < 3:
                    dve.wait_ge(acc_bank, 3 * n + 2 * t + j + 1)
                else:
                    wait_done(dve, last_unit)
                if t + j == 0 and n > 0:
                    dve.wait_ge(x_new, 2 * n)
                half = slice(j * 512, j * 512 + 512)
                link.mark(nc.vector.scalar_tensor_tensor(
                    out=res[:, t, half], in0=x[:, t, half], scalar=ALPHA,
                    in1=ps[:, 2 * t + j, :], op0=ALU.mult, op1=ALU.add))

            for t in range(TT):
                for j in range(2):
                    residual(t, j)
                    dve.wait_ge(link.s, link.n)
                    link.mark(nc.vector.bn_stats(stats[:, 2 * t + j, :],
                                                 res[:, t, j * 512:(j + 1) * 512]))
            dve.wait_ge(link.s, link.n)
            for t in range(TT):
                link.mark(nc.vector.bn_aggr(mv[:, t, :], stats[:, 2 * t:2 * t + 2, :].rearrange(
                    "p a b -> p (a b)")))
            dve.wait_ge(link.s, link.n)
            v, w, k = nt[:, 1, 0:TT], nt[:, 1, TT:2 * TT], nt[:, 0, 0:TT]
            link.mark(nc.vector.tensor_scalar_add(v, mv[:, 0:TT, 1], LN_EPS))
            link.mark(nc.vector.tensor_scalar(w, mv[:, 0:TT, 1], LN_EPS, -0.5, ALU.add, ALU.mult))
            dve.wait_ge(link.s, link.n - 1)
            link(nc.vector.tensor_scalar(ln_root.bitcast(I32), v.bitcast(I32), -0.5, RSQRT_SEED,
                                         ALU.mult, ALU.add))
            for _ in range(3):
                for t in range(TT):
                    y = ln_root[:, t:t + 1]
                    link.mark(nc.vector.scalar_tensor_tensor(
                        out=k[:, t:t + 1], in0=y, scalar=w[:, t:t + 1], in1=y, op0=ALU.mult,
                        op1=ALU.mult))
                dve.wait_ge(link.s, link.n)
                link(nc.vector.scalar_tensor_tensor(out=ln_root, in0=k, scalar=1.5, in1=ln_root,
                                                    op0=ALU.add, op1=ALU.mult))
            nc.vector.scalar_tensor_tensor(out=ln_shift, in0=mv[:, 0:TT, 0], scalar=-1.0,
                                           in1=ln_root, op0=ALU.mult, op1=ALU.mult).then_inc(ln_r, 1)
            for t in range(TT):
                nc.vector.tensor_scalar(x[:, t, 0:D // 2], res[:, t, 0:D // 2], mv[:, t, 0:1],
                                        ln_root[:, t:t + 1], ALU.subtract,
                                        ALU.mult).then_inc(ln_z, 1)

        def ln_vector_t(dve, link, n):
            def shift_bank(b):
                dve.wait_ge(ln_t, BC * (n + 1) + b + 1)
                for j in range(2):
                    m = ln_chunk(n, b, j, lambda o, i, g, s: nc.vector.tensor_scalar(
                        o, i, g, s, ALU.mult, ALU.add))
                    if j == 0:
                        link.mark(m)
                m.then_inc(x_32, 1)

            def low(b):
                dve.wait_ge(x_hi, BC * (n + 1) + b + 1)
                if b % 2 == 0:
                    dve.wait_ge(x_32, BC // 2 * n + b // 2 + 1)
                    dve.wait_ge(link.s, link.n)
                nc.vector.tensor_tensor(pair(xtlo, b), shifted(b), pair(xthi, b).bitcast(F32),
                                        ALU.subtract).then_inc(x_lo, 1)

            shift_bank(0)
            low(0)
            shift_bank(2)
            for b in range(1, BC):
                low(b)

        def ln_gpsimd(pool, n):
            pool.wait_ge(ln_t, BC * (n + 2))
            pool.wait_ge(gb_loaded, 32 * (n + 1))
            for k, op in enumerate((ALU.mult, ALU.add)):
                for t in range(TT):
                    m = nc.gpsimd.tensor_tensor(x[:, t, :], x[:, t, :], gb[:, k, :], op)
                m.then_inc(x_new, 1)
                pool.wait_ge(x_new, 2 * n + k + 1)
            load_gb(pool, n + 1)

        def load_gb(pool, n):
            for k, src in enumerate(layer_norm_params(n)):
                pool.dma_start(gb[:, k, :], src.rearrange("(a n) -> a n", a=1).broadcast_to([P, D])) \
                    .then_inc(gb_loaded, 16)

        def hidden(f, s):
            return (ythi, ytlo) if own_last(f, s) else (hhi, hlo)

        def own_last(f, s):
            return s == f.steps - 1 and f is not ffns[0]

        def hidden_row(f, s, part):
            return hidden(f, s)[part][:, 0:2, :].rearrange("p a b -> p (a b)")

        GATE, UP = 4, 5

        def ffn_loops(f):
            if f.gated:
                return (2, f.steps - 2), (1, f.steps - 2)
            return (2, (f.steps - 2) // 2), (1, (f.steps - 3) // 2)

        def ffn_sync(sp, f):
            head = [("G", 0), ("U", 0), ("D", 0)] if f.gated else [("U", 0), ("D", 0), ("U", 1), ("D", 1)]
            for k in head:
                load(sp, f.first[k])
            if f.gated:
                for k in "GU":
                    load(sp, f.first[k, 1])
                with sp.Fori(0, f.steps - 2) as i:
                    for k, s in (("G", 2), ("U", 2), ("D", 1)):
                        load(sp, f.first[k, s], f.source(k, s, i)[0], i)
                load(sp, f.first["D", f.steps - 1])
            else:
                with sp.Fori(0, (f.steps - 2) // 2) as i:
                    for j in range(2):
                        for k in "UD":
                            load(sp, f.first[k, 2 + j], f.source(k, 2 + j, i)[0], i)

        def up_bank(f, s):
            return UP if f.gated or s % 2 else GATE

        def ffn_up(pe, f, base, s, i=0):
            for kind in f.kinds[:-1]:
                u = f.first[kind, s]
                bank = up_bank(f, s) if kind == "U" else GATE
                wait_split(pe, u, i)
                if not (isinstance(i, int) and s < f.per):
                    pe.wait_ge(f_act if kind == "G" else f_h, i * f.per + (base + s + 1 - f.per))
                for j in range(2):
                    for c in range(KC):
                        if isinstance(i, int) and s == 0 and j == 0 and kind == f.kinds[0]:
                            pe.wait_ge(x_lo, x_count[id(f)] + c // 2 + 1)
                        m = product(ps[:, bank, j * S:(j + 1) * S],
                                    w_parts(u, c, slice(j * P, (j + 1) * P)), t_parts(xt, c),
                                    c == 0, c == KC - 1)
                m.then_inc(w_done[u.slot], 1)

        def ffn_down(pe, f, base, s, i=0, first=False, last=False):
            u = f.first["D", s]
            wait_split(pe, u, i)
            pe.wait_ge(f_lo, i * f.per + (base + s + 1))
            acc_product(pe, u, hidden(f, s), 0, first, last, half=last)

        def ffn_tensor(pe, f, base, between=None):
            (s0, turns), _ = ffn_loops(f)
            ffn_up(pe, f, base, 0)
            if between:
                between[0]()
            ffn_up(pe, f, base, 1)
            ffn_down(pe, f, base, 0, first=True)
            if between:
                between[1]()
            with pe.Fori(0, turns) as i:
                for j in range(f.per):
                    ffn_up(pe, f, base, s0 + j, i)
                    ffn_down(pe, f, base, s0 + j - 1, i)
            ffn_down(pe, f, base, f.steps - 1, last=True)

        def f_view(k):
            return arena[:, k * 2 * S:(k + 1) * 2 * S]

        def ffn_scalar(act, f, base, split, between=None):
            def features(s, i=0):
                kind = f.kinds[0]
                u = f.first[kind, s]
                wait_done(act, u, i)
                if not (isinstance(i, int) and base + s == 0):
                    act.wait_ge(f_h, i * f.per + (base + s))
                nc.scalar.activation(f_view(0), ps[:, GATE if f.gated else up_bank(f, s), :],
                                     ACT.Silu if f.gated else ACT.Relu).then_inc(f_act, 1)

            def high(s, i=0):
                act.wait_ge(f_h, i * f.per + (base + s + 1))
                if not (isinstance(i, int) and s == 0 or own_last(f, s)):
                    wait_done(act, f.first["D", s - 1], i)
                nc.scalar.activation(hidden_row(f, s, 0), f_view(1),
                                     ACT.Copy).then_inc(f_hi, 1)

            ffn_split_loop(act, f, features, high, split, split_hi, between)

        def ffn_vector(dve, f, base, split, between=None):
            def features(s, i=0):
                dve.wait_ge(f_act, i * f.per + (base + s + 1))
                if f.gated:
                    wait_done(dve, f.first["U", s], i)
                if not (isinstance(i, int) and base + s == 0):
                    dve.wait_ge(f_lo, i * f.per + (base + s))
                nc.vector.scalar_tensor_tensor(out=f_view(1), in0=f_view(0),
                                               scalar=0.5 if f.gated else 1.0,
                                               in1=ps[:, up_bank(f, s), :],
                                               op0=ALU.mult, op1=ALU.mult).then_inc(f_h, 1)

            def low(s, i=0):
                dve.wait_ge(f_hi, i * f.per + (base + s + 1))
                nc.vector.tensor_tensor(hidden_row(f, s, 1), f_view(1),
                                        hidden_row(f, s, 0).bitcast(F32),
                                        ALU.subtract).then_inc(f_lo, 1)

            ffn_split_loop(dve, f, features, low, split, split_lo, between,
                           most=1 if f.gated or f is ffns[0] else 0, early=True)

        def ffn_split_loop(eng, f, features, part, split, split_one, between, most=SLOTS,
                           early=False):
            last = f.steps - 1
            if f.gated:
                if early:
                    split_one(eng, f.first["G", 1])
                    features(0)
                else:
                    features(0)
                    split_one(eng, f.first["G", 1])
                split_one(eng, f.first["U", 1])
                part(0)
                with eng.Fori(0, last - 1) as i:
                    features(1, i)
                    split_one(eng, f.first["G", 2], i)
                    split_one(eng, f.first["U", 2], i)
                    part(1, i)
                    split_one(eng, f.first["D", 1], i)
                split_one(eng, f.first["D", last])
                if early:
                    split.after(f.first["U", last], 1)
                features(last)
                if not early:
                    split.after(f.first["U", last], 1)
                part(last)
                split.after(f.first["D", last - 1], most)
            else:
                features(0)
                split_one(eng, f.first["U", 2])
                part(0)
                if between:
                    between()
                with eng.Fori(0, (last - 3) // 2) as i:
                    for s in (1, 2):
                        features(s, i)
                        split_one(eng, f.first["U", s + 2], i)
                        part(s, i)
                        split_one(eng, f.first["D", s + 1], i)
                features(last - 2)
                split_one(eng, f.first["U", last])
                part(last - 2)
                split_one(eng, f.first["D", last - 1])
                features(last - 1)
                part(last - 1)
                split.after(f.first["U", last - 1])
                split_one(eng, f.first["D", last])
                features(last)
                part(last)
                split.after(f.first["D", last - 1], most)

        ffn_base, n = {}, 0
        for f in ffns:
            ffn_base[id(f)] = n
            n += f.steps
        x_count = {id(f): BC * (k + 1) for f, k in zip(ffns, (0, 2, 3, 5, 6, 8))}

        class Attention:

            def __init__(self, name, heads, maps, causal, scale, mem):
                self.name, self.heads, self.maps, self.causal, self.scale = \
                    name, heads, maps, causal, scale
                self.width = 3 * P if causal else 4 * P
                self.rows = ((0, P), (P, 3 * P)) if causal else ((0, 2 * P), (2 * P, 4 * P))
                self.blocks = [(0, 0, 0), (1, 1, P), (1, 0, 2 * P)] if causal else \
                    [(0, 0, 0), (0, 1, P), (1, 0, 2 * P), (1, 1, 3 * P)]
                self.place = {(0, 0): 0, (1, 0): P, (1, 1): 2 * P} if causal else \
                    {(0, 0): 0, (1, 0): P, (0, 1): 2 * P, (1, 1): 3 * P}
                self.p = mem.take(2, maps, self.width)
                self.pt = mem.take(2, self.width)
                self.scored = sem(f"{name}_scored")
                self.maxed = sem(f"{name}_maxed")
                self.exped = sem(f"{name}_exped")
                self.normed = sem(f"{name}_normed")
                self.turned = sem(f"{name}_turned")
                self.copied = sem(f"{name}_copied")
                self.summed = sem(f"{name}_summed")

            def s_bank(self, h, m):
                return ps[:, (h % 2) * self.maps + m, 0:self.width]

            def tensor(self, pe, score, result, read, count0=0, before_turn=None):
                for i in range(self.heads + 3):
                    if i < self.heads:
                        if i >= 2:
                            pe.wait_ge(self.exped, 2 * self.maps * (i - 1))
                        for m in range(self.maps):
                            last = score(i, m, self.s_bank(i, m))
                        last.then_inc(self.scored, 1)
                    h = i - 2
                    if h == 0 and before_turn:
                        before_turn()
                    if 0 <= h < self.heads:
                        pe.wait_ge(self.normed, h + 1)
                        if h >= 2:
                            pe.wait_ge(self.copied, h - 1)
                        for q, k, c in self.blocks:
                            to = self.place[q, k]
                            last = T(ps[:, 4 + h % 2, to:to + P], self.p[:, h % 2, 0, c:c + P])
                        last.then_inc(self.turned, 1)
                    h = i - 3
                    if 0 <= h < self.heads:
                        pe.wait_ge(self.copied, h + 1)
                        if h >= 2:
                            pe.wait_ge(read, count0 + h - 1)
                        result(h, self.pt[:, h % 2, :], ps[:, 6 + h % 2, :]).then_inc(self.summed, 1)

            def m_at(self, h):
                return small[:, 8 * (h % 2):8 * (h % 2) + 8]

            def vector(self, dve, link, normalise, read=None):
                for i in range(self.heads + 3):
                    if i < self.heads:
                        dve.wait_ge(self.scored, i + 1)
                        if i:
                            dve.wait_ge(self.maxed, i)
                        for m in range(self.maps):
                            bank = self.s_bank(i, m)
                            if self.causal:
                                d = bank[:, 0:2 * P].rearrange("p (a b) -> p a b", b=P)
                                link(nc.vector.tensor_tensor(
                                    d, d, masks[:, 0:1, :].broadcast_to([P, 2, P]), ALU.add))
                            for t, (lo, hi) in enumerate(self.rows):
                                link.mark(nc.vector.tensor_reduce(
                                    out=small[:, 16 + 2 * m + t:17 + 2 * m + t], in_=bank[:, lo:hi],
                                    axis=AX.X, op=ALU.max))
                        dve.wait_ge(link.s, link.n)
                        nc.vector.tensor_scalar(self.m_at(i)[:, 0:2 * self.maps],
                                                small[:, 16:16 + 2 * self.maps], -self.scale, None,
                                                ALU.mult).then_inc(self.maxed, 1)
                    h = i - 1
                    if 0 <= h < self.heads:
                        dve.wait_ge(self.exped, 2 * self.maps * (h + 1))
                        r = small[:, 32:32 + 2 * self.maps]
                        if h:
                            dve.wait_ge(self.normed, h)
                        link(nc.vector.reciprocal(r, self.sums(h)))
                        normalise(link, h, self.p[:, h % 2], r, self.rows, self.normed)
                    h = i - 3
                    if 0 <= h < self.heads and read:
                        read(h)

            def sums(self, h):
                return small[:, 40 + 8 * (h % 2):40 + 8 * (h % 2) + 2 * self.maps]

            def scalar(self, act, read):
                for i in range(self.heads + 3):
                    if i < self.heads:
                        act.wait_ge(self.maxed, i + 1)
                        if i >= 2:
                            act.wait_ge(self.turned, i - 1)
                        for m in range(self.maps):
                            for t, (lo, hi) in enumerate(self.rows):
                                k = 2 * m + t
                                nc.scalar.activation(
                                    self.p[:, i % 2, m, lo:hi], self.s_bank(i, m)[:, lo:hi], ACT.Exp,
                                    bias=self.m_at(i)[:, k:k + 1], scale=self.scale,
                                    accum_out=self.sums(i)[:, k:k + 1]).then_inc(self.exped, 1)
                    h = i - 2
                    if 0 <= h < self.heads:
                        act.wait_ge(self.turned, h + 1)
                        if h >= 2:
                            act.wait_ge(self.summed, h - 1)
                        nc.scalar.activation(self.pt[:, h % 2, :], ps[:, 4 + h % 2, 0:self.width],
                                             ACT.Copy).then_inc(self.copied, 1)
                    h = i - 3
                    if 0 <= h < self.heads:
                        act.wait_ge(self.summed, h + 1)
                        read(h, ps[:, 6 + h % 2, :])

        def scale_rows(link, h, p, r, rows_, done):
            for t, (lo, hi) in enumerate(rows_):
                m = nc.vector.tensor_scalar(p[:, 0, lo:hi], p[:, 0, lo:hi], r[:, t:t + 1], None,
                                            ALU.mult)
                if t == 0:
                    link.mark(m)
            m.then_inc(done, 1)

        A = Arena()
        mla_qn = A.take(H1, S)
        mla_kn = A.take(H1, S)
        mla_qp = A.take(H1 // 2, S)
        mla_kp = A.take(S)
        mla_v = A.take(TT, H1 * VD)
        mla_att = Attention("mla", H1, 1, True, (NOPE + ROPE) ** -0.5, A)
        latent = res[:, :, 0:QL + KVL + P]
        qpe = latent[:, :, 0:H1 * ROPE]
        rope_tmp = mla_att.p.rearrange("p a b c -> p (a b c)")[:, 0:H1 * ROPE]
        m_square = sem("m_square")
        m_latent = sem("m_latent")
        m_turned = sem("m_turned")
        m_hi = sem("m_hi")
        m_lo = sem("m_lo")
        m_qpe = sem("m_qpe")
        m_qpt = sem("m_qpt")
        m_copied = sem("m_copied")
        m_v0 = sem("m_v0")
        m_vcopied = sem("m_vcopied")
        assert QC == 3 and VC == 2
        LC = QC + VC + 1

        def latent_bank(i, lo=0, n=S):
            j = i if i < QC else i - QC + 4
            return ps[:, 4 + j // 2, (j % 2) * S + lo:(j % 2) * S + lo + n]

        def mla_tensor(pe):
            dq, dkv, (qp, qn0, qn1, kn, v), o = mla_u[0:2], mla_u[2:4], mla_u[4:9], mla_u[9:]

            def turn_latents(chunks, before):
                for t in range(TT):
                    pe.wait_ge(m_latent, before + t + 1)
                    for i in chunks:
                        m = T(latent_bank(i, t * P, P), latent[:, t, i * P:(i + 1) * P])
                        if t == TT - 1 and i in (1, QC - 1, QC + VC - 1, LC - 1):
                            m.then_inc(m_turned, 1)

            for group, bank0 in ((dq, 0), (dkv, 2)):
                for j, u in enumerate(group):
                    wait_split(pe, u)
                    for t in range(TT):
                        for c in range(4):
                            if t == 0 and bank0 == 0:
                                pe.wait_ge(x_lo, (4 * j + c) // 2 + 1)
                            m = product(ps[:, bank0 + t, 0:u.dims[1]],
                                        t_parts(xt, 4 * j + c, t * P, P), w_parts(u, c),
                                        4 * j + c == 0, 4 * j + c == KC - 1)
                    m.then_inc(w_done[u.slot], 1)
                    if u is dq[0]:
                        params_tensor(pe)
                    if u is dkv[0]:
                        lambda_tensor(pe)
                        turn_latents(range(QC), 0)
            wait_split(pe, qp)
            pe.wait_ge(m_lo, QC)
            for t in range(TT):
                for c in range(QC):
                    m = product(ps[:, t, :], t_parts(xt, c, t * P, P),
                                tuple(w.rearrange("p a b -> p (a b)") for w in w_parts(qp, c)),
                                c == 0, c == QC - 1)
            m.then_inc(w_done[qp.slot], 1)
            pe.wait_ge(par_c, 2)
            turn_latents(range(QC, LC), TT)
            for u, bank in ((qn0, 2), (qn1, 4)):
                wait_split(pe, u)
                for h in range(4):
                    for c in range(QC):
                        m = product(ps[:, bank + h // 2, (h % 2) * S:(h % 2) * S + S],
                                    w_parts(u, c, h), t_parts(xt, c), c == 0, c == QC - 1)
                m.then_inc(w_done[u.slot], 1)
            wait_split(pe, kn)
            pe.wait_ge(m_lo, QC + VC)
            pe.wait_ge(m_hi, LC)
            for h in range(H1):
                if h == 4:
                    pe.wait_ge(m_copied, 2)
                bank = (6 if h < 4 else 2) + (h % 4) // 2
                for c in range(VC):
                    m = product(ps[:, bank, (h % 2) * S:(h % 2) * S + S], w_parts(kn, c, h),
                                t_parts(xt, QC + c), c == 0, c == VC - 1)
            m.then_inc(w_done[kn.slot], 1)
            wait_split(pe, v)
            pe.wait_ge(m_copied, 4)
            for t in range(TT):
                if t == 1:
                    m.then_inc(m_v0, 1)
                    pe.wait_ge(m_qpe, TT)
                for n in range(2):
                    for c in range(VC):
                        m = product(ps[:, (4, 0)[t] + n, :], t_parts(xt, QC + c, t * P, P),
                                    tuple(w.rearrange("p a b -> p (a b)")
                                          for w in w_parts(v, c, slice(4 * n, 4 * n + 4))),
                                    c == 0, c == VC - 1)
            m.then_inc(w_done[v.slot], 1)
            pe.wait_ge(m_copied, 6)
            for t in range(TT):
                for i in range(H1 // 2):
                    m = T(ps[:, 6 + i // 2, (i % 2) * S + t * P:(i % 2) * S + t * P + P],
                          qpe[:, t, i * P:(i + 1) * P])
            m.then_inc(m_qpt, 1)
            pe.wait_ge(m_copied, 10)
            pe.wait_ge(m_vcopied, 2 * TT)

            def score(h, m_, bank):
                r = slice(ROPE * (h % 2), ROPE * (h % 2) + ROPE)
                for q, ks, lo, hi in ((0, 0, 0, P), (1, 1, P, 2 * P), (1, 0, 2 * P, 3 * P)):
                    qs, kk = slice(q * P, q * P + P), slice(ks * P, ks * P + P)
                    nc.tensor.matmul(bank[:, lo:hi], mla_qn[:, h, qs], mla_kn[:, h, kk],
                                     start=True, stop=False, skip_group_check=True)
                    m = nc.tensor.matmul(bank[:, lo:hi], mla_qp[r, h // 2, qs], mla_kp[r, kk],
                                         start=False, stop=True, skip_group_check=True)
                return m

            def result(h, pt, o_):
                vs = slice(h * VD, (h + 1) * VD)
                nc.tensor.matmul(o_[:, 0:S], mla_v[:, 0, vs], pt[:, 0:S], start=True, stop=False,
                                 skip_group_check=True)
                return nc.tensor.matmul(o_[:, P:S], mla_v[:, 1, vs], pt[:, 2 * P:3 * P],
                                        start=False, stop=True, skip_group_check=True)

            mla_att.tensor(pe, score, result, m_ylo)
            out_tensor(pe, o, m_ylo)

        def out_tensor(pe, o, ylo, counts=(2, 4, 6, 8)):
            for j, u in enumerate(o):
                wait_split(pe, u)
                pe.wait_ge(ylo, counts[j])
                acc_product(pe, u, yt, 2 * j, j == 0, j == len(o) - 1, half=j == len(o) - 1)

        m_yhi = sem("m_yhi")
        m_ylo = sem("m_ylo")

        def y_hi(act, signal, c, src):
            nc.scalar.activation(ythi[:, c, :], src, ACT.Copy).then_inc(signal, 1)

        def y_lo(dve, hi, n, lo, c, src):
            dve.wait_ge(hi, n)
            nc.vector.tensor_tensor(ytlo[:, c, :], src, ythi[:, c, :].bitcast(F32),
                                    ALU.subtract).then_inc(lo, 1)

        def mla_scalar(act, link, split):
            dq, dkv, (qp, qn0, qn1, kn, v), o = mla_u[0:2], mla_u[2:4], mla_u[4:9], mla_u[9:]

            def latent_highs(chunks):
                for i in chunks:
                    act.wait_ge(m_turned, (1, 1, 2, 3, 3, 4)[i])
                    if i == LC - 1:
                        nc.scalar.activation(mla_kp, latent_bank(i), ACT.Copy).then_inc(m_hi, 1)
                        continue
                    g = col("q_norm", i) if i < QC else col("kv_norm", i - QC)
                    nc.scalar.activation(xthi[:, i, :], latent_bank(i), ACT.Copy,
                                         scale=g).then_inc(m_hi, 1)

            for group, bank, n, k in ((dq, 0, QL, 0), (dkv, 2, KVL, TT)):
                split.after(group[0])
                wait_done(act, group[1])
                for t in range(TT):
                    nc.scalar.activation(res[:, t, 256 * k:256 * k + n], ps[:, bank + t, 0:n], ACT.Square,
                                         accum_out=small[:, k + t:k + t + 1]).then_inc(m_square, 1)
                if k == 0:
                    split.after(dq[1])
                    split.after(dkv[0])
                    act.wait_ge(par_c, 1)
                    latent_highs(range(QC))
            latent_highs(range(QC, LC))
            split.after(dkv[1])
            for u, bank, dst in ((qn0, 2, mla_qn[:, 0:4]), (qn1, 4, mla_qn[:, 4:8]),
                                 (kn, 6, mla_kn[:, 0:4]), (kn, 2, mla_kn[:, 4:8])):
                wait_done(act, u)
                for j in range(2):
                    nc.scalar.activation(dst[:, 2 * j:2 * j + 2].rearrange("p a b -> p (a b)"),
                                         ps[:, bank + j, :], ACT.Copy).then_inc(m_copied, 1)
                split.after(u)
            act.wait_ge(m_qpt, 1)
            for j in range(2):
                nc.scalar.activation(mla_qp[:, 2 * j:2 * j + 2].rearrange("p a b -> p (a b)"),
                                     ps[:, 6 + j, :], ACT.Copy).then_inc(m_copied, 1)
            mla_att.scalar(act, read=lambda h, o_: y_hi(act, m_yhi, h, o_[:, 0:S]))
            split.after(v)

        def rotate(link, src, dst, tables, heads, half, tmp):
            cc, ss = tables
            n = 2 * half

            def every(tb, lo, hi):
                return tb[:, lo:hi].rearrange("p (a b) -> p a b", a=1).broadcast_to([P, heads, hi - lo])

            link.mark(nc.vector.tensor_tensor(tmp[:, :, 0:half], src[:, :, half:n], every(ss, 0, half),
                                              ALU.mult))
            link.mark(nc.vector.tensor_tensor(tmp[:, :, half:n], src[:, :, 0:half],
                                              every(ss, half, n), ALU.mult))
            link(nc.vector.tensor_tensor(dst, src, every(cc, 0, n), ALU.mult))
            return nc.vector.tensor_tensor(dst, dst, tmp, ALU.add)

        def mla_vector(dve, link, split):
            dq, dkv, (qp, qn0, qn1, kn, v), o = mla_u[0:2], mla_u[2:4], mla_u[4:9], mla_u[9:]

            def roots(k, width):
                dve.wait_ge(m_square, TT + k)
                link(nc.vector.tensor_scalar(nt[:, 1, k:k + TT], small[:, k:k + TT], 1.0 / width,
                                             RMS_EPS, ALU.mult, ALU.add))
                rsqrt(link, rs[:, k:k + TT], nt[:, 1, k:k + TT], TT)

            def lows(chunks, highs):
                for i in chunks:
                    g = col("q_norm", i) if i < QC else col("kv_norm", i - QC)
                    dve.wait_ge(m_hi, highs[i - chunks[0]])
                    nc.vector.scalar_tensor_tensor(out=xtlo[:, i, :], in0=latent_bank(i), scalar=g,
                                                   in1=xthi[:, i, :].bitcast(F32), op0=ALU.mult,
                                                   op1=ALU.subtract).then_inc(m_lo, 1)

            split.after(dq[0])
            roots(0, QL)
            for t in range(TT):
                nc.vector.tensor_scalar(latent[:, t, 0:QL], ps[:, t, 0:QL], rs[:, t:t + 1],
                                        None, ALU.mult).then_inc(m_latent, 1)
            split.after(dq[1])
            lows(range(QC), (2, 2, 3))
            lambda_vector(dve, link)
            split.after(dkv[0])
            roots(TT, KVL)
            for t in range(TT):
                link.mark(nc.vector.tensor_scalar(latent[:, t, QL:QL + KVL], ps[:, 2 + t, 0:KVL],
                                                  rs[:, 2 + t:3 + t], None, ALU.mult))
                src = ps[:, 2 + t, KVL:KVL + ROPE].rearrange("p (a b) -> p a b", a=1)
                kp = latent[:, t, QL + KVL:QL + KVL + P]
                tmp = rope_tmp[:, 0:ROPE].rearrange("p (a b) -> p a b", a=1)
                link(rotate(link, src, kp[:, 0:ROPE].rearrange("p (a b) -> p a b", a=1),
                            (rope_m[:, t, 0], rope_m[:, t, 1]), 1, ROPE // 2, tmp))
                nc.vector.tensor_copy(kp[:, ROPE:P], kp[:, 0:ROPE]).then_inc(m_latent, 1)
            split.after(dkv[1])
            lows(range(QC, LC - 1), (QC + 2, QC + 2))
            wait_done(dve, qp)
            dve.wait_ge(m_turned, 4)
            split.after(qp)
            for t in range(TT):
                src = ps[:, t, :].rearrange("p (h e) -> p h e", e=ROPE)
                dst = qpe[:, t, :].rearrange("p (h e) -> p h e", e=ROPE)
                tmp = rope_tmp.rearrange("p (h e) -> p h e", e=ROPE)
                rotate(link, src, dst, (rope_m[:, t, 0], rope_m[:, t, 1]), H1, ROPE // 2,
                       tmp).then_inc(m_qpe, 1)
                dve.wait_ge(m_qpe, t + 1)
            split.after(qn1)
            for t in range(TT):
                if t == 0:
                    dve.wait_ge(m_v0, 1)
                else:
                    wait_done(dve, v)
                for n in range(2):
                    nc.vector.tensor_copy(mla_v[:, t, n * 512:(n + 1) * 512],
                                          ps[:, (4, 0)[t] + n, :]).then_inc(m_vcopied, 1)
            mla_att.vector(dve, link, scale_rows,
                           read=lambda h: y_lo(dve, m_yhi, h + 1, m_ylo, h, ps[:, 6 + h % 2, 0:S]))
            split.after(v)

        mem_tok = arena[:, 4 * S:4 * S + TT * D].rearrange("p (t d) -> p t d", d=D)
        mem_t = sem("mem_t")
        mem_hi = sem("mem_hi")
        mem_lo = sem("mem_lo")
        mem_c = sem("mem_c")

        def mem_bank(c):
            return ps[:, 6 + (c // 2) % 2, (c % 2) * S:(c % 2) * S + S]

        def mem_tensor_t(pe, chunks):
            pe.wait_ge(mem_loaded, 16)
            pe.wait_ge(x_lo, BC * 2)
            for c in chunks:
                if c >= 4 and c % 2 == 0:
                    pe.wait_ge(mem_lo, c // 2 - 1)
                for t in range(TT):
                    m = T(mem_bank(c)[:, t * P:(t + 1) * P], mem_tok[:, t, c * P:(c + 1) * P])
                if c % 2:
                    m.then_inc(mem_t, 1)

        def mem_scalar_t(act, chunks):
            for b in range(chunks[0] // 2, chunks[-1] // 2 + 1):
                act.wait_ge(mem_t, b + 1)
                nc.scalar.activation(pair(ythi, b), ps[:, 6 + b % 2, :], ACT.Copy).then_inc(mem_hi, 1)

        def mem_vector_t(dve, chunks):
            for b in range(chunks[0] // 2, chunks[-1] // 2 + 1):
                dve.wait_ge(mem_hi, b + 1)
                nc.vector.tensor_tensor(pair(ytlo, b), ps[:, 6 + b % 2, :], pair(ythi, b).bitcast(F32),
                                        ALU.subtract).then_inc(mem_lo, 1)

        MEM_BANKS = (6, 7, 0, 3)

        def mem_tensor(pe):
            pe.wait_ge(mem_lo, BC)
            for l in range(2):
                k, v = mem_u[2 * l:2 * l + 2]
                if l:
                    pe.wait_ge(ln_r, 2)
                wait_split(pe, k)
                columns_product(pe, k, 0, [ps[:, MEM_BANKS[2 * l], j * S:(j + 1) * S]
                                           for j in range(2)], yt).then_inc(w_done[k.slot], 1)
                if l:
                    pe.wait_ge(mem_c, 2)
                    ln_tensor(pe, 1)
                wait_split(pe, v)
                for t in range(TT):
                    for c in range(KC):
                        m = product(ps[:, MEM_BANKS[2 * l + 1], t * S:(t + 1) * S],
                                    t_parts(yt, c, t * P, P), w_parts(v, c), c == 0, c == KC - 1)
                m.then_inc(w_done[v.slot], 1)

        def mem_scalar(act, split, l):
            for j in range(2):
                u = mem_u[2 * l + j]
                wait_done(act, u)
                nc.scalar.activation(kvm[:, l, j, :], ps[:, MEM_BANKS[2 * l + j], :],
                                     ACT.Copy).then_inc(mem_c, 1)
                split.after(u)

        def mem_vector(dve, split, l):
            for u in mem_u[2 * l:2 * l + 2]:
                split.after(u)

        A = Arena()
        d_tok = A.take(TT, D)
        d_q = A.take(KC, S)
        d_k = A.take(KC, S)
        d_v = res
        d_toks = (d_tok, res)
        d_att = Attention("diff", KC, 2, True, DH ** -0.5, A)
        d_tmp, d_src = (d_att.p.rearrange("p a b c -> p (a b c)")[:, k * 512:(k + 1) * 512].rearrange(
            "p (t h e) -> p t h e", h=2 * KC, e=ROT) for k in range(2))
        d_o = d_tok
        d_junk = A.take(2, TT, P)
        lam = small[:, 60:61]
        d_copied = sem("d_copied")
        d_rot = sem("d_rot")
        d_t = sem("d_t")
        d_tc = sem("d_tc")
        d_vc = sem("d_vc")
        d_oc = sem("d_oc")
        d_on = sem("d_on")
        d_ot = sem("d_ot")
        d_yhi = sem("d_yhi")
        d_ylo = sem("d_ylo")
        d_sq = sem("d_sq")

        def diff_tensor(pe):
            q, k, v, o = (diff_u[4 * g:4 * g + 4] for g in range(4))

            def project(group, bank0):
                for j, u in enumerate(group):
                    wait_split(pe, u)
                    for t in range(TT):
                        for n in range(2):
                            for c in range(2):
                                if bank0 == 0 and t + n == 0:
                                    pe.wait_ge(x_lo, 2 * BC + j + 1)
                                if bank0 == 0 and j == 0 and c == 0 and t == n:
                                    pe.wait_ge(mem_c, 3 + t)
                                m = product(ps[:, bank0 + 2 * t + n, :],
                                            t_parts(xt, 2 * j + c, t * P, P),
                                            w_parts(u, c, slice(n * 512, n * 512 + 512)),
                                            j + c == 0, 2 * j + c == KC - 1)
                    m.then_inc(w_done[u.slot], 1)

            def turn_over(n):
                for t in range(TT):
                    pe.wait_ge(d_rot, TT * n + t + 1)
                    for c in range(KC):
                        m = T(ps[:, c // 2, (c % 2) * S + t * P:(c % 2) * S + t * P + P],
                              d_toks[n][:, t, c * P:(c + 1) * P])
                        if t == TT - 1 and c % 2:
                            m.then_inc(d_t, 1)

            project(q, 0)
            project(k, 4)
            turn_over(0)
            pe.wait_ge(d_copied, 4)
            project(v, 4)
            pe.wait_ge(d_tc, 4)
            turn_over(1)

            def score(h, m_, bank):
                if h < 2:
                    pe.wait_ge(d_tc, 6 + 2 * h)
                r = slice(DH * m_, DH * m_ + DH)
                for q_, k_, lo in ((0, 0, 0), (1, 1, P), (1, 0, 2 * P)):
                    m = nc.tensor.matmul(bank[:, lo:lo + P], d_q[r, h, q_ * P:q_ * P + P],
                                         d_k[r, h, k_ * P:k_ * P + P], start=True, stop=True,
                                         skip_group_check=True)
                return m

            def result(h, pt, o_):
                vs = slice(h * P, (h + 1) * P)
                nc.tensor.matmul(o_[:, 0:P], pt[:, 0:P], d_v[:, 0, vs], start=True, stop=True,
                                 skip_group_check=True)
                nc.tensor.matmul(o_[:, P:2 * P], pt[:, P:2 * P], d_v[:, 0, vs], start=True,
                                 stop=False, skip_group_check=True)
                return nc.tensor.matmul(o_[:, P:2 * P], pt[:, 2 * P:3 * P], d_v[:, 1, vs],
                                        start=False, stop=True, skip_group_check=True)

            d_att.tensor(pe, score, result, d_oc, before_turn=lambda: pe.wait_ge(d_vc, TT))
            for t in range(TT):
                pe.wait_ge(d_on, t + 1)
                for c in range(KC):
                    m = T(tchunk(c, t * P, P), d_o[:, t, c * P:(c + 1) * P])
                    if t == TT - 1 and c % 2:
                        m.then_inc(d_ot, 1)
            out_tensor(pe, o, d_ylo, (1, 2, 3, 4))

        def diff_scalar(act, link, split):
            q, k, v, o = (diff_u[4 * g:4 * g + 4] for g in range(4))

            def transposes(n):
                for j in range(4):
                    act.wait_ge(d_t, 4 * n + j + 1)
                    nc.scalar.activation(
                        (d_q, d_k)[n][:, 2 * j:2 * j + 2].rearrange("p a b -> p (a b)"),
                        ps[:, j, :], ACT.Copy).then_inc(d_tc, 1)

            for n, group in enumerate((q, k)):
                for u in group[:-1]:
                    split.after(u)
                wait_done(act, group[-1])
                for t in range(TT):
                    nc.scalar.activation(
                        d_toks[n][:, t, :], ps[:, 4 * n + 2 * t:4 * n + 2 * t + 2, :].rearrange(
                            "p a b -> p (a b)"), ACT.Copy).then_inc(d_copied, 1)
                split.after(group[-1])
            transposes(0)
            for u in v[:-1]:
                split.after(u)
            transposes(1)

            def read(h, o_):
                if h >= 2:
                    act.wait_ge(d_sq, TT * (h - 1))
                for t in range(TT):
                    nc.scalar.activation(d_junk[:, h % 2, t], o_[:, t * P:(t + 1) * P], ACT.Square,
                                         accum_out=nt[:, 1, t * KC + h:t * KC + h + 1]) \
                        .then_inc(d_sq, 1)
                nc.scalar.activation(
                    d_o[:, :, h * P:(h + 1) * P], o_[:, 0:2 * P].rearrange("p (t e) -> p t e", e=P),
                    ACT.Copy).then_inc(d_oc, 1)

            d_att.scalar(act, read=read)
            split.after(v[-1])
            for b in range(BC):
                act.wait_ge(d_ot, b + 1)
                nc.scalar.activation(pair(ythi, b), ps[:, 4 + b, :], ACT.Copy,
                                     scale=small[:, 61:62]).then_inc(d_yhi, 1)

        def diff_vector(dve, link, split):
            q, k, v, o = (diff_u[4 * g:4 * g + 4] for g in range(4))
            for n, group in enumerate((q, k)):
                for u in group:
                    split.after(u)
                for t in range(TT):
                    dve.wait_ge(d_copied, TT * n + t + 1)
                    tok = d_toks[n][:, t, :].rearrange("p (h e) -> p h e", e=DH)[:, :, 0:ROT]
                    src = d_src[:, t]
                    link(nc.vector.tensor_copy(src, tok))
                    rotate(link, src, tok, (rope_d[:, t, 0], rope_d[:, t, 1]), 2 * KC, ROT // 2,
                           d_tmp[:, t]).then_inc(d_rot, 1)
            for u in v[:-1]:
                split.after(u)
            wait_done(dve, v[-1])
            dve.wait_ge(d_t, 8)
            for t in range(TT):
                nc.vector.tensor_copy(d_v[:, t, :], ps[:, 4 + 2 * t:6 + 2 * t, :].rearrange(
                    "p a b -> p (a b)")).then_inc(d_vc, 1)

            def difference(link_, h, p, r, rows_, done):
                link_(nc.vector.tensor_scalar(small[:, 36:38], r[:, 2:4], lam, None, ALU.mult))
                for t, (lo, hi) in enumerate(rows_):
                    link_.mark(nc.vector.tensor_scalar(p[:, 1, lo:hi], p[:, 1, lo:hi],
                                                       small[:, 36 + t:37 + t], None, ALU.mult))
                dve.wait_ge(link_.s, link_.n)
                for t, (lo, hi) in enumerate(rows_):
                    m = nc.vector.scalar_tensor_tensor(out=p[:, 0, lo:hi], in0=p[:, 0, lo:hi],
                                                       scalar=r[:, t:t + 1], in1=p[:, 1, lo:hi],
                                                       op0=ALU.mult, op1=ALU.add)
                    if t == 0:
                        link_.mark(m)
                m.then_inc(done, 1)

            d_att.vector(dve, link, difference)
            dve.wait_ge(d_oc, KC)
            heads = "p (h e) -> p h e"
            dve.wait_ge(d_sq, TT * KC)
            link(nc.vector.tensor_scalar(nt[:, 1, :], nt[:, 1, :], 1.0 / P, RMS_EPS, ALU.mult, ALU.add))
            rsqrt(link, rs[:, 0:2 * KC], nt[:, 1, 0:2 * KC], 2 * KC)
            for t in range(TT):
                v_ = d_o[:, t, :].rearrange(heads, e=P)
                r = rs[:, t * KC:(t + 1) * KC].rearrange("p (h e) -> p h e", e=1).broadcast_to([P, KC, P])
                nc.vector.tensor_tensor(v_, v_, r, ALU.mult).then_inc(d_on, 1)
            split.after(v[-1])
            for b in range(BC):
                dve.wait_ge(d_yhi, b + 1)
                nc.vector.scalar_tensor_tensor(out=pair(ytlo, b), in0=ps[:, 4 + b, :],
                                               scalar=small[:, 61:62],
                                               in1=pair(ythi, b).bitcast(F32), op0=ALU.mult,
                                               op1=ALU.subtract).then_inc(d_ylo, 1)

        def cross(name, layer, xq, mem, ylo, count0):
            att = Attention(name, XH, 1, False, XD ** -0.5, mem)
            yhi = sem(f"{name}_yhi")
            keys = kvm[:, layer, 0, :].rearrange("p (c s) -> p c s", s=S)
            vals = kvm[:, layer, 1, :].rearrange("p (t e) -> p t e", e=DXA)

            def rows_of(h):
                return slice(XD * (h % 2), XD * (h % 2) + XD)

            def score(h, m_, bank):
                for t in range(TT):
                    m = nc.tensor.matmul(bank[:, t * S:(t + 1) * S],
                                         xq[rows_of(h), h // 2, t * P:(t + 1) * P],
                                         keys[rows_of(h), h // 2, :], start=True, stop=True,
                                         skip_group_check=True)
                return m

            def result(h, pt, o_):
                for t in range(TT):
                    m = nc.tensor.matmul(o_[rows_of(h), 0:S], vals[:, t, h * XD:(h + 1) * XD],
                                         pt[:, t * S:(t + 1) * S], start=t == 0, stop=t == TT - 1,
                                         skip_group_check=True)
                return m

            def read_hi(h, o_):
                nc.scalar.activation(ythi[rows_of(h), TC + h // 2, :], o_[rows_of(h), 0:S],
                                     ACT.Copy).then_inc(yhi, 1)

            def scalar(act):
                att.scalar(act, read_hi)

            def vector(dve, link):
                def read_lo(h):
                    dve.wait_ge(yhi, h + 1)
                    nc.vector.tensor_tensor(ytlo[rows_of(h), TC + h // 2, :],
                                            ps[rows_of(h), 6 + h % 2, 0:S],
                                            ythi[rows_of(h), TC + h // 2, :].bitcast(F32),
                                            ALU.subtract).then_inc(ylo, 1)
                att.vector(dve, link, scale_rows, read_lo)

            def tensor(pe, before_turn=None):
                att.tensor(pe, score, result, ylo, count0, before_turn)

            return tensor, scalar, vector

        A = Arena()
        PAD = CW - 1
        c_c = A.take(2, 2, S)
        c_x = A.take(2, 2, PAD + S)
        c_s = A.take(2, 2, S)
        c_y = A.take(2, 2, S)
        c_q = A.take(2, S)
        c_zero = sem("c_zero")
        c_copied = sem("c_copied")
        c_tok = sem("c_tok")
        c_yhi = sem("c_yhi")
        c_ylo = sem("c_ylo")
        c_qc = sem("c_qc")
        TRI = TC // 2
        cross0_tensor, cross0_scalar, cross0_vector = cross("cross0", 0, c_q, A, c_ylo, TC)

        def conv_tensor(pe):
            o = conv_u[3 * TRI + 1:]
            for n in range(3 * TRI + 1):
                u = conv_u[n]
                i = n // 3
                bank = 6 if n == 3 * TRI else (i % 2) * 3 + n % 3
                if 2 <= i < TRI:
                    pe.wait_ge(c_tok, i - 1)
                wait_split(pe, u)
                columns_product(pe, u, 0, [ps[:, bank, j * S:(j + 1) * S] for j in range(2)],
                                x_from=5 * BC if n == 0 else None).then_inc(w_done[u.slot], 1)
            pe.wait_ge(c_qc, 1)
            pe.wait_ge(c_tok, TRI)
            cross0_tensor(pe)
            out_tensor(pe, o, c_ylo, (2, 4, 6, TC + XH))

        def conv_scalar(act, link, split):
            def high(i):
                act.wait_ge(c_tok, i + 1)
                for j in range(2):
                    nc.scalar.activation(ythi[:, 2 * i + j, :], c_y[:, i % 2, j, :],
                                         ACT.Copy).then_inc(c_yhi, 1)

            for i in range(TRI):
                c, x_, b = conv_u[3 * i:3 * i + 3]
                wait_done(act, c)
                if i >= 2:
                    act.wait_ge(c_tok, i - 1)
                nc.scalar.activation(c_c[:, i % 2].rearrange("p a b -> p (a b)"),
                                     ps[:, (i % 2) * 3, :], ACT.Copy).then_inc(c_copied, 1)
                split.after(c)
                if i:
                    high(i - 1)
                split.after(x_)
                split.after(b)
            q = conv_u[3 * TRI]
            wait_done(act, q)
            nc.scalar.activation(c_q.rearrange("p a b -> p (a b)"), ps[:, 6, :],
                                 ACT.Copy).then_inc(c_qc, 1)
            high(TRI - 1)
            cross0_scalar(act)
            split.after(q)

        def conv_vector(dve, link, split):
            link(nc.vector.memset(c_x[:, :, :, 0:PAD], 0.0))

            def low(i):
                for j in range(2):
                    dve.wait_ge(c_yhi, 2 * i + j + 1)
                    nc.vector.tensor_tensor(ytlo[:, 2 * i + j, :], c_y[:, i % 2, j, :],
                                            ythi[:, 2 * i + j, :].bitcast(F32),
                                            ALU.subtract).then_inc(c_ylo, 1)

            for i in range(TRI):
                c, x_, b = conv_u[3 * i:3 * i + 3]
                k = i % 2
                split.after(c)
                dve.wait_ge(c_copied, i + 1)
                wait_done(dve, x_)
                link(nc.vector.tensor_tensor(
                    c_x[:, k, :, PAD:], c_c[:, k], ps[:, 3 * k + 1, :].rearrange(
                        "p (a b) -> p a b", b=S), ALU.mult))
                split.after(x_)
                for w in range(CW):
                    for j in range(2):
                        tap = c_x[:, k, j, w:w + S]
                        weight = col("conv_w", w * TC + 2 * i + j)
                        if w == 0:
                            m = nc.vector.tensor_scalar(c_s[:, k, j], tap, weight, None, ALU.mult)
                        else:
                            m = nc.vector.scalar_tensor_tensor(out=c_s[:, k, j], in0=tap, scalar=weight,
                                                               in1=c_s[:, k, j], op0=ALU.mult,
                                                               op1=ALU.add)
                        link.mark(m)
                    dve.wait_ge(link.s, link.n)
                wait_done(dve, b)
                if i >= 2:
                    dve.wait_ge(c_yhi, 2 * (i - 1))
                nc.vector.tensor_tensor(c_y[:, k].rearrange("p a b -> p (a b)"),
                                        c_s[:, k].rearrange("p a b -> p (a b)"),
                                        ps[:, 3 * k + 2, :], ALU.mult).then_inc(c_tok, 1)
                split.after(b)
                if i:
                    low(i - 1)
            low(TRI - 1)
            cross0_vector(dve, link)
            split.after(conv_u[3 * TRI])

        A = Arena()
        QPAD = QW - 1
        l_x = A.take(2, 2, QPAD + S)
        l_s = A.take(2, 2, S)
        shared = A.at
        l_qk = A.take(2 * TC, S)
        l_v = A.take(TT, MH, MD + 1)
        l_o = A.take(TT, DTOK)
        l_gain = A.take(DTOK)
        B_ = Arena()
        cross1_mem = B_
        l_q = res[:, 1, D // 2:].rearrange("p (c s) -> p c s", s=S)
        l_h = res[:, :, :].rearrange("p t d -> p (t d)")[:, 0:TT * DTOK].rearrange(
            "p (t d) -> p t d", d=DTOK)
        C_ = Arena()
        l_e = C_.take(3 * P)
        l_w = C_.take(2, 3 * P)
        l_sc = C_.take(2, 3 * P)
        assert C_.at <= shared
        rowt = kvm[0:MH, 0, :, :].rearrange("p a (b s) -> p (a b) s", s=S)
        g_tok = small[:, 64:80]
        g_tmp = small[:, 80:88]
        l_shift = g_tmp[:, 0:MH]
        gcol = sb("gcol", [P, 2, TT, MH])
        g_bias = sb("g_bias", [P, 2 * MH])
        names = ("l_copied", "l_conv", "l_qkd", "l_g", "l_gexp", "l_gln", "l_gts", "l_gt", "l_row",
                 "l_col", "l_gc", "l_xq", "l_vc", "l_oc", "l_og", "l_mb", "l_sT", "l_ed", "l_wd",
                 "l_scd", "l_num", "l_hd", "l_root", "l_hn", "l_tok", "l_tt", "l_yhi", "l_ylo")
        L = {n: sem(n) for n in names}
        cross1_tensor, cross1_scalar, cross1_vector = cross("cross1", 1, l_q, B_, L["l_ylo"], 0)
        assert B_.at <= shared
        QK, GX, XQ = ml_u[0:TC], ml_u[TC], ml_u[TC + 1]
        VU, OU, WO = ml_u[TC + 2:TC + 6], ml_u[TC + 6:TC + 10], ml_u[TC + 10:]

        def head_rows(h):
            got, f = [], h * MD
            while f < (h + 1) * MD:
                n = min(P - f % P, (h + 1) * MD - f)
                got.append((f // P, slice(f % P, f % P + n)))
                f += n
            return got

        def ml_tensor(pe):
            for j, u in enumerate(QK):
                wait_split(pe, u)
                if j >= 2:
                    pe.wait_ge(L["l_copied"], j - 1)
                columns_product(pe, u, 0, [ps[:, j % 2, n * S:(n + 1) * S] for n in range(2)],
                                x_from=8 * BC if j == 0 else None).then_inc(w_done[u.slot], 1)
            wait_split(pe, GX)
            for t in range(TT):
                for c in range(KC):
                    m = product(ps[:, 2, t * 2 * MH:(t + 1) * 2 * MH], t_parts(xt, c, t * P, P),
                                w_parts(GX, c), c == 0, c == KC - 1)
            m.then_inc(w_done[GX.slot], 1)
            wait_split(pe, XQ)
            columns_product(pe, XQ, 0, [ps[:, 3, n * S:(n + 1) * S] for n in range(2)]) \
                .then_inc(w_done[XQ.slot], 1)

            def tokens(group, banks):
                for j, u in enumerate(group):
                    wait_split(pe, u)
                    for t in range(TT):
                        for lo, hi in ((0, 512), (512, DTOK)):
                            for c in range(2):
                                m = product(ps[:, banks[t] + lo // 512, 0:hi - lo],
                                            t_parts(xt, 2 * j + c, t * P, P),
                                            w_parts(u, c, slice(lo, hi)), j + c == 0,
                                            2 * j + c == KC - 1)
                    m.then_inc(w_done[u.slot], 1)

            tokens(VU, (4, 6))
            pe.wait_ge(L["l_g"], 2)
            for k in range(2):
                for t in range(TT):
                    m = T(ps[0:MH, 2, k * S + t * P:k * S + t * P + P],
                          g_tok[:, t * 2 * MH + k * MH:t * 2 * MH + (k + 1) * MH])
            m.then_inc(L["l_gt"], 1)
            pe.wait_ge(L["l_copied"], TC)
            pe.wait_ge(L["l_vc"], TT)
            tokens(OU, (0, 4))
            pe.wait_ge(L["l_row"], 3)
            pe.wait_ge(L["l_xq"], 1)
            for k in range(2):
                for t in range(TT):
                    m = T(ps[:, 3, (k * TT + t) * MH:(k * TT + t + 1) * MH],
                          rowt[:, 2 * k, t * P:(t + 1) * P])
            m.then_inc(L["l_col"], 1)
            pe.wait_ge(L["l_oc"], 1)
            cross1_tensor(pe, before_turn=lambda: pe.wait_ge(L["l_oc"], TT))
            pe.wait_ge(L["l_gc"], 2)
            pe.wait_ge(L["l_ylo"], XH)
            pe.wait_ge(L["l_qkd"], TC)
            for i in range(MH + 1):
                if i < MH:
                    if i >= 2:
                        pe.wait_ge(L["l_ed"], i - 1)
                        pe.wait_ge(L["l_scd"], i - 1)
                    nc.tensor.matmul(ps[:, 6 + i % 2, 0:S], sel[:, i, :], rowt[:, 3, :], start=True,
                                     stop=True, skip_group_check=True).then_inc(L["l_mb"], 1)
                    pieces = head_rows(i)
                    for to, k0, q0 in ((slice(0, S), 0, 0), (slice(S, 3 * P), P, P)):
                        for n, (c, r) in enumerate(pieces):
                            m = nc.tensor.matmul(ps[:, 2 + i % 2, to], l_qk[r, TC + c, k0:k0 + P],
                                                 l_qk[r, c, q0:S], start=n == 0,
                                                 stop=n == len(pieces) - 1, skip_group_check=True)
                    m.then_inc(L["l_sT"], 1)
                h = i - 1
                if h >= 0:
                    pe.wait_ge(L["l_scd"], h + 1)
                    if h >= 2:
                        pe.wait_ge(L["l_hd"], h - 1)
                    b = ps[:, h % 2, :]
                    sc = l_sc[:, h % 2]
                    n1 = MD + 1
                    nc.tensor.matmul(b[:, 0:n1], sc[:, 0:P], l_v[:, 0, h, :], start=True, stop=True,
                                     skip_group_check=True)
                    nc.tensor.matmul(b[:, n1:2 * n1], sc[:, P:S], l_v[:, 0, h, :], start=True,
                                     stop=False, skip_group_check=True)
                    nc.tensor.matmul(b[:, n1:2 * n1], sc[:, S:3 * P], l_v[:, 1, h, :], start=False,
                                     stop=True, skip_group_check=True).then_inc(L["l_num"], 1)
            for t in range(TT):
                pe.wait_ge(L["l_tok"], t + 1)
                for c in range(TC):
                    m = T(tchunk(c, t * P, P), l_h[:, t, c * P:(c + 1) * P])
                    if t == TT - 1 and c % 2:
                        m.then_inc(L["l_tt"], 1)
            out_tensor(pe, WO, L["l_ylo"], (XH + 1, XH + 2, XH + 3, XH + 3))

        def ml_scalar(act, link, split):
            for j in range(TC + 1):
                if j < TC:
                    u = QK[j]
                    wait_done(act, u)
                    if j == 0:
                        act.wait_ge(L["l_conv"], 1)
                    if j >= 2:
                        act.wait_ge(L["l_conv"], j)
                    nc.scalar.activation(l_x[:, j % 2, :, QPAD:],
                                         ps[:, j % 2, :].rearrange("p (a b) -> p a b", b=S),
                                         ACT.Copy).then_inc(L["l_copied"], 1)
                    split.after(u)
                if j >= 1:
                    act.wait_ge(L["l_conv"], j + 1)
                    nc.scalar.activation(
                        l_qk[:, 2 * (j - 1):2 * j].rearrange("p a b -> p (a b)"),
                        l_s[:, (j - 1) % 2].rearrange("p a b -> p (a b)"),
                        ACT.Silu).then_inc(L["l_qkd"], 1)
            split.after(GX)
            wait_done(act, XQ)
            nc.scalar.activation(l_q.rearrange("p a b -> p (a b)"), ps[:, 3, :],
                                 ACT.Copy).then_inc(L["l_xq"], 1)
            split.after(XQ)
            act.wait_ge(L["l_g"], 1)
            nc.scalar.activation(g_tmp, g_tmp, ACT.Exp, scale=-1.0).then_inc(L["l_gexp"], 1)
            act.wait_ge(L["l_gexp"], 1)
            nc.scalar.activation(g_tmp, g_tmp, ACT.Ln, bias=1.0).then_inc(L["l_gln"], 1)
            for u in VU[:-1]:
                split.after(u)
            wait_done(act, VU[-1])
            for t in range(TT):
                nc.scalar.activation(
                    l_v[:, t, :, 0:MD],
                    ps[:, 4 + 2 * t:6 + 2 * t, :].rearrange("p a b -> p (a b)")[:, 0:DTOK].rearrange(
                        "p (h e) -> p h e", e=MD), ACT.Copy).then_inc(L["l_vc"], 1)
            split.after(VU[-1])
            for u in OU[:-1]:
                split.after(u)
            wait_done(act, OU[-1])
            for t in range(TT):
                nc.scalar.activation(
                    l_o[:, t, :], ps[:, 4 * t:4 * t + 2, :].rearrange(
                        "p a b -> p (a b)")[:, 0:DTOK], ACT.Sigmoid).then_inc(L["l_oc"], 1)
            cross1_scalar(act)
            act.wait_ge(L["l_gc"], 1)
            nc.scalar.activation(gcol[:, 1].rearrange("p a b -> p (a b)"),
                                 ps[:, 3, TT * MH:2 * TT * MH], ACT.Exp,
                                 scale=-1.0).then_inc(L["l_gc"], 1)
            act.wait_ge(L["l_gc"], 2)
            for h in range(MH):
                if h == 1:
                    split.after(OU[-1])
                act.wait_ge(L["l_ed"], h + 1)
                if h >= 2:
                    act.wait_ge(L["l_scd"], h - 1)
                for s, (lo, hi) in enumerate(((0, S), (S, 3 * P))):
                    nc.scalar.activation(l_w[:, h % 2, lo:hi], l_e[:, lo:hi], ACT.Exp, scale=-1.0,
                                         bias=gcol[:, 0, s, h:h + 1]).then_inc(L["l_wd"], 1)
            act.wait_ge(L["l_root"], 1)
            for h in range(MH):
                v_ = l_h[:, 1, h * MD:(h + 1) * MD]
                nc.scalar.activation(v_, v_, ACT.Identity, bias=l_shift[:, h:h + 1],
                                     scale=rs[:, MH + h:MH + h + 1]).then_inc(L["l_hn"], 1)
            for b in range(TC // 2):
                act.wait_ge(L["l_tt"], b + 1)
                nc.scalar.activation(pair(ythi, b), ps[:, 4 + b, :], ACT.Copy) \
                    .then_inc(L["l_yhi"], 1)

        def ml_vector(dve, link, split):
            nc.vector.memset(l_x[:, :, :, 0:QPAD], 0.0).then_inc(L["l_conv"], 1)
            link(nc.vector.memset(l_v[:, :, :, MD:], 1.0))
            for j, u in enumerate(QK):
                k = j % 2
                split.after(u)
                dve.wait_ge(L["l_copied"], j + 1)
                if j >= 2:
                    dve.wait_ge(L["l_qkd"], j - 1)
                for w in range(QW):
                    for n in range(2):
                        tap = l_x[:, k, n, w:w + S]
                        weight = col("qk_conv_w", w * 2 * TC + 2 * j + n)
                        if w == 0:
                            m = nc.vector.tensor_scalar(l_s[:, k, n], tap, weight, None, ALU.mult)
                        else:
                            m = nc.vector.scalar_tensor_tensor(out=l_s[:, k, n], in0=tap, scalar=weight,
                                                               in1=l_s[:, k, n], op0=ALU.mult,
                                                               op1=ALU.add)
                        if w == QW - 1 and n == 1:
                            m.then_inc(L["l_conv"], 1)
                        else:
                            link.mark(m)
                    if w < QW - 1:
                        dve.wait_ge(link.s, link.n)
            split.after(GX)
            wait_done(dve, GX)
            dve.wait_ge(gain_loaded, 32)
            g3 = g_tok.rearrange("p (t g) -> p t g", g=2 * MH)
            link(nc.vector.tensor_tensor(
                g3, ps[:, 2, 0:2 * TT * MH].rearrange("p (t g) -> p t g", g=2 * MH),
                g_bias[:, :].rearrange("p (a g) -> p a g", a=1).broadcast_to([P, TT, 2 * MH]), ALU.add))
            f3 = g3[:, :, MH:]
            tmp3 = g_tmp.rearrange("p (t g) -> p t g", g=MH)
            nc.vector.scalar_tensor_tensor(out=tmp3, in0=f3, scalar=-1.0, in1=f3, op0=ALU.mult,
                                           op1=ALU.max).then_inc(L["l_g"], 1)
            dve.wait_ge(L["l_gln"], 1)
            nc.vector.scalar_tensor_tensor(out=f3, in0=f3, scalar=0.0, in1=tmp3, op0=ALU.min,
                                           op1=ALU.subtract).then_inc(L["l_g"], 1)
            split.after(XQ)
            for u in VU:
                split.after(u)
            dve.wait_ge(L["l_gt"], 1)
            link(nc.vector.tensor_copy(rowt[:, 0:2, :].rearrange("p a s -> p (a s)"), ps[0:MH, 2, :]))
            a_, b_, m_ = rowt[:, 0, :], rowt[:, 1, :], rowt[:, 3, :]
            link(nc.vector.tensor_tensor_scan(rowt[:, 2, :], ones[0:MH, :], b_, 0.0,
                                              op0=ALU.mult, op1=ALU.add))
            nc.vector.tensor_tensor(a_, a_, rowt[:, 2, :], ALU.subtract).then_inc(L["l_row"], 1)
            dve.wait_ge(L["l_row"], 1)
            nc.vector.tensor_tensor_scan(m_, a_, a_, 0.0, op0=ALU.max,
                                         op1=ALU.max).then_inc(L["l_row"], 1)
            dve.wait_ge(L["l_row"], 2)
            nc.vector.tensor_tensor(rowt[:, 2, :], rowt[:, 2, :], m_, ALU.add).then_inc(L["l_row"], 1)
            for u in OU[:-1]:
                split.after(u)
            dve.wait_ge(L["l_col"], 1)
            nc.vector.tensor_copy(gcol[:, 0].rearrange("p a b -> p (a b)"),
                                  ps[:, 3, 0:TT * MH]).then_inc(L["l_gc"], 1)
            cross1_vector(dve, link)
            dve.wait_ge(L["l_gc"], 2)

            def head_stats(h):
                dve.wait_ge(L["l_hd"], h + 1)
                dve.wait_ge(link.s, link.n)
                for t in range(TT):
                    link.mark(nc.vector.bn_stats(stats[:, t * MH + h, :],
                                                 l_h[:, t, h * MD:(h + 1) * MD]))

            for i in range(MH + 1):
                if i == 1:
                    split.after(OU[-1])
                if i < MH:
                    dve.wait_ge(L["l_mb"], i + 1)
                    if i:
                        dve.wait_ge(L["l_wd"], 2 * i)
                    mb = ps[:, 6 + i % 2, :]
                    link(nc.vector.tensor_tensor(l_e[:, 0:S], mb[:, 0:S], mtril[:, :], ALU.add))
                    nc.vector.tensor_tensor(l_e[:, S:3 * P], mb[:, P:S], mtril[:, 0:P],
                                            ALU.add).then_inc(L["l_ed"], 1)
                    dve.wait_ge(L["l_sT"], i + 1)
                    dve.wait_ge(L["l_wd"], 2 * i + 2)
                    if i >= 2:
                        dve.wait_ge(L["l_num"], i - 1)
                    nc.vector.scalar_tensor_tensor(out=l_sc[:, i % 2], in0=ps[:, 2 + i % 2, 0:3 * P],
                                                   scalar=MD ** -0.5, in1=l_w[:, i % 2], op0=ALU.mult,
                                                   op1=ALU.mult).then_inc(L["l_scd"], 1)
                h = i - 1
                if h >= 1:
                    head_stats(h - 1)
                if h >= 0:
                    dve.wait_ge(L["l_num"], h + 1)
                    b = ps[:, h % 2, 0:2 * (MD + 1)].rearrange("p (t e) -> p t e", e=MD + 1)
                    dv = small[:, TT * h:TT * (h + 1)]
                    d = dv.rearrange("p (t e) -> p t e", e=1)
                    link(nc.vector.tensor_copy(d, b[:, :, MD:]))
                    link(nc.vector.scalar_tensor_tensor(out=d, in0=d, scalar=-1.0, in1=d,
                                                        op0=ALU.mult, op1=ALU.max))
                    link(nc.vector.tensor_tensor(d, d, gcol[:, 1, :, h:h + 1], ALU.max))
                    link(nc.vector.reciprocal(dv, dv))
                    for t in range(TT):
                        m = nc.vector.tensor_scalar(l_h[:, t, h * MD:(h + 1) * MD], b[:, t, 0:MD],
                                                    dv[:, t:t + 1], None, ALU.mult)
                        if t == 0:
                            link.mark(m)
                    m.then_inc(L["l_hd"], 1)
            head_stats(MH - 1)
            dve.wait_ge(link.s, link.n)
            for k in range(TT * MH):
                link.mark(nc.vector.bn_aggr(mv[:, k, :], stats[:, k, :]))
            dve.wait_ge(link.s, link.n)
            link(nc.vector.tensor_scalar_add(nt[:, 1, 0:TT * MH], mv[:, :, 1], LN_EPS))
            rsqrt(link, rs[:, 0:TT * MH], nt[:, 1, 0:TT * MH], TT * MH)
            nc.vector.scalar_tensor_tensor(out=l_shift, in0=mv[:, MH:TT * MH, 0], scalar=-1.0,
                                           in1=rs[:, MH:TT * MH], op0=ALU.mult,
                                           op1=ALU.mult).then_inc(L["l_root"], 1)
            for h in range(MH):
                v_ = l_h[:, 0, h * MD:(h + 1) * MD]
                link.mark(nc.vector.tensor_scalar(v_, v_, mv[:, h, 0:1], rs[:, h:h + 1],
                                                  ALU.subtract, ALU.mult))
            for t in range(TT):
                if t == 0:
                    dve.wait_ge(link.s, link.n)
                else:
                    dve.wait_ge(L["l_hn"], MH)
                dve.wait_ge(L["l_og"], t + 1)
                nc.vector.tensor_tensor(l_h[:, t, :], l_h[:, t, :], l_o[:, t, :],
                                        ALU.mult).then_inc(L["l_tok"], 1)
            for b in range(TC // 2):
                dve.wait_ge(L["l_yhi"], b + 1)
                nc.vector.tensor_tensor(pair(ytlo, b), ps[:, 4 + b, :], pair(ythi, b).bitcast(F32),
                                        ALU.subtract).then_inc(L["l_ylo"], 1)

        def ml_gpsimd(pool):
            pool.wait_ge(gain_loaded, 32)
            for t in range(TT):
                pool.wait_ge(L["l_oc"], t + 1)
                nc.gpsimd.tensor_tensor(l_o[:, t, :], l_o[:, t, :], l_gain, ALU.mult) \
                    .then_inc(L["l_og"], 1)

        mtril = sb("mtril", [P, S])
        lam_rows = sb("lam_rows", [1, 4, DH])
        lam_t = sb("lam_t", [1, 2, DH])
        lam_e = sb("lam_e", [1, 2])
        ang = sb("ang", [P, TT, 3, ROPE // 2 + ROT // 2])
        lam_s = sem("lam_s")
        lam_x = sem("lam_x")
        lam_b = sem("lam_b")
        NF = ROPE // 2 + ROT // 2
        N_ROW_DMAS = len(row_dmas) + TT

        def freqs(theta, d):
            return [np.float32(theta) ** np.float32(-np.float32(i) / np.float32(d))
                    for i in range(0, d, 2)]

        def start_gpsimd(pool):
            load_gb(pool, 0)
            nc.gpsimd.memset(ident[:, :], 0.0)
            nc.gpsimd.memset(masks[:, :, :], 0.0)
            nc.gpsimd.memset(mtril[:, :], 0.0)
            nc.gpsimd.memset(sel[:, :, :], 0.0)
            nc.gpsimd.memset(ones[:, :], 1.0)
            for k, f in enumerate(freqs(10000.0, ROPE) + freqs(500000.0, ROT)):
                m = nc.gpsimd.memset(rope_f[:, k:k + 1], float(f))
            m.then_inc(consts, 1)
            pool.wait_ge(consts, 1)
            nc.gpsimd.affine_select(out=ident[:, :], in_=ident[:, :], compare_op=ALU.not_equal,
                                    fill=1.0, base=0, pattern=[[-1, P]], channel_multiplier=1)
            nc.gpsimd.affine_select(out=masks[:, 0, :], in_=masks[:, 0, :], compare_op=ALU.is_ge,
                                    fill=NEG, base=0, pattern=[[-1, P]], channel_multiplier=1)
            nc.gpsimd.affine_select(out=mtril[:, 0:P], in_=mtril[:, 0:P], compare_op=ALU.is_ge,
                                    fill=-NEG, base=0, pattern=[[1, P]], channel_multiplier=-1)
            nc.gpsimd.affine_select(out=sel[:, :, :], in_=sel[:, :, :], compare_op=ALU.not_equal,
                                    fill=1.0, base=0, pattern=[[1, MH], [0, P]],
                                    channel_multiplier=-1).then_inc(consts, 1)

        def start_loads(sp):
            for k, r, src, n in row_dmas:
                sp.dma_start(par_rows[r:r + n, k, :], src).then_inc(row_loaded, 16)
            for t in range(TT):
                sp.dma_start(pos_i[:, t:t + 1], a["positions"][0, t * P:(t + 1) * P].rearrange(
                    "(p a) -> p a", a=1)).then_inc(row_loaded, 16)
            for k, w in enumerate(("q1", "k1", "q2", "k2")):
                sp.dma_start(lam_rows[:, k, :], a[f"diff_lambda_{w}"]).then_inc(lam_loaded, 16)

        def start_tensor(pe):
            pe.wait_ge(consts, 2)
            for t in range(TT):
                pe.wait_ge(x_loaded[t], 16)
                for c in range(KC):
                    m = T(tchunk(c, t * P, P), x[:, t, c * P:(c + 1) * P])
                    if t == TT - 1 and c % 2:
                        m.then_inc(ln_t, 1)

        def params_tensor(pe):
            pe.wait_ge(row_loaded, 16 * N_ROW_DMAS)
            pe.wait_ge(x_lo, BC)
            for k in range(PAR_TILES):
                n = min(P, NPAR - k * P)
                m = T(ps[:, 4 + k, 0:n], par_rows[0:n, k, :])
            m.then_inc(par_t, 1)

        def lambda_tensor(pe):
            pe.wait_ge(lam_x, 1)
            nc.tensor.matmul(ps[:, 7, 0:2], ones[0:1, 0:P], lam_e[:, :], start=True,
                             stop=True).then_inc(lam_b, 1)

        def start_scalar(act, split):
            for b in range(BC):
                act.wait_ge(ln_t, b + 1)
                nc.scalar.activation(pair(xthi, b), ps[:, 4 + b, :], ACT.Copy).then_inc(x_hi, 1)
                if b == 1:
                    split.after(None, 1)
            split.after(None)
            act.wait_ge(lam_s, 1)
            nc.scalar.activation(lam_e[:, :], lam_e[:, :], ACT.Exp).then_inc(lam_x, 1)
            act.wait_ge(rope_ang, 1)
            nc.scalar.activation(ang[:, :, 1, :], ang[:, :, 0, :], ACT.Sin).then_inc(rope_sin, 1)
            nc.scalar.activation(ang[:, :, 2, :], ang[:, :, 0, :], ACT.Sin,
                                 scale=0.5).then_inc(rope_sin, 1)

        def start_vector(dve, link, split):
            for b in range(BC):
                dve.wait_ge(x_hi, b + 1)
                nc.vector.tensor_tensor(pair(xtlo, b), ps[:, 4 + b, :], pair(xthi, b).bitcast(F32),
                                        ALU.subtract).then_inc(x_lo, 1)
                if b == 1:
                    split.after(None, 1)
            split.after(None)
            dve.wait_ge(lam_loaded, 64)
            l4 = lam_rows[:, :, :].rearrange("p (a b) e -> p a b e", b=2)
            link(nc.vector.tensor_tensor(lam_t[:, :, :], l4[:, :, 0, :], l4[:, :, 1, :], ALU.mult))
            nc.vector.tensor_reduce(out=lam_e[:, :], in_=lam_t[:, :, :], axis=AX.X,
                                    op=ALU.add).then_inc(lam_s, 1)
            dve.wait_ge(consts, 1)
            dve.wait_ge(row_loaded, 16 * N_ROW_DMAS)
            link(nc.vector.tensor_copy(pos_f[:, :], pos_i[:, :]))
            for t in range(TT):
                link.mark(nc.vector.tensor_scalar(ang[:, t, 0, :], rope_f[:, :], pos_f[:, t:t + 1],
                                                  None, ALU.mult))
            dve.wait_ge(link.s, link.n)
            th, turns = ang[:, :, 0, :], ang[:, :, 1, :]
            link(nc.vector.tensor_scalar(turns, th, 1.0 / (2 * math.pi), MAGIC_ROUND, ALU.mult, ALU.add))
            link(nc.vector.tensor_scalar_add(turns, turns, -MAGIC_ROUND))
            c1 = 6.28125
            c2 = float(np.float32(np.round((2 * math.pi - c1) * 2 ** 21) / 2 ** 21))
            c3 = float(np.float32(2 * math.pi - c1 - c2))
            for c in (c1, c2, c3):
                link(nc.vector.scalar_tensor_tensor(out=th, in0=turns, scalar=-c, in1=th,
                                                    op0=ALU.mult, op1=ALU.add))
            nc.vector.tensor_scalar(th, th, 3.1415925, -3.1415925, ALU.min,
                                    ALU.max).then_inc(rope_ang, 1)
            dve.wait_ge(rope_sin, 2)
            half = ang[:, :, 2, :]
            link(nc.vector.tensor_tensor(half, half, half, ALU.mult))
            link(nc.vector.tensor_scalar(half, half, -2.0, 1.0, ALU.mult, ALU.add))
            for tb, lo, n in ((rope_m, 0, ROPE // 2), (rope_d, ROPE // 2, ROT // 2)):
                cos, sin = ang[:, :, 2, lo:lo + n], ang[:, :, 1, lo:lo + n]
                link.mark(nc.vector.tensor_copy(tb[:, :, 0, 0:n], cos))
                link.mark(nc.vector.tensor_copy(tb[:, :, 0, n:2 * n], cos))
                link.mark(nc.vector.tensor_scalar(tb[:, :, 1, 0:n], sin, -1.0, None, ALU.mult))
                link.mark(nc.vector.tensor_copy(tb[:, :, 1, n:2 * n], sin))
            dve.wait_ge(par_t, 1)
            for k in range(PAR_TILES):
                n = min(P, NPAR - k * P)
                m = nc.vector.tensor_copy(par[:, k * P:k * P + n], ps[:, 4 + k, 0:n])
                if k < PAR_TILES - 1:
                    link.mark(m)
            m.then_inc(par_c, 1)
            dve.wait_ge(par_c, 1)
            dve.wait_ge(link.s, link.n)
            link.mark(nc.vector.tensor_scalar(small[:, 61:62], col("subln"), 1.0 - LAMBDA_INIT, None,
                                              ALU.mult))

        def lambda_vector(dve, link):
            dve.wait_ge(lam_b, 1)
            nc.vector.tensor_copy(small[:, 62:64], ps[:, 7, 0:2]).then_inc(par_c, 1)
            dve.wait_ge(par_c, 2)
            link(nc.vector.scalar_tensor_tensor(out=lam, in0=small[:, 63:64], scalar=LAMBDA_INIT,
                                                in1=small[:, 62:63], op0=ALU.subtract,
                                                op1=ALU.subtract))

        def end_vector(dve, link):
            dve.wait_ge(gb_loaded, 32 * N_LN)
            dve.wait_ge(ln_z, TT * N_LN)
            dve.wait_ge(ln_z2, TT * N_LN)
            for t in range(TT):
                link(nc.vector.tensor_tensor(x[:, t, :], x[:, t, :], gb[:, 0, :], ALU.mult))
                nc.vector.tensor_tensor(x[:, t, :], x[:, t, :], gb[:, 1, :],
                                        ALU.add).then_inc(x_new, 1)

        gpsimd_units = [ffns[k].first["G", 0] for k in (3, 5)]
        lasts = [mla_u[-1], ffns[0].first["D", ffns[0].steps - 1], diff_u[-1],
                 ffns[1].first["D", ffns[1].steps - 1], ffns[2].first["D", ffns[2].steps - 1],
                 conv_u[-1], ffns[3].first["D", ffns[3].steps - 1],
                 ffns[4].first["D", ffns[4].steps - 1], ml_u[-1],
                 ffns[5].first["D", ffns[5].steps - 1]]
        stages = ["mla", 0, "diff", 1, 2, "conv", 3, 4, "ml", 5]

        @block.sync
        def _(sp):
            sp.dma_start(x[:, 0, :], a["x"][0, 0:P, :]).then_inc(x_loaded[0], 16)
            for k, item in enumerate(order):
                if k == SLOTS:
                    start_loads(sp)
                if isinstance(item, FFN):
                    ffn_sync(sp, item)
                else:
                    load(sp, item)
            for t in range(TT):
                sp.wait_ge(x_new, 2 * (N_LN - 1) + t + 1)
                sp.dma_start(out[0, t * P:(t + 1) * P, :], x[:, t, :]).then_inc(out_done, 16)
            sp.wait_ge(out_done, 16 * TT)

        @block.gpsimd
        def _(pool):
            start_gpsimd(pool)
            pool.wait_ge(m_ylo, KC)
            pool.dma_start(mem_tok, a["mem_2"][0].rearrange("(t p) d -> p t d", p=P)) \
                .then_inc(mem_loaded, 16)
            for n in range(N_LN - 1):
                if stages[n] == "ml":
                    ml_gpsimd(pool)
                if stages[n] in ("conv", "ml"):
                    split_lo(pool, gpsimd_units[("conv", "ml").index(stages[n])], ops=nc.gpsimd)
                ln_gpsimd(pool, n)
                if n == 7:
                    pool.dma_start(l_gain, a["head_norm_g_2"][0].rearrange("h e -> (h e)").rearrange(
                        "(a n) -> a n", a=1).broadcast_to([P, DTOK])).then_inc(gain_loaded, 16)
                    pool.dma_start(g_bias[:, :], a["b_gates_2"].broadcast_to([P, 2 * MH])) \
                        .then_inc(gain_loaded, 16)

        @block.scalar
        def _(act):
            link, split = Chain(act, act_step), Splitter(act, split_hi)
            act.dma_start(x[:, 1, :], a["x"][0, P:S, :]).then_inc(x_loaded[1], 16)
            start_scalar(act, split)
            mixers = {"mla": mla_scalar, "diff": diff_scalar, "conv": conv_scalar, "ml": ml_scalar}
            for n, stage in enumerate(stages):
                if stage in mixers:
                    mixers[stage](act, link, split)
                    for u in {"mla": mla_u[-4:], "diff": diff_u[-4:], "conv": conv_u[-4:],
                              "ml": ml_u[-4:]}[stage][:-1]:
                        split.after(u)
                else:
                    f = ffns[stage]
                    ffn_scalar(act, f, ffn_base[id(f)], split,
                               (lambda: mem_scalar_t(act, range(KC))) if stage == 0 else None)
                ln_scalar_z(act, n)
                if stage == 0:
                    split.after(lasts[n])
                    mem_scalar(act, split, 0)
                if n < N_LN - 1:
                    ln_scalar(act, n)
                if stage == 0:
                    mem_scalar(act, split, 1)
                split.after(lasts[n])

        @block.vector
        def _(dve):
            link, split = Chain(dve, dve_step), Splitter(dve, split_lo, gpsimd_units)
            start_vector(dve, link, split)
            mixers = {"mla": mla_vector, "diff": diff_vector, "conv": conv_vector, "ml": ml_vector}
            for n, stage in enumerate(stages):
                if stage in mixers:
                    mixers[stage](dve, link, split)
                    for u in {"mla": mla_u[-4:], "diff": diff_u[-4:], "conv": conv_u[-4:],
                              "ml": ml_u[-4:]}[stage][:-2]:
                        split.after(u)
                else:
                    f = ffns[stage]
                    ffn_vector(dve, f, ffn_base[id(f)], split,
                               (lambda: mem_vector_t(dve, range(KC))) if stage == 0 else None)
                ln_vector(dve, link, n, lasts[n])
                if stage == 0:
                    split.after(lasts[n])
                    mem_vector(dve, split, 0)
                if n < N_LN - 1:
                    ln_vector_t(dve, link, n)
                if stage == 0:
                    mem_vector(dve, split, 1)
                split.after(lasts[n])
            end_vector(dve, link)

        @block.tensor
        def _(pe):
            start_tensor(pe)
            mixers = {"mla": mla_tensor, "diff": diff_tensor, "conv": conv_tensor, "ml": ml_tensor}
            for n, stage in enumerate(stages):
                if stage in mixers:
                    mixers[stage](pe)
                else:
                    f = ffns[stage]
                    ffn_tensor(pe, f, ffn_base[id(f)],
                               (lambda: mem_tensor_t(pe, range(4)),
                                lambda: mem_tensor_t(pe, range(4, KC))) if stage == 0 else None)
                    if stage == 0:
                        mem_tensor(pe)
                if n < N_LN - 1 and stage != 0:
                    ln_tensor(pe, n)


INPUTS = ["x", "positions", "ln_mix_g", "ln_mix_b", "mla_w_dq", "mla_q_norm", "mla_w_uq", "mla_w_dkv",
          "mla_kv_norm", "mla_w_ukv", "mla_w_o", "diff_w_qkv", "diff_lambda_q1", "diff_lambda_k1",
          "diff_lambda_q2", "diff_lambda_k2", "diff_subln", "diff_w_o", "ln_ffn_g", "ln_ffn_b",
          "ffn_w_up", "ffn_w_down", "mem_2", "ln_g_2", "ln_b_2", "ffn_w_gate_2", "ffn_w_up_2",
          "ffn_w_down_2", "w_kv_mem_2", "w_out_2", "w_in_conv_2", "conv_w_2", "w_in_mlstm_2",
          "b_gates_2", "qk_conv_w_2", "head_norm_g_2"]


def kernel(**inputs):
    import concourse.bacc as bacc
    from concourse.bass_utils import run_bass_kernel_spmd

    nc = bacc.Bacc("TRN2", target_bir_lowering=False, num_devices=1,
                   dynamic_dma_scratch_size=8192)
    arrays, aps = {}, {}
    for name in INPUTS:
        v = np.ascontiguousarray(inputs[name])
        arrays[f"in_{name}"] = v
        aps[name] = nc.dram_tensor(f"in_{name}", v.shape, mybir.dt.from_np(v.dtype),
                                   kind="ExternalInput").ap()
    out = nc.dram_tensor("out", aps["x"].shape, F32, kind="ExternalOutput").ap()
    build(nc, aps, out)
    got = run_bass_kernel_spmd(nc, [arrays], core_ids=[0])
    return got.results[0]["out"]
```
